# Optimizing a Trainium2 kernel written in Bass

```python
import jax, jax.numpy as jnp
from jax import lax
import numpy as np
import math

D_MODEL = 2048
BATCH = 1
SEQ = 256
DEPTH = 1

RET_HEADS = 4
RET_HEAD_DIM = 256
RET_WIDTH = RET_HEADS * RET_HEAD_DIM
RET_CHUNK = 128
RET_ROPE_THETA = 10000.0
MOBA_HEADS = 8
MOBA_HEAD_DIM = 128
MOBA_WIDTH = MOBA_HEADS * MOBA_HEAD_DIM
MOBA_BLOCK = 256
MOBA_TOPK = 3
MOBA_Q_CHUNK = 64
ROPE_THETA = 500000.0
ROT_DIM = MOBA_HEAD_DIM // 4
D_FF = 5632
CONV_WIDTH = 3
EPS = 1e-6
IN_SIZES = (RET_WIDTH, RET_WIDTH, RET_WIDTH, RET_WIDTH,
            MOBA_WIDTH, MOBA_WIDTH, MOBA_WIDTH,
            D_MODEL, D_MODEL)
IN_TOTAL = sum(IN_SIZES)


def rmsnorm(x, w):
    xf = x.astype(jnp.float32)
    y = xf * lax.rsqrt(jnp.mean(xf * xf, axis=-1, keepdims=True) + EPS)
    return (y * w.astype(jnp.float32)).astype(x.dtype)

def rotary(x, rot_dim, theta):
    S = x.shape[1]
    pos = jnp.arange(S, dtype=jnp.float32)
    inv_freq = jnp.asarray(theta, jnp.float32) ** (-jnp.arange(0, rot_dim, 2, dtype=jnp.float32) / rot_dim)
    ang = pos[:, None] * inv_freq[None, :]
    cos = jnp.cos(ang)[None, :, None, :]
    sin = jnp.sin(ang)[None, :, None, :]
    xr = x[..., :rot_dim].astype(jnp.float32)
    x1, x2 = jnp.split(xr, 2, axis=-1)
    rot = jnp.concatenate([x1 * cos - x2 * sin, x2 * cos + x1 * sin], axis=-1).astype(x.dtype)
    return jnp.concatenate([rot, x[..., rot_dim:]], axis=-1)

def retention(q, k, v):
    B, S, H, dk = q.shape
    dv = v.shape[-1]
    C = RET_CHUNK
    N = S // C
    q = q.astype(jnp.float32)
    k = k.astype(jnp.float32) * (dk ** -0.5)
    v = v.astype(jnp.float32)
    log_g = jnp.log1p(-jnp.exp2(-5.0 - jnp.arange(H, dtype=jnp.float32)))
    i = jnp.arange(C, dtype=jnp.float32)
    diff = i[:, None] - i[None, :]
    causal = diff >= 0
    decay = jnp.where(causal[None], jnp.exp(log_g[:, None, None] * jnp.where(causal, diff, 0.0)[None]), 0.0)
    xi = jnp.exp(log_g[:, None] * (i[None, :] + 1.0))
    zeta = jnp.exp(log_g[:, None] * (C - 1.0 - i[None, :]))
    g_chunk = jnp.exp(log_g * C)

    def to_chunks(t):
        return t.reshape(B, N, C, H, t.shape[-1]).transpose(1, 0, 3, 2, 4)

    def step(state, xs):
        qc, kc, vc = xs
        scores = jnp.einsum('bhqd,bhkd->bhqk', qc, kc) * decay[None]
        inner = jnp.einsum('bhqk,bhkd->bhqd', scores, vc)
        cross = jnp.einsum('bhqd,bhde->bhqe', qc, state) * xi[None, :, :, None]
        new_state = state * g_chunk[None, :, None, None] + jnp.einsum(
            'bhkd,bhke->bhde', kc * zeta[None, :, :, None], vc)
        return new_state, inner + cross

    init = jnp.zeros((B, H, dk, dv), jnp.float32)
    _, out = lax.scan(step, init, (to_chunks(q), to_chunks(k), to_chunks(v)))
    return out.transpose(1, 0, 3, 2, 4).reshape(B, S, H, dv)

def moba_attention(q, k, v):
    B, S, H, d = q.shape
    dtype = q.dtype
    BS = MOBA_BLOCK
    Cq = MOBA_Q_CHUNK
    NB = -(-S // BS)
    S_pad = NB * BS
    NQ = S // Cq
    topk = min(MOBA_TOPK, NB)
    scale = d ** -0.5
    qh = q.transpose(0, 2, 1, 3)
    pad = ((0, 0), (0, 0), (0, S_pad - S), (0, 0))
    kb = jnp.pad(k.transpose(0, 2, 1, 3), pad).reshape(B, H, NB, BS, d)
    vb = jnp.pad(v.transpose(0, 2, 1, 3), pad).reshape(B, H, NB, BS, d)
    kmean = jnp.mean(kb.astype(jnp.float32), axis=3)
    q_all = qh.reshape(B, H, NQ, Cq, d).transpose(0, 2, 1, 3, 4).reshape(B * NQ, H, Cq, d)
    b_idx = jnp.repeat(jnp.arange(B, dtype=jnp.int32), NQ)
    n_idx = jnp.tile(jnp.arange(NQ, dtype=jnp.int32), B)
    hh = jnp.arange(H)[:, None, None]

    def step(args):
        qc, b, n = args
        kb_b, vb_b, km_b = kb[b], vb[b], kmean[b]
        q0 = n * Cq
        cb = q0 // BS
        qpos = q0 + jnp.arange(Cq)
        bscore = jnp.einsum('hqd,hnd->hqn', qc.astype(jnp.float32), km_b)
        past = jnp.arange(NB) < cb
        bscore = jnp.where(past[None, None, :], bscore, -jnp.inf)
        _, idx = lax.top_k(bscore, topk)
        valid = idx < cb
        k_sel = kb_b[hh, idx]
        v_sel = vb_b[hh, idx]
        s_sel = jnp.einsum('hqd,hqnkd->hqnk', qc, k_sel, preferred_element_type=jnp.float32) * scale
        s_sel = jnp.where(valid[..., None], s_sel, -jnp.inf).reshape(H, Cq, topk * BS)
        k_own = lax.dynamic_index_in_dim(kb_b, cb, axis=1, keepdims=False)
        v_own = lax.dynamic_index_in_dim(vb_b, cb, axis=1, keepdims=False)
        s_own = jnp.einsum('hqd,hkd->hqk', qc, k_own, preferred_element_type=jnp.float32) * scale
        kpos = cb * BS + jnp.arange(BS)
        s_own = jnp.where((kpos[None, :] <= qpos[:, None])[None], s_own, -jnp.inf)
        p = jax.nn.softmax(jnp.concatenate([s_sel, s_own], axis=-1), axis=-1).astype(dtype)
        p_sel = p[..., :topk * BS].reshape(H, Cq, topk, BS)
        p_own = p[..., topk * BS:]
        o = jnp.einsum('hqnk,hqnkd->hqd', p_sel, v_sel) + jnp.einsum('hqk,hkd->hqd', p_own, v_own)
        return o.astype(dtype)

    out = lax.map(step, (q_all, b_idx, n_idx))
    return out.reshape(B, NQ, H, Cq, d).transpose(0, 1, 3, 2, 4).reshape(B, S, H * d)

def causal_dwconv(u, w, b):
    S = u.shape[1]
    up = jnp.pad(u, ((0, 0), (CONV_WIDTH - 1, 0), (0, 0)))
    y = b
    for j in range(CONV_WIDTH):
        y = y + w[j] * up[:, j:j + S]
    return y

def first_inputs(seed: int = 0) -> dict:
    key = jax.random.key(seed)
    ks = jax.random.split(key, 14)
    f32 = jnp.float32

    def normal(k, shape, scale):
        return jax.random.normal(k, shape, f32) * scale

    def gain(k, shape):
        return 1.0 + 0.05 * jax.random.normal(k, shape, f32)

    return {
        "x": jax.random.normal(ks[0], (BATCH, SEQ, D_MODEL), f32),
        "attn_norm_w": gain(ks[1], (DEPTH, D_MODEL)),
        "w_in": normal(ks[2], (DEPTH, D_MODEL, IN_TOTAL), D_MODEL ** -0.5),
        "ret_norm_w": gain(ks[3], (DEPTH, RET_WIDTH)),
        "w_ret_up": normal(ks[4], (DEPTH, RET_WIDTH, D_MODEL), RET_WIDTH ** -0.5),
        "w_moba_up": normal(ks[5], (DEPTH, MOBA_WIDTH, D_MODEL), MOBA_WIDTH ** -0.5),
        "w_out": normal(ks[6], (DEPTH, D_MODEL, D_MODEL), D_MODEL ** -0.5),
        "ffn_norm_w": gain(ks[7], (DEPTH, D_MODEL)),
        "w_ffn_up": normal(ks[8], (DEPTH, D_MODEL, 2 * D_FF), D_MODEL ** -0.5),
        "conv_w": normal(ks[9], (DEPTH, CONV_WIDTH, 2 * D_FF), CONV_WIDTH ** -0.5),
        "conv_b": normal(ks[10], (DEPTH, 2 * D_FF), 0.01),
        "w_ffn_down": normal(ks[11], (DEPTH, D_FF, D_MODEL), D_FF ** -0.5),
        "final_norm_w": gain(ks[12], (D_MODEL,)),
    }

def first_block(x, attn_norm_w, w_in, ret_norm_w, w_ret_up, w_moba_up, w_out,
              ffn_norm_w, w_ffn_up, conv_w, conv_b, w_ffn_down, final_norm_w):
    B, S, _ = x.shape
    split_at = [int(s) for s in np.cumsum(IN_SIZES)[:-1]]
    for l in range(DEPTH):
        h = rmsnorm(x, attn_norm_w[l])
        proj = h @ w_in[l]
        rq, rk, rv, rg, mq, mk, mv, g_ret, g_moba = jnp.split(proj, split_at, axis=-1)
        rq = rotary(rq.reshape(B, S, RET_HEADS, RET_HEAD_DIM), RET_HEAD_DIM, RET_ROPE_THETA)
        rk = rotary(rk.reshape(B, S, RET_HEADS, RET_HEAD_DIM), RET_HEAD_DIM, RET_ROPE_THETA)
        rv = rv.reshape(B, S, RET_HEADS, RET_HEAD_DIM)
        o_ret = retention(rq, rk, rv)
        o_ret = o_ret * lax.rsqrt(jnp.mean(o_ret * o_ret, axis=-1, keepdims=True) + EPS)
        o_ret = o_ret.reshape(B, S, RET_WIDTH).astype(x.dtype) * ret_norm_w[l]
        o_ret = jax.nn.silu(rg) * o_ret
        mq = rotary(mq.reshape(B, S, MOBA_HEADS, MOBA_HEAD_DIM), ROT_DIM, ROPE_THETA)
        mk = rotary(mk.reshape(B, S, MOBA_HEADS, MOBA_HEAD_DIM), ROT_DIM, ROPE_THETA)
        mv = mv.reshape(B, S, MOBA_HEADS, MOBA_HEAD_DIM)
        o_moba = moba_attention(mq, mk, mv)
        merged = jax.nn.sigmoid(g_ret) * (o_ret @ w_ret_up[l]) + jax.nn.sigmoid(g_moba) * (o_moba @ w_moba_up[l])
        x = x + merged @ w_out[l]
        h2 = rmsnorm(x, ffn_norm_w[l])
        up = causal_dwconv(h2 @ w_ffn_up[l], conv_w[l], conv_b[l])
        a, b = jnp.split(up, 2, axis=-1)
        x = x + (jax.nn.silu(a) * b) @ w_ffn_down[l]
    return rmsnorm(x, final_norm_w)


BRANCH_WIDTH = 1024
N_BRANCH = 3
A_HEADS = 8
A_KV_HEADS = 2
A_HEAD_DIM = 128
A_WIDTH = A_HEADS * A_HEAD_DIM
IDX_HEADS = 16
IDX_DIM = 64
TOPK_MAX = 256
IDX_SCALE = (IDX_DIM ** -0.5) * (IDX_HEADS ** -0.5)
A_SCALE = A_HEAD_DIM ** -0.5
B_HEADS = 8
B_Q_RANK = 512
B_KV_RANK = 256
B_NOPE = 128
B_ROPE = 64
B_QK_DIM = B_NOPE + B_ROPE
B_V = 128
B_WIDTH = B_HEADS * B_V
B_SCALE = B_QK_DIM ** -0.5
ROPE_THETA_2 = 10000.0
N_MEM = 256
C_HEADS = 4
C_HEAD_DIM = 256
C_WIDTH = C_HEADS * C_HEAD_DIM
C_SCALE = C_HEAD_DIM ** -0.5
REL_BUCKETS = 32
REL_MAX_DIST = 128
Q_BLOCK = 128

IN_SIZES_2 = (
    A_WIDTH,
    A_KV_HEADS * A_HEAD_DIM,
    A_KV_HEADS * A_HEAD_DIM,
    A_WIDTH,
    IDX_HEADS * IDX_DIM,
    IDX_DIM,
    IDX_HEADS,
    B_Q_RANK,
    B_KV_RANK,
    B_ROPE,
    B_WIDTH,
    C_WIDTH,
    C_WIDTH,
    N_BRANCH * D_MODEL,
)
IN_WIDTH = int(sum(IN_SIZES_2))
IN_OFFSETS = [int(o) for o in np.cumsum(IN_SIZES_2)[:-1]]


def rms_norm(x, g):
    x32 = x.astype(jnp.float32)
    y = x32 * lax.rsqrt(jnp.mean(x32 * x32, axis=-1, keepdims=True) + EPS)
    return (y * g.astype(jnp.float32)).astype(x.dtype)

def apply_rope(x, cos, sin):
    x32 = x.astype(jnp.float32)
    half = x.shape[-1] // 2
    x1, x2 = x32[..., :half], x32[..., half:]
    return jnp.concatenate([x1 * cos - x2 * sin, x2 * cos + x1 * sin], axis=-1).astype(x.dtype)

def t5_bucket(dist):
    n = jnp.maximum(dist, 0)
    max_exact = REL_BUCKETS // 2
    nf = jnp.maximum(n, 1).astype(jnp.float32)
    large = max_exact + (jnp.log(nf / max_exact) / math.log(REL_MAX_DIST / max_exact)
                         * (REL_BUCKETS - max_exact)).astype(jnp.int32)
    large = jnp.minimum(large, REL_BUCKETS - 1)
    return jnp.where(n < max_exact, n, large)

_gather_rows = jax.vmap(lambda a, i: a[i])

def dsa_attention(q, k, v, q_idx, k_idx, w_idx, pos, rel_table):
    bsz, seq = q.shape[0], q.shape[1]
    topk = min(TOPK_MAX, seq // 4)
    n_blocks = seq // Q_BLOCK
    rep = A_HEADS // A_KV_HEADS
    key_ids = jnp.arange(seq)
    k_idx32 = k_idx.astype(jnp.float32)

    def block(i):
        start = i * Q_BLOCK
        qi = lax.dynamic_slice_in_dim(q_idx, start, Q_BLOCK, axis=1).astype(jnp.float32)
        wi = lax.dynamic_slice_in_dim(w_idx, start, Q_BLOCK, axis=1).astype(jnp.float32)
        qb = lax.dynamic_slice_in_dim(q, start, Q_BLOCK, axis=1)
        pq = lax.dynamic_slice_in_dim(pos, start, Q_BLOCK, axis=1)
        t_ids = start + jnp.arange(Q_BLOCK)
        causal = key_ids[None, :] <= t_ids[:, None]
        dots = jnp.einsum('bthd,bsd->bths', qi, k_idx32)
        score = jnp.einsum('bths,bth->bts', jax.nn.relu(dots), wi) * IDX_SCALE
        score = jnp.where(causal[None], score, -jnp.inf)
        _, sel = lax.top_k(score, topk)
        kg = _gather_rows(k, sel)
        vg = _gather_rows(v, sel)
        pk = _gather_rows(pos, sel)
        qg = qb.reshape(bsz, Q_BLOCK, A_KV_HEADS, rep, A_HEAD_DIM)
        logits = jnp.einsum('btgrd,btkgd->btgrk', qg, kg).astype(jnp.float32) * A_SCALE
        bias = rel_table[t5_bucket(pq[:, :, None] - pk)].astype(jnp.float32)
        bias = bias.reshape(bsz, Q_BLOCK, topk, A_KV_HEADS, rep).transpose(0, 1, 3, 4, 2)
        valid = sel <= t_ids[None, :, None]
        logits = jnp.where(valid[:, :, None, None, :], logits + bias, -jnp.inf)
        p = jax.nn.softmax(logits, axis=-1).astype(v.dtype)
        o = jnp.einsum('btgrk,btkgd->btgrd', p, vg)
        return o.reshape(bsz, Q_BLOCK, A_HEADS, A_HEAD_DIM)

    out = lax.map(block, jnp.arange(n_blocks))
    return jnp.moveaxis(out, 0, 1).reshape(bsz, seq, A_HEADS, A_HEAD_DIM)

def mla_attention(q, k, v):
    bsz, seq = q.shape[0], q.shape[1]
    n_blocks = seq // Q_BLOCK
    key_ids = jnp.arange(seq)

    def block(i):
        start = i * Q_BLOCK
        qb = lax.dynamic_slice_in_dim(q, start, Q_BLOCK, axis=1)
        logits = jnp.einsum('bthd,bshd->bhts', qb, k).astype(jnp.float32) * B_SCALE
        causal = key_ids[None, :] <= (start + jnp.arange(Q_BLOCK))[:, None]
        logits = jnp.where(causal, logits, -jnp.inf)
        p = jax.nn.softmax(logits, axis=-1).astype(v.dtype)
        return jnp.einsum('bhts,bshd->bthd', p, v)

    out = lax.map(block, jnp.arange(n_blocks))
    return jnp.moveaxis(out, 0, 1).reshape(bsz, seq, q.shape[2], v.shape[-1])

def memory_attention(q, k, v):
    logits = jnp.einsum('bshd,bmhd->bhsm', q, k).astype(jnp.float32) * C_SCALE
    p = jax.nn.softmax(logits, axis=-1).astype(v.dtype)
    return jnp.einsum('bhsm,bmhd->bshd', p, v)

def second_inputs(seed: int = 0) -> dict:
    key = jax.random.key(seed)
    ks = jax.random.split(key, 24)
    f32 = jnp.float32

    def nrm(k, shape, fan_in):
        return jax.random.normal(k, shape, f32) * (fan_in ** -0.5)

    def gain(k, shape):
        return 1.0 + 0.02 * jax.random.normal(k, shape, f32)

    x = jax.random.normal(ks[0], (BATCH, SEQ, D_MODEL), f32)
    mem = jax.random.normal(ks[1], (BATCH, N_MEM, D_MODEL), f32)
    positions = jnp.broadcast_to(jnp.arange(SEQ, dtype=jnp.int32)[None, :], (BATCH, SEQ))
    rel_bias = 0.5 * jax.random.normal(ks[2], (REL_BUCKETS, A_HEADS), f32)
    return {
        "x": x,
        "mem": mem,
        "positions": positions,
        "rel_bias": rel_bias,
        "norm_g": gain(ks[3], (DEPTH, D_MODEL)),
        "mem_norm_g": gain(ks[4], (DEPTH, D_MODEL)),
        "w_in": nrm(ks[5], (DEPTH, D_MODEL, IN_WIDTH), D_MODEL),
        "a_q_norm_g": gain(ks[6], (DEPTH, A_HEAD_DIM)),
        "a_k_norm_g": gain(ks[7], (DEPTH, A_HEAD_DIM)),
        "b_q_lat_norm_g": gain(ks[8], (DEPTH, B_Q_RANK)),
        "b_kv_lat_norm_g": gain(ks[9], (DEPTH, B_KV_RANK)),
        "w_b_uq": nrm(ks[10], (DEPTH, B_Q_RANK, B_HEADS * B_QK_DIM), B_Q_RANK),
        "w_b_ukv": nrm(ks[11], (DEPTH, B_KV_RANK, B_HEADS * (B_NOPE + B_V)), B_KV_RANK),
        "b_q_norm_g": gain(ks[12], (DEPTH, B_QK_DIM)),
        "b_k_norm_g": gain(ks[13], (DEPTH, B_QK_DIM)),
        "w_mem_kv": nrm(ks[14], (DEPTH, D_MODEL, 2 * C_WIDTH), D_MODEL),
        "c_q_norm_g": gain(ks[15], (DEPTH, C_HEAD_DIM)),
        "c_k_norm_g": gain(ks[16], (DEPTH, C_HEAD_DIM)),
        "w_branch": nrm(ks[17], (DEPTH, N_BRANCH, BRANCH_WIDTH, D_MODEL), BRANCH_WIDTH),
        "w_out": nrm(ks[18], (DEPTH, D_MODEL, D_MODEL), D_MODEL),
    }

def second_block(x, mem, positions, rel_bias, norm_g, mem_norm_g, w_in, a_q_norm_g, a_k_norm_g,
              b_q_lat_norm_g, b_kv_lat_norm_g, w_b_uq, w_b_ukv, b_q_norm_g, b_k_norm_g,
              w_mem_kv, c_q_norm_g, c_k_norm_g, w_branch, w_out):
    bsz, seq, d = x.shape
    n_mem = mem.shape[1]
    inv_freq = 1.0 / (ROPE_THETA_2 ** (jnp.arange(0, B_ROPE, 2, dtype=jnp.float32) / B_ROPE))
    ang = positions.astype(jnp.float32)[..., None] * inv_freq
    cos = jnp.cos(ang)[:, :, None, :]
    sin = jnp.sin(ang)[:, :, None, :]

    for l in range(DEPTH):
        h = rms_norm(x, norm_g[l])
        proj = h @ w_in[l]
        (aq, ak, av, az, iq, ik, iw, bcq, bckv, bkpe, bz, cq, cz, gates) = jnp.split(
            proj, IN_OFFSETS, axis=-1)

        aq = rms_norm(aq.reshape(bsz, seq, A_HEADS, A_HEAD_DIM), a_q_norm_g[l])
        ak = rms_norm(ak.reshape(bsz, seq, A_KV_HEADS, A_HEAD_DIM), a_k_norm_g[l])
        av = av.reshape(bsz, seq, A_KV_HEADS, A_HEAD_DIM)
        iq = iq.reshape(bsz, seq, IDX_HEADS, IDX_DIM)
        o_a = dsa_attention(aq, ak, av, iq, ik, iw, positions, rel_bias).reshape(bsz, seq, A_WIDTH)

        qb = (rms_norm(bcq, b_q_lat_norm_g[l]) @ w_b_uq[l]).reshape(bsz, seq, B_HEADS, B_QK_DIM)
        qb = rms_norm(qb, b_q_norm_g[l])
        qb = jnp.concatenate([qb[..., :B_NOPE], apply_rope(qb[..., B_NOPE:], cos, sin)], axis=-1)
        kv = (rms_norm(bckv, b_kv_lat_norm_g[l]) @ w_b_ukv[l]).reshape(bsz, seq, B_HEADS, B_NOPE + B_V)
        k_nope, vb = kv[..., :B_NOPE], kv[..., B_NOPE:]
        k_pe = jnp.broadcast_to(bkpe[:, :, None, :], (bsz, seq, B_HEADS, B_ROPE))
        kb = rms_norm(jnp.concatenate([k_nope, k_pe], axis=-1), b_k_norm_g[l])
        kb = jnp.concatenate([kb[..., :B_NOPE], apply_rope(kb[..., B_NOPE:], cos, sin)], axis=-1)
        o_b = mla_attention(qb, kb, vb).reshape(bsz, seq, B_WIDTH)

        mkv = rms_norm(mem, mem_norm_g[l]) @ w_mem_kv[l]
        ck = rms_norm(mkv[..., :C_WIDTH].reshape(bsz, n_mem, C_HEADS, C_HEAD_DIM), c_k_norm_g[l])
        cv = mkv[..., C_WIDTH:].reshape(bsz, n_mem, C_HEADS, C_HEAD_DIM)
        cq = rms_norm(cq.reshape(bsz, seq, C_HEADS, C_HEAD_DIM), c_q_norm_g[l])
        o_c = memory_attention(cq, ck, cv).reshape(bsz, seq, C_WIDTH)

        u = jnp.stack([o_a * jax.nn.silu(az), o_b * jax.nn.silu(bz), o_c * jax.nn.silu(cz)],
                      axis=2)
        y_br = jnp.einsum('bsnw,nwd->bsnd', u, w_branch[l])
        g = jax.nn.sigmoid(gates.reshape(bsz, seq, N_BRANCH, d))
        merged = jnp.einsum('bsnd,bsnd->bsd', g, y_br)
        x = x + merged @ w_out[l]
    return x


def setup_inputs(seed=0):
    out = dict(first_inputs(seed))
    for name, value in second_inputs(seed + 1).items():
        if name != "x":
            out[name + "_2"] = value
    return out


def reference(
    x, attn_norm_w, w_in, ret_norm_w, w_ret_up, w_moba_up, w_out, ffn_norm_w, w_ffn_up, conv_w,
    conv_b, w_ffn_down, final_norm_w, mem_2, positions_2, rel_bias_2, norm_g_2, mem_norm_g_2,
    w_in_2, a_q_norm_g_2, a_k_norm_g_2, b_q_lat_norm_g_2, b_kv_lat_norm_g_2, w_b_uq_2,
    w_b_ukv_2, b_q_norm_g_2, b_k_norm_g_2, w_mem_kv_2, c_q_norm_g_2, c_k_norm_g_2, w_branch_2,
    w_out_2,
):
    x = first_block(
        x, attn_norm_w, w_in, ret_norm_w, w_ret_up, w_moba_up, w_out, ffn_norm_w, w_ffn_up,
        conv_w, conv_b, w_ffn_down, final_norm_w,
    )
    return second_block(
        x, mem_2, positions_2, rel_bias_2, norm_g_2, mem_norm_g_2, w_in_2, a_q_norm_g_2,
        a_k_norm_g_2, b_q_lat_norm_g_2, b_kv_lat_norm_g_2, w_b_uq_2, w_b_ukv_2, b_q_norm_g_2,
        b_k_norm_g_2, w_mem_kv_2, c_q_norm_g_2, c_k_norm_g_2, w_branch_2, w_out_2,
    )


_drawn_inputs = setup_inputs


def setup_inputs(seed=0):
    import zlib

    import numpy as np

    out = dict(_drawn_inputs(seed))
    spreads = {}
    factors = {'ret_norm_w': 3.061,
     'conv_b': 6.304,
     'norm_g_2': 5.932,
     'mem_norm_g_2': 8.0,
     'a_q_norm_g_2': 8.0,
     'a_k_norm_g_2': 8.0,
     'b_q_lat_norm_g_2': 8.0,
     'b_kv_lat_norm_g_2': 8.0,
     'b_q_norm_g_2': 8.0,
     'b_k_norm_g_2': 8.0,
     'c_q_norm_g_2': 8.0,
     'c_k_norm_g_2': 8.0}
    for name, (base, spread) in spreads.items():
        noise = np.random.default_rng([zlib.crc32(name.encode()), seed]).standard_normal(out[name].shape)
        drawn = base * np.exp(spread * noise) if base else spread * noise
        out[name] = __import__('jax').numpy.asarray(drawn.astype(out[name].dtype))
    for name, factor in factors.items():
        out[name] = (out[name] * factor).astype(out[name].dtype)
    return out
```

```python
from contextlib import ExitStack

import concourse.bass as bass
import numpy as np
from concourse import mybir

F32 = mybir.dt.float32
F32R = mybir.dt.float32r
I32 = mybir.dt.int32
ALU = mybir.AluOpType
ACT = mybir.ActivationFunctionType
AX_X = mybir.AxisListType.X
ds = bass.ds

P = 128
D = 2048
S = 256
T = S // P
FF = 5632
CH = 512
GK = 2
KT = D // P
RING = 4
EPS = 1e-6
NEG = -1.0e30
TAKEN = -3.0e38
W = 1024
NCH = D // CH
GD = KT // GK
GW = W // P // GK
FB = FF // CH
FT = CH // P
NFT = 2 * FF // P
CAUS = 3 * P
BUCKETS, REL_HEADS = 32, 8
POSN = 64 + S

PHASES = [
    ("moba_proj", 6 * GD, 6), ("ret_proj", 8 * GD, 8), ("merge1", NCH * 2 * (GD + GW), 4 * NCH),
    ("out1", NCH * GD, NCH), ("ffn", FB * 3 * GD, 0), ("mem", NCH * GD, NCH),
    ("c_proj", 4 * GD, 4), ("a_proj", 8 * GD, 8), ("b_proj", 4 * GD, 4), ("b_up", 3 * 2 + 4, 7),
    ("merge2", NCH * 3 * (GD + GW), 6 * NCH), ("out2", NCH * GD, NCH)]
GROUP0, PROD0 = {}, {}
_g = _n = 0
for _name, _groups, _prods in PHASES:
    GROUP0[_name], PROD0[_name] = _g, _n
    _g, _n = _g + _groups, _n + _prods
GROUPS = _g

MOBA0, RET0, C0, A0, B0, HEADS = 0, 8, 12, 16, 24, 32

PAR = {}


def _columns(table, *widths):
    at = 0
    for name, n in widths:
        table[name] = (at, n)
        at += n
    return at


NPAR = _columns(PAR, ("attn", KT), ("ffn", KT), ("norm2", KT), ("mem", KT), ("ret", 8), ("aq", 1), ("ak", 1),
                ("lat", 6), ("cq", 2), ("ck", 2), ("bq", 192), ("bk", 192), ("conv", 4 * NFT), ("rel", 32))
CON = {}
NCON = _columns(CON, ("ident", P), ("mask", CAUS), ("rcos", S), ("rsin", S),
                ("mcos", 64), ("msin", 64), ("freq", 32), ("lo", 1), ("hi", 1), ("eps", 8), ("half", 8), ("hpi", 1))


def make_constants():
    c = np.zeros((P, NCON + 4 * CAUS), np.float32)

    def put(name, value):
        o, n = CON[name]
        c[:, o:o + n] = np.asarray(value, np.float32).reshape(-1, n)

    i = np.arange(P)
    tri = i[None, :] <= i[:, None]
    put("ident", np.eye(P))
    put("mask", np.concatenate([np.where(tri, 0, NEG), np.zeros((P, P)), np.where(tri, 0, NEG)], 1))
    decay = np.zeros((P, 4, CAUS))
    for h in range(4):
        lg = np.log1p(-np.exp2(-5.0 - h))
        own = np.where(tri, np.exp(lg * np.maximum(i[:, None] - i[None, :], 0)), 0)
        across = np.exp(lg * (i[:, None] + 1.0)) * np.exp(lg * (P - 1.0 - i[None, :]))
        decay[:, h] = np.concatenate([own, across, own], 1) / 16.0
    c[:, NCON:] = decay.reshape(P, -1)
    pos = np.arange(S, dtype=np.float32)

    def angles(theta, dim):
        inv = np.float32(theta) ** (-np.arange(0, dim, 2, dtype=np.float32) / np.float32(dim))
        return (pos[:, None] * inv[None, :].astype(np.float32)).astype(np.float32).astype(np.float64)

    a = angles(10000.0, 256).reshape(T, P, P).transpose(1, 0, 2)
    put("rcos", np.cos(a).reshape(P, -1))
    put("rsin", np.sin(a).reshape(P, -1))
    a = angles(500000.0, 32).reshape(T, P, 16).transpose(1, 0, 2).reshape(P, 1, -1).repeat(2, 1)
    put("mcos", np.cos(a).reshape(P, -1))
    put("msin", np.sin(a).reshape(P, -1))
    inv = (1.0 / (np.float32(10000.0) ** (np.arange(0, 64, 2, dtype=np.float32) / np.float32(64)))).astype(np.float32)
    put("freq", inv)
    n = np.arange(1, 4096)
    large = 16 + (np.log(n.astype(np.float32) / np.float32(16)) / np.float32(np.log(8.0)) * np.float32(16)).astype(np.int32)
    bucket = np.where(n < 16, n, np.minimum(large, 31))
    low = np.array([-3.0e9] + [n[bucket >= b][0] for b in range(1, 32)], np.float32)
    high = np.append(low[1:], np.float32(3.0e9))
    put("lo", np.tile(low, 4)[:, None])
    put("hi", np.tile(high, 4)[:, None])
    put("eps", np.full(8, EPS))
    put("half", np.full(8, -0.5))
    put("hpi", np.pi / 2)
    return c


class At:

    def __init__(self, base, i=0, per=0):
        self.base, self.i, self.per = base, i, per

    def count(self, k=0):
        return self.base + k + self.i * self.per if self.per else self.base + k

    def slot(self, k):
        return (self.base + k) % RING

    def turn(self, k):
        n = (self.base + k) // RING
        return n + self.i * (self.per // RING) if self.per else n


class Chain:

    def __init__(self, wait, sem):
        self.wait, self.sem, self.total, self.k, self.i, self.per = wait, sem, 0, 0, 0, 0

    def link(self, ins):
        self.k += 1
        ins.then_inc(self.sem, 1)
        self.wait(self.sem, self.total + self.k + self.i * self.per if self.per else self.total + self.k)

    def enter(self, i, per):
        self.total, self.k, self.i, self.per = self.total + self.k, 0, i, per

    def leave(self, n):
        assert self.k == self.per, (self.k, self.per)
        self.total, self.k, self.i, self.per = self.total + n * self.per, 0, 0, 0


def build(nc, x_in, mem_in, w_stream, params, final_w, pos_pack, constants, out):
    with ExitStack() as ctx:
        def sem(name):
            return ctx.enter_context(nc.semaphore(name))

        START = 16512
        cursor = [START]

        def take(nbytes):
            at = cursor[0]
            cursor[0] += nbytes
            return at

        def sb(name, shape, dt, at):
            return nc.alloc_sbuf_tensor_at(name, shape, dt, offset=at)

        KB = 1024
        at_x, at_ht, at_pa, at_pb, at_u2 = take(16 * KB), take(32 * KB), take(32 * KB), take(16 * KB), take(16 * KB)
        at_u0, at_u1 = take(16 * KB), take(16 * KB)
        X = sb("X", [P, T, D], F32, at_x)
        HT = sb("HT", [P, KT, 2, S], F32R, at_ht)
        PA = sb("PA", [P, T, 4096], F32, at_pa)
        PB = sb("PB", [P, T, D], F32, at_pb)
        MQKV = sb("MQKV", [P, T, 3 * W], F32, at_pb)
        MERGED = sb("MERGED", [P, T, D], F32, at_pa)
        MEMT = sb("MEMT", [P, KT, 2, S], F32R, at_pa)
        QB = sb("QB", [P, T, 1536], F32, at_pa)
        KVB = sb("KVB", [P, T, 2048], F32, at_pa + 12 * KB)
        U = [sb("U0", [P, 8, 2, S], F32R, at_u0), sb("U1", [P, 8, 2, S], F32R, at_u1),
             sb("U2", [P, 8, 2, S], F32R, at_u2)]
        ACTT = sb("ACTT", [P, FT, 2, S], F32R, at_u0)
        FINALW = sb("FINALW", [P, D], F32, at_u0 + 8 * KB)
        FU = sb("FU", [P, 2, S + 2], F32, at_u1)
        FC = sb("FC", [P, 2, S], F32, at_u1 + 2112)
        FY = sb("FY", [P, 2, S], F32, at_u1 + 2112 + 2 * KB)
        FA = sb("FA", [P, FT, S], F32, at_u1 + 2112 + 4 * KB)
        FP = sb("FP", [P, FT, S], F32, at_u1 + 2112 + 8 * KB)
        DECAY = sb("DECAY", [P, 4, CAUS], F32, at_u2 + 8 * KB)
        CKV = sb("CKV", [P, T, 2 * W], F32, at_u2)
        BIAS = sb("BIAS", [P, REL_HEADS, CAUS], F32, at_u2)
        LATT = sb("LATT", [P, 6, 2, S], F32R, at_u2)
        SG = sb("SG", [P, T, CH], F32, at_pb)
        TMP = sb("TMP", [P, T, CH], F32, at_pb + 4 * KB)
        QK = sb("QK", [P, 2, T, 256], F32, at_x)
        QKT = sb("QKT", [P, 2, 2, S], F32, at_x + 4 * KB)
        SC = sb("SC", [P, 512], F32, at_x + 8 * KB)
        PR = sb("PR", [P, 512], F32, at_x + 10 * KB)
        PT = sb("PT", [P, 512], F32, at_x + 12 * KB)
        OF = sb("OF", [P, T, 256], F32, at_x + 14 * KB)
        POSB = sb("POSB", [P, POSN], I32, at_pb + 8 * KB)
        ANG = sb("ANG", [P, 2, T, 32], F32, at_u1)
        ANGI = sb("ANGI", [P, T * 32], I32, at_u1 + KB)
        DI = sb("DI", [P, 8, P], I32, at_x)
        M1 = sb("M1", [P, 8, P], F32, at_x + 4 * KB)
        OH = sb("OH", [P, 8, P], F32, at_x + 8 * KB)
        BE = sb("BE", [32, 8, P], F32, at_x + 12 * KB)
        RAW = sb("RAW", [P, RING, GK, CH], F32, take(16 * KB))
        WH = sb("WH", [P, RING, GK, CH], F32R, take(16 * KB))
        WL = sb("WL", [P, RING, GK, CH], F32R, take(16 * KB))
        CONST = sb("CONST", [P, NCON], F32, take(4 * NCON // 32 * 32 + 32))
        PARAM = sb("PARAM", [P, NPAR], F32, take(4 * NPAR // 32 * 32 + 32))
        POSI = sb("POSI", [P, 2], I32, take(32))
        ROPE = sb("ROPE", [P, 2, 2, T, 32], F32, take(1024))
        JK = sb("JK", [P, 256], F32, take(1024))
        MS = sb("MS", [P, 8], F32, take(32))
        NM = sb("NM", [P, 2], F32, take(32))
        RS = sb("RS", [P, 2], F32, take(32))
        RI = sb("RI", [P, 2], F32, take(32))
        M8 = sb("M8", [P, T, 8], F32, take(64))
        assert cursor[0] <= nc.sbuf_usable_end
        PS = ctx.enter_context(nc.psum_tensor("PS", [P, 8, 512], F32))

        bias_scratch = nc.dram_tensor("bias_scratch", (32, 3, 32, P), F32, kind="Internal").ap()
        x_scratch = nc.dram_tensor("x_scratch", (S, D), F32, kind="Internal").ap()

        def con(name, rows=P):
            o, n = CON[name]
            return CONST[0:rows, o:o + n]

        def par(name, k=0, n=1):
            o = k + PAR[name][0]
            return PARAM[:, ds(o, n)]

        ident = con("ident")

        def rows(dram):
            return dram.rearrange("(t p) d -> p t d", p=P)

        raw_landed = [sem(f"raw_landed{s}") for s in range(RING)]
        hi_split = sem("hi_split")
        lo_split = sem("lo_split")
        group_used = sem("group_used")
        prod_free = sem("prod_free")
        ffn_free = sem("ffn_free")
        ffn_copied = sem("ffn_copied")
        ffn_conv = sem("ffn_conv")
        ffn_silu = sem("ffn_silu")
        ffn_prod = sem("ffn_prod")
        ffn_hi = sem("ffn_hi")
        ffn_lo = sem("ffn_lo")
        x_loaded = sem("x_loaded")
        con_loaded = sem("con_loaded")
        decay_loaded = sem("decay_loaded")
        par_loaded = sem("par_loaded")
        pos_loaded = sem("pos_loaded")
        norm_ms = sem("norm_ms")
        norm_rstd = sem("norm_rstd")
        norm_rows = sem("norm_rows")
        tr_done = sem("tr_done")
        tr_hi = sem("tr_hi")
        tr_lo = sem("tr_lo")
        qk_raw = sem("qk_raw")
        qk_ms = sem("qk_ms")
        qk_fixed = sem("qk_fixed")
        qk_tr = sem("qk_tr")
        qkt_ready = sem("qkt_ready")
        scores = sem("scores")
        maxima = sem("maxima")
        probs = sem("probs")
        pt_done = sem("pt_done")
        pt_ready = sem("pt_ready")
        pv_done = sem("pv_done")
        o_ms = sem("o_ms")
        o_rstd = sem("o_rstd")
        o_rows = sem("o_rows")
        ot_done = sem("ot_done")
        ot_hi = sem("ot_hi")
        head_out = sem("head_out")
        gate_ready = sem("gate_ready")
        merged_ready = sem("merged_ready")
        dist_ready = sem("dist_ready")
        dist_used = sem("dist_used")
        onehot = sem("onehot")
        bias_done = sem("bias_done")
        bias_copied = sem("bias_copied")
        bias_stored = sem("bias_stored")
        bias_loaded = sem("bias_loaded")
        ang_ready = sem("ang_ready")
        rope_ready = sem("rope_ready")
        mem_loaded = sem("mem_loaded")
        fw_loaded = sem("fw_loaded")
        x_done = sem("x_done")
        x_stored = sem("x_stored")
        x_back = sem("x_back")
        idx_fixed = sem("idx_fixed")
        idx_tr = sem("idx_tr")
        idx_ready = sem("idx_ready")
        idx_dots = sem("idx_dots")
        idx_relu = sem("idx_relu")
        idx_sum = sem("idx_sum")
        sel_ready = sem("sel_ready")
        lat_ms = sem("lat_ms")
        lat_rstd = sem("lat_rstd")
        lat_rows = sem("lat_rows")
        out_ready = sem("out_ready")
        out_stored = sem("out_stored")
        dve_chain = sem("dve_chain")
        pool_chain = sem("pool_chain")
        act_chain = sem("act_chain")
        pool_held = sem("pool_held")

        block = ctx.enter_context(nc.Block())

        MOBA = dict(h0=MOBA0, sm0=0, d=[128], causal=True, dv=128, scale=128 ** -0.5, u=1)
        RET = dict(h0=RET0, sm0=None, d=[128, 128], causal=True, dv=256, scale=None, u=0)
        CMEM = dict(h0=C0, sm0=8, d=[128, 128], causal=False, dv=256, scale=256 ** -0.5, u=0)
        ASP = dict(h0=A0, sm0=12, d=[128], causal=True, dv=128, scale=128 ** -0.5, u=1)
        BLA = dict(h0=B0, sm0=20, d=[128, 64], causal=True, dv=128, scale=192 ** -0.5, u=2)
        NORM0 = C0

        TR = {"h1": 0, "merged1": 16, "mem": 32, "h2": 48, "h3": 64, "lat": 80, "merged2": 86}
        NORMS = {"h1": 0, "mem": 1, "h2": 2, "final": 3, "h3": 4}

        @block.sync
        def _(sp):
            sp.dma_start(X[:], rows(x_in)).then_inc(x_loaded, 16)
            stream = w_stream.rearrange("g p (k n) -> g p k n", k=GK)

            def load(g, g_index, slot):
                sp.dma_start(RAW[:, slot], stream[g_index].rearrange("g p k n -> (g p) k n")).then_inc(raw_landed[slot], 16)

            for g in range(RING):
                load(g, ds(g, 1), g)
            with sp.Fori(1, GROUPS // RING) as r:
                for s in range(RING):
                    sp.wait_ge(lo_split, r * RING + (s + 1 - RING))
                    load(None, ds(r * RING + s, 1), s)
            for g in range(GROUPS // RING * RING, GROUPS):
                sp.wait_ge(lo_split, g + 1 - RING)
                load(g, ds(g, 1), g % RING)

        @block.gpsimd
        def _(pool):
            def hold(sem, value):
                pool.wait_ge(sem, value)
                pool.sem_inc(pool_held, 1)

            ch = Chain(hold, pool_chain)
            link = ch.link

            def rstd(n, ready, done_sem, value):
                hold(ready, value)
                link(pool.tensor_tensor(MS[:, 0:n], MS[:, 0:n], con("eps")[:, 0:n], ALU.add))
                ins = pool.tensor_tensor(MS[:, 0:n], MS[:, 0:n], con("half")[:, 0:n], ALU.pow)
                if done_sem is None:
                    link(ins)
                else:
                    ins.then_inc(done_sem, 1)

            def rotate(x1, x2, cos, sin, t1, t2, last_sem):
                link(pool.tensor_tensor(t1, x2, sin, ALU.mult))
                link(pool.tensor_tensor(t2, x1, sin, ALU.mult))
                link(pool.tensor_tensor(x1, x1, cos, ALU.mult))
                link(pool.tensor_tensor(x2, x2, cos, ALU.mult))
                link(pool.tensor_tensor(x1, x1, t1, ALU.subtract))
                pool.tensor_tensor(x2, x2, t2, ALU.add).then_inc(last_sem, 1)

            hold(con_loaded, 16)
            rstd(2, norm_ms, norm_rstd, 1)

            hold(prod_free, 2 + 6)
            with pool.Fori(0, 8) as h:
                ch.enter(h, 7)
                H = At(MOBA0, h, 1)
                hold(qk_tr, H.count(1))
                link(pool.tensor_copy(QK[:, 0, :, 0:P], MQKV[:, :, ds(h * P, P)]))
                link(pool.tensor_copy(QK[:, 1, :, 0:P], MQKV[:, :, ds(h * P + W, P)]))
                v = JK[:, 0:128].rearrange("p (z a t d) -> p z a t d", z=2, a=2, t=T)
                tab = [con(n).rearrange("p (a t d) -> p a t d", a=2, t=T) for n in ("mcos", "msin")]
                rotate(QK[:, :, :, 0:16], QK[:, :, :, 16:32], tab[0], tab[1], v[:, 0], v[:, 1], qk_fixed)
            ch.leave(8)

            hold(prod_free, 2 + 6 + 8)
            cos = con("rcos").rearrange("p (t d) -> p t d", t=T)
            sin = con("rsin").rearrange("p (t d) -> p t d", t=T)
            tmp = JK[:, 0:256].rearrange("p (t d) -> p t d", t=T)
            with pool.Fori(0, 4) as h:
                ch.enter(h, 2 * 5 + 1 + 1)
                H = At(RET0, h, 1)
                hold(qk_tr, H.count(1))
                for a in range(2):
                    x1 = PA[:, :, ds(h * 256 + a * W, P)]
                    x2 = PA[:, :, ds(h * 256 + (a * W + P), P)]
                    y1, y2 = QK[:, a, :, 0:P], QK[:, a, :, P:256]
                    link(pool.tensor_tensor(y1, x1, cos, ALU.mult))
                    link(pool.tensor_tensor(tmp, x2, sin, ALU.mult))
                    link(pool.tensor_tensor(y1, y1, tmp, ALU.subtract))
                    link(pool.tensor_tensor(y2, x2, cos, ALU.mult))
                    link(pool.tensor_tensor(tmp, x1, sin, ALU.mult))
                    ins = pool.tensor_tensor(y2, y2, tmp, ALU.add)
                    if a:
                        ins.then_inc(qk_fixed, 1)
                    else:
                        link(ins)
                hold(o_ms, At(0, h, 1).count(1))
                link(pool.tensor_tensor(MS[:, 0:2], MS[:, 0:2], con("eps")[:, 0:2], ALU.add))
                pool.tensor_tensor(MS[:, 0:2], MS[:, 0:2], con("half")[:, 0:2], ALU.pow).then_inc(o_rstd, 1)
            ch.leave(4)

            hold(head_out, RET0 + 4 + 1)
            hold(pos_loaded, 32)
            with pool.Fori(0, NCH) as i:
                for seg in range(3):
                    hold(dist_used, At(seg + 1, i, 3).count())
                    q = POSB[:, ds(i * 8 + (32 if seg else 0), 8)].unsqueeze(2).broadcast_to([P, 8, P])
                    k = POSB[:, 64 + (P if seg == 2 else 0):64 + (P if seg == 2 else 0) + P].unsqueeze(1).broadcast_to([P, 8, P])
                    pool.tensor_tensor(DI[:], q, k, ALU.subtract).then_inc(dist_ready, 1)

            rstd(2, norm_ms, norm_rstd, 2)
            rstd(2, norm_ms, norm_rstd, 3)
            rstd(2, norm_ms, norm_rstd, 4)
            rstd(2, norm_ms, norm_rstd, 5)

            def normed(H, N, d, copies, gains, rope):
                hold(qk_tr, H.count(1))
                for n, (dst, src) in enumerate(copies):
                    ins = pool.tensor_copy(dst, src)
                    if n + 1 < len(copies):
                        link(ins)
                    else:
                        ins.then_inc(qk_raw, 1)
                rstd(4, qk_ms, None, N.count(1))
                f = QK[:, :, :, 0:d].rearrange("p a t d -> p (a t) d")
                ins = pool.tensor_tensor(f, f, MS[:, 0:4].unsqueeze(2).broadcast_to([P, 4, d]), ALU.mult)
                if not gains:
                    ins.then_inc(qk_fixed, 1)
                    return
                link(ins)
                for a, name in enumerate(gains):
                    f = QK[:, a, :, 0:d]
                    link(pool.tensor_tensor(f, f, par(name, 0, d).unsqueeze(1).broadcast_to([P, T, d]), ALU.mult))
                t = JK[:, 0:256].rearrange("p (z a t d) -> p z a t d", z=2, a=2, t=T)
                rotate(QK[:, :, :, P:P + 32], QK[:, :, :, P + 32:P + 64], ROPE[:, 0], ROPE[:, 1], t[:, 0], t[:, 1], qk_fixed)

            hold(x_stored, 16)
            hold(prod_free, 2 + PROD0["a_proj"])
            with pool.Fori(0, 4) as h:
                ch.enter(h, 3)
                normed(At(C0, h, 1), At(C0 - NORM0, h, 1), 256,
                       [(QK[:, 0], PB[:, :, ds(h * 256, 256)]), (QK[:, 1], CKV[:, :, ds(h * 256, 256)])], None, False)
            ch.leave(4)

            hold(prod_free, 2 + PROD0["b_proj"])
            hold(head_out, C0 + 4 + 1)
            link(pool.tensor_copy(QK[:, 1, :, 0:64], PA[:, :, 3584:3648]))
            pool.tensor_copy(QK[:, 1, :, 64:P], PA[:, :, 3584:3648]).then_inc(idx_fixed, 1)
            with pool.Fori(0, 8) as p:
                hold(idx_tr, At(2, p, 1).count())
                pool.tensor_copy(QK[:, 0, :, 0:P], PA[:, :, ds(p * P + 2560, P)]).then_inc(idx_fixed, 1)

            hold(sel_ready, 1)
            with pool.Fori(0, 2) as kv:
                ch.enter(kv, 4 * 3)
                for r in range(4):
                    normed(At(A0 + r, kv, 4), At(A0 - NORM0 + r, kv, 4), P,
                           [(QK[:, 0, :, 0:P], PA[:, :, ds(kv * CH + r * P, P)]),
                            (QK[:, 1, :, 0:P], PA[:, :, ds(kv * P + W, P)])], None, False)
            ch.leave(2)

            hold(lat_ms, 1)
            link(pool.tensor_tensor(MS[:, 0:4], MS[:, 0:4], con("eps")[:, 0:4], ALU.add))
            pool.tensor_tensor(MS[:, 0:4], MS[:, 0:4], con("half")[:, 0:4], ALU.pow).then_inc(lat_rstd, 1)

            hold(prod_free, 2 + PROD0["merge2"])
            hold(rope_ready, 1)
            with pool.Fori(0, 8) as h:
                ch.enter(h, 4 + 1 + 2 + 5)
                normed(At(B0, h, 1), At(B0 - NORM0, h, 1), 192,
                       [(QK[:, 0, :, 0:192], QB[:, :, ds(h * 192, 192)]), (QK[:, 1, :, 0:P], KVB[:, :, ds(h * 256, P)]),
                        (QK[:, 1, :, P:192], PB[:, :, 768:832])], ("bq", "bk"), True)
            ch.leave(8)

        @block.tensor
        def _(pe):
            def group(g, j, body):
                pe.wait_ge(lo_split, g.count(j + 1))
                body(g.slot(j)).then_inc(group_used, 1)

            def rows_product(g, n, j, q, nq, left):
                pair = 2 * (n % 2)

                def body(slot):
                    for kk in range(GK):
                        k = q * GK + kk
                        for t in range(T):
                            hi, lo = left[:, k, 0, t * P:(t + 1) * P], left[:, k, 1, t * P:(t + 1) * P]
                            o = PS[:, pair + t, :]
                            pe.matmul(o, hi, WH[:, slot, kk, :], start=k == 0, stop=False)
                            pe.matmul(o, hi, WL[:, slot, kk, :], start=False, stop=False)
                            ins = pe.matmul(o, lo, WH[:, slot, kk, :], start=False, stop=k == nq * GK - 1)
                    return ins
                group(g, j, body)

            def product(g, n, j, nq, left, steps=None):
                pe.wait_ge(prod_free, n.count(1))
                for q in range(nq):
                    rows_product(g, n.base, j + q, q, nq, left)
                    if steps:
                        steps(j + q)

            def product_loop(name, iters, parts, steps=None):
                per = sum(nq for nq, _ in parts)
                with pe.Fori(0, iters) as i:
                    j = 0
                    for m, (nq, left) in enumerate(parts):
                        g, n = At(GROUP0[name], i, per), At(PROD0[name] + m, i, len(parts))
                        product(g, n, j, nq, left, (lambda p: steps(i, p)) if steps else None)
                        j += nq

            def transposed(name, src, count, wait_sem, wait_value):
                pe.wait_ge(wait_sem, wait_value)
                for k in range(count):
                    at = TR[name] + k
                    if k >= 4:
                        pe.wait_ge(tr_lo, at - 3)
                    for t in range(T):
                        ins = pe.transpose(PS[:, 4 + k % 4, t * P:(t + 1) * P], src(k, t), ident)
                    ins.then_inc(tr_done, 1)

            def head_transpose(br, H):
                pe.wait_ge(qk_fixed, H.count(1))
                pe.wait_ge(head_out, H.count(1))
                for a in range(2):
                    for c, n in enumerate(br["d"]):
                        for t in range(T):
                            ins = pe.transpose(PS[0:n, 4 + a, c * S + t * P:c * S + (t + 1) * P],
                                               QK[:, a, t, c * P:c * P + n], ident)
                ins.then_inc(qk_tr, 1)

            def head_scores(br, H):
                pe.wait_ge(qkt_ready, H.count(1))
                last = len(br["d"]) - 1
                col = 0
                for t in range(T):
                    keys = (t + 1) * P if br["causal"] else S
                    for c, n in enumerate(br["d"]):
                        ins = pe.matmul(PS[:, 6, col:col + keys], QKT[0:n, 0, c, t * P:(t + 1) * P],
                                        QKT[0:n, 1, c, 0:keys], start=c == 0, stop=c == last)
                    col += keys
                ins.then_inc(scores, 1)

            def head_probs(br, H):
                pe.wait_ge(probs, H.count(1))
                src = SC if br is RET else PR
                for b in range(3 if br["causal"] else 4):
                    ins = pe.transpose(PS[:, 7, b * P:(b + 1) * P], src[:, b * P:(b + 1) * P], ident)
                ins.then_inc(pt_done, 1)

            def head_values(br, H, v):
                pe.wait_ge(pt_ready, H.count(1))
                dv = br["dv"]
                blocks = ([[0], [1, 2]] if br["causal"] else [[0, 1], [2, 3]])
                for t in range(T):
                    for s, b in enumerate(blocks[t]):
                        ins = pe.matmul(PS[:, 4, t * dv:(t + 1) * dv], PT[:, b * P:(b + 1) * P], v(s),
                                        start=s == 0, stop=s == len(blocks[t]) - 1)
                ins.then_inc(pv_done, 1)

            def head_output(br, H):
                pe.wait_ge(o_rows, H.count(1))
                for c in range(br["dv"] // P):
                    for t in range(T):
                        ins = pe.transpose(PS[:, 5, c * S + t * P:c * S + (t + 1) * P], OF[:, t, c * P:(c + 1) * P], ident)
                ins.then_inc(ot_done, 1)

            def head_steps(br, H, v):
                return {0: lambda: head_transpose(br, H), 1: lambda: head_scores(br, H), 3: lambda: head_probs(br, H),
                        4: lambda: head_values(br, H, v), 6: lambda: head_output(br, H)}

            pe.wait_ge(con_loaded, 16)
            pe.sem_inc(qk_tr, 1)
            pe.sem_inc(idx_tr, 1)
            pe.sem_inc(bias_done, 1)
            transposed("h1", lambda k, t: PB[:, t, k * P:(k + 1) * P], KT, norm_rows, 1)
            pe.wait_ge(tr_lo, TR["h1"] + KT)
            product_loop("moba_proj", 3, [(GD, HT)] * 2)

            def moba_step(i, p):
                for r in range(2):
                    h = i * 2 + r
                    st = head_steps(MOBA, At(MOBA0 + r, i, 2), lambda s: MQKV[:, s, ds(h * P + 2 * W, P)])
                    if p - 8 * r in st:
                        st[p - 8 * r]()
            product_loop("ret_proj", 4, [(GD, HT)] * 2, moba_step)
            with pe.Fori(0, 4) as h:
                for step in head_steps(RET, At(RET0, h, 1), lambda s: PA[:, s, ds(h * 256 + 2 * W, 256)]).values():
                    step()

            def bias_step(i, p):
                if p % 8 != 3:
                    return
                k = At(p // 8, i, 3)
                pe.wait_ge(onehot, k.count(1))
                pe.wait_ge(bias_copied, k.count(1))
                for b in range(2):
                    ins = pe.matmul(PS[0:32, 4 + b, :], par("rel", 0, 32),
                                    OH[:, 4 * b:4 * b + 4, :].rearrange("p q s -> p (q s)"), start=True, stop=True)
                ins.then_inc(bias_done, 1)
            pe.wait_ge(head_out, RET0 + 4 + 1)
            product_loop("merge1", NCH, [(GD, HT), (GW, U[0]), (GD, HT), (GW, U[1])], bias_step)
            transposed("merged1", lambda k, t: MERGED[:, t, k * P:(k + 1) * P], KT, merged_ready, 1)
            pe.wait_ge(tr_lo, TR["merged1"] + KT)
            product_loop("out1", 2, [(GD, HT)] * 2)
            pe.wait_ge(norm_ms, 3)
            transposed("mem", lambda k, t: PB[:, t, k * P:(k + 1) * P], KT, norm_rows, 2)
            pe.wait_ge(tr_lo, TR["mem"] + KT)
            transposed("h2", lambda k, t: PB[:, t, k * P:(k + 1) * P], KT, norm_rows, 3)
            pe.wait_ge(tr_lo, TR["h2"] + KT)

            def ffn_up(g, u, j):
                half = 4 * (u.base % 2)
                pe.wait_ge(ffn_free, u.count(1))
                for q in range(GD):
                    def body(slot):
                        for kk in range(GK):
                            k = q * GK + kk
                            for f in range(FT):
                                pe.matmul(PS[:, half + f, :], WH[:, slot, kk, f * P:(f + 1) * P], HT[:, k, :, :],
                                          start=k == 0, stop=False, skip_group_check=True)
                                ins = pe.matmul(PS[:, half + f, 0:S], WL[:, slot, kk, f * P:(f + 1) * P], HT[:, k, 0, :],
                                                start=False, stop=k == KT - 1, skip_group_check=True)
                        return ins
                    group(g, j + q, body)

            def ffn_down(g, u, j, blk):
                for c in range(NCH):
                    v = At(u.base + c // 2, u.i, u.per)
                    if c % 2 == 0:
                        pe.wait_ge(ffn_free, v.count(1))
                    if c == 0:
                        pe.wait_ge(ffn_lo, blk.count(1))
                    for q in range(2):
                        def body(slot):
                            for kk in range(GK):
                                k = q * GK + kk
                                for t in range(T):
                                    hi, lo = ACTT[:, k, 0, t * P:(t + 1) * P], ACTT[:, k, 1, t * P:(t + 1) * P]
                                    o = PS[:, 4 * (v.base % 2) + 2 * (c % 2) + t, :]
                                    pe.matmul(o, hi, WH[:, slot, kk, :], start=k == 0, stop=False)
                                    pe.matmul(o, hi, WL[:, slot, kk, :], start=False, stop=False)
                                    ins = pe.matmul(o, lo, WH[:, slot, kk, :], start=False, stop=k == FT - 1)
                            return ins
                        group(g, j + 2 * c + q, body)

            g0 = GROUP0["ffn"]
            ffn_up(At(g0), At(0), 0)
            ffn_up(At(g0), At(1), GD)
            with pe.Fori(0, FB - 1) as b:
                g = At(g0 + 2 * GD, b, 3 * GD)
                ffn_up(g, At(2, b, 4), 0)
                ffn_up(g, At(3, b, 4), GD)
                ffn_down(g, At(4, b, 4), 2 * GD, At(0, b, 1))
            ffn_down(At(g0 + (3 * FB - 1) * GD), At(4 * FB - 2), 0, At(FB - 1))
            pe.wait_ge(ffn_free, 2 + 4 * FB)

            product_loop("mem", 2, [(GD, MEMT)] * 2)
            transposed("h3", lambda k, t: PB[:, t, k * P:(k + 1) * P], KT, norm_rows, 5)
            pe.wait_ge(tr_lo, TR["h3"] + KT)
            product_loop("c_proj", 2, [(GD, HT)] * 2)

            def c_step(i, p):
                st = head_steps(CMEM, At(C0, i, 1), lambda s: CKV[:, s, ds(i * 256 + W, 256)])
                if p % 2 == 0 and p // 2 - 1 in st:
                    st[p // 2 - 1]()
            product_loop("a_proj", 4, [(GD, HT)] * 2, c_step)

            pe.wait_ge(idx_fixed, 1)
            for t in range(T):
                ins = pe.transpose(PS[:, 5, t * P:(t + 1) * P], QK[:, 1, t, 0:P], ident)
            ins.then_inc(idx_tr, 1)

            def index_step(i, p):
                r = p // 4
                k = At(r, i, 4)
                if p % 4 == 0:
                    pe.wait_ge(idx_fixed, k.count(2))
                    for t in range(T):
                        ins = pe.transpose(PS[:, 4, t * P:(t + 1) * P], QK[:, 0, t, 0:P], ident)
                    ins.then_inc(idx_tr, 1)
                elif p % 4 == 1:
                    pe.wait_ge(idx_ready, k.count(2))
                    pe.wait_ge(idx_relu, k.count(1))
                    for j in range(2):
                        q = slice(64 * j, 64 * j + 64)
                        pe.matmul(PS[:, 6 + j, 0:P], QKT[q, 0, 0, 0:P], QKT[q, 1, 0, 0:P], start=True, stop=True)
                        ins = pe.matmul(PS[:, 6 + j, P:CAUS], QKT[q, 0, 0, P:S], QKT[q, 1, 0, :], start=True, stop=True)
                    ins.then_inc(idx_dots, 1)
            product_loop("b_proj", 2, [(GD, HT)] * 2, index_step)

            with pe.Fori(0, 2) as kv:
                for r in range(4):
                    for step in head_steps(ASP, At(A0 + r, kv, 4), lambda s: PA[:, s, ds(kv * P + 1280, P)]).values():
                        step()
            transposed("lat", lambda k, t: PB[:, t, k * P:(k + 1) * P], 6, lat_rows, 1)
            pe.wait_ge(tr_lo, TR["lat"] + 6)
            g0, n0 = GROUP0["b_up"], PROD0["b_up"]
            for c in range(3):
                product(At(g0), At(n0 + c), 2 * c, 2, LATT)
            for c in range(4):
                product(At(g0), At(n0 + 3 + c), 6 + c, 1, LATT[:, 4:6])
            with pe.Fori(0, 8) as h:
                for step in head_steps(BLA, At(B0, h, 1), lambda s: KVB[:, s, ds(h * 256 + P, P)]).values():
                    step()
            pe.wait_ge(head_out, HEADS + 1)
            product_loop("merge2", NCH, [(GD, HT), (GW, U[1]), (GD, HT), (GW, U[2]), (GD, HT), (GW, U[0])])
            transposed("merged2", lambda k, t: MERGED[:, t, k * P:(k + 1) * P], KT, merged_ready, 2)
            pe.wait_ge(tr_lo, TR["merged2"] + KT)
            product_loop("out2", 2, [(GD, HT)] * 2)

        @block.scalar
        def _(act):
            ch = Chain(act.wait_ge, act_chain)
            link = ch.link

            def split(g, j):
                act.wait_ge(raw_landed[g.slot(j)], g.turn(j) * 16 + 16)
                if g.per or g.base + j >= RING:
                    act.wait_ge(group_used, g.count(j + 1 - RING))
                act.activation(WH[:, g.slot(j)], RAW[:, g.slot(j)], ACT.Copy).then_inc(hi_split, 1)

            def evacuate(n, end, dst):
                act.wait_ge(group_used, end)
                pair = 2 * (n.base % 2)
                act.activation(dst, PS[:, pair:pair + 2, :], ACT.Copy).then_inc(prod_free, 1)

            def project(name, iters, dst, steps=None, links=0):
                with act.Fori(0, iters) as i:
                    ch.enter(i, links)
                    g = At(GROUP0[name], i, 2 * GD)
                    for p in range(2 * GD):
                        split(g, p + RING)
                        if p % GD == GD - 1:
                            c = p // GD
                            evacuate(At(PROD0[name] + c, i, 2), g.count(p + 1), dst(i * (2 * CH) + c * CH))
                        if steps:
                            steps(i, p)
                ch.leave(iters)

            def mean_squares(pairs, scale, done, junk=None):
                for n, (src, acc) in enumerate(pairs):
                    o = junk if junk is not None else PS[:, 4:8, :].rearrange("p b n -> p (b n)")
                    ins = act.activation(o, src, ACT.Square, scale=scale, accum_out=acc)
                    if n + 1 < len(pairs):
                        link(ins)
                ins.then_inc(done, 1)

            def transposed(name, dst, count, gain):
                for k in range(count):
                    act.wait_ge(tr_done, TR[name] + k + 1)
                    act.activation(dst[:, k, 0, :], PS[:, 4 + k % 4, 0:S], ACT.Copy,
                                   scale=par(gain, k) if gain else 1.0).then_inc(tr_hi, 1)

            def head_transpose(br, H, gains):
                act.wait_ge(qk_tr, H.count(2))
                for a in range(2):
                    whole = len(set(br["d"])) == 1 and not gains
                    for c, n in enumerate([P] if whole else br["d"]):
                        w = S * len(br["d"]) if whole else S
                        dst = QKT[:, a].rearrange("p c s -> p (c s)")[0:n, c * S:c * S + w]
                        ins = act.activation(dst, PS[0:n, 4 + a, c * S:c * S + w], ACT.Copy,
                                             scale=par(gains[a], c) if gains else 1.0)
                ins.then_inc(qkt_ready, 1)

            def head_exp(br, H, M):
                act.wait_ge(maxima, M.count(1))
                cut = P if br["causal"] else S
                end = CAUS if br["causal"] else 2 * S
                act.activation(PR[:, 0:cut], SC[:, 0:cut], ACT.Exp, bias=NM[:, 0:1], accum_out=RS[:, 0:1])
                act.activation(PR[:, cut:end], SC[:, cut:end], ACT.Exp, bias=NM[:, 1:2], accum_out=RS[:, 1:2]).then_inc(probs, 1)

            def head_probs(br, H):
                act.wait_ge(pt_done, H.count(1))
                n = CAUS if br["causal"] else 512
                act.activation(PT[:, 0:n], PS[:, 7, 0:n], ACT.Copy).then_inc(pt_ready, 1)

            def head_output(br, H, h):
                act.wait_ge(ot_done, H.count(1))
                nd = br["dv"] // P
                for c in range(nd):
                    dst = U[br["u"]][:, ds(h * nd + c, 1), 0, :]
                    ins = act.activation(dst, PS[:, 5:6, c * S:(c + 1) * S], ACT.Copy,
                                         scale=par("ret", h * nd + c) if br is RET else 1.0)
                ins.then_inc(ot_hi, 1)

            def head_squares(br, N):
                act.wait_ge(qk_raw, N.count(1))
                d = sum(br["d"])
                mean_squares([(QK[:, a, t, 0:d], MS[:, 2 * a + t:2 * a + t + 1]) for a in range(2) for t in range(T)],
                             float(d) ** -0.5, qk_ms, JK[:, 0:d])

            def head_steps(br, H, M, h, gains=None):
                return {0: lambda: head_transpose(br, H, gains), 1: lambda: head_exp(br, H, M),
                        3: lambda: head_probs(br, H), 6: lambda: head_output(br, H, h)}

            act.dma_start(CONST[:], constants[:, 0:NCON]).then_inc(con_loaded, 16)
            act.dma_start(DECAY[:].rearrange("p h n -> p (h n)"), constants[:, NCON:]).then_inc(decay_loaded, 16)
            act.dma_start(PARAM[:], params).then_inc(par_loaded, 16)
            act.dma_start(POSI[:], pos_pack[:, POSN:POSN + 2]).then_inc(pos_loaded, 16)
            act.sem_inc(prod_free, 2)
            act.sem_inc(bias_copied, 1)
            act.sem_inc(idx_relu, 1)

            act.wait_ge(ang_ready, 1)
            act.wait_ge(con_loaded, 16)
            for a in range(2):
                act.activation(ROPE[:, 1, a], ANG[:, 0], ACT.Sin)
                ins = act.activation(ROPE[:, 0, a], ANG[:, 1], ACT.Sin, scale=-1.0, bias=con("hpi"))
            ins.then_inc(rope_ready, 1)

            act.wait_ge(x_loaded, 16)
            mean_squares([(X[:, t, :], MS[:, t:t + 1]) for t in range(T)], D ** -0.5, norm_ms)
            act.wait_ge(par_loaded, 16)
            for j in range(RING):
                split(At(0), j)
            transposed("h1", HT, KT, "attn")
            project("moba_proj", 3, lambda c: MQKV[:, :, ds(c, CH)])

            def moba_step(i, p):
                for r in range(2):
                    st = head_steps(MOBA, At(MOBA0 + r, i, 2), At(r, i, 2), i * 2 + r)
                    if p - 8 * r in st:
                        st[p - 8 * r]()
            project("ret_proj", 4, lambda c: PA[:, :, ds(c, CH)], moba_step)

            act.wait_ge(prod_free, 2 + PROD0["merge1"])
            act.activation(PA[:, :, 3 * W:4 * W], PA[:, :, 3 * W:4 * W], ACT.Silu).then_inc(gate_ready, 1)
            with act.Fori(0, 4) as h:
                ch.enter(h, 1)
                H = At(RET0, h, 1)
                head_transpose(RET, H, None)
                head_probs(RET, H)
                act.wait_ge(pv_done, H.count(1))
                mean_squares([(PS[:, 4, t * 256:(t + 1) * 256], MS[:, t:t + 1]) for t in range(T)], 1 / 16.0, o_ms, JK[:])
                head_output(RET, H, h)
            ch.leave(4)

            def merge(name, iters, order, extra=None):
                per = order * (GD + GW)
                with act.Fori(0, iters) as i:
                    g = At(GROUP0[name], i, per)
                    for p in range(per):
                        split(g, p + RING)
                        b, r = p // (GD + GW), p % (GD + GW)
                        if r == GD - 1:
                            n = At(PROD0[name] + 2 * b, i, 2 * order)
                            act.wait_ge(group_used, g.count(p + 1))
                            act.wait_ge(prod_free, n.count(2))
                            pair = 2 * (n.base % 2)
                            act.activation(SG[:], PS[:, pair:pair + 2, :], ACT.Sigmoid).then_inc(prod_free, 1)
                        if extra:
                            extra(i, p)

            def bias_step(i, p):
                if p % 8 != 3:
                    return
                s = p // 8
                k = At(s, i, 3)
                act.wait_ge(bias_done, k.count(2))
                if s:
                    act.wait_ge(bias_stored, k.count() * 16)
                act.activation(BE[:].rearrange("p (b q) s -> p b (q s)", b=2), PS[0:32, 4:6, :], ACT.Copy).then_inc(bias_copied, 1)
                act.wait_ge(bias_copied, k.count(2))
                act.dma_start(bias_scratch[:, s, ds(i * 8, 8), :], BE[:]).then_inc(bias_stored, 16)
                if s == 2:
                    act.wait_ge(bias_stored, k.count(1) * 16)

            act.wait_ge(head_out, RET0 + 4 + 1)
            act.dma_start(POSB[:], pos_pack[:, 0:POSN]).then_inc(pos_loaded, 16)
            merge("merge1", NCH, 2, bias_step)
            act.wait_ge(merged_ready, 1)
            act.dma_start(PB[:], rows(mem_in)).then_inc(mem_loaded, 16)
            act.dma_start(X[:], rows(x_in)).then_inc(x_loaded, 16)
            transposed("merged1", HT, KT, None)
            with act.Fori(0, 2) as i:
                for p in range(2 * GD):
                    split(At(GROUP0["out1"], i, 2 * GD), p + RING)
            act.dma_start(FINALW[:], final_w.partition_broadcast(P)).then_inc(fw_loaded, 16)
            act.wait_ge(mem_loaded, 16)
            mean_squares([(PB[:, t, :], MS[:, t:t + 1]) for t in range(T)], D ** -0.5, norm_ms)
            act.wait_ge(norm_rows, 2)
            act.wait_ge(x_done, 1)
            mean_squares([(X[:, t, :], MS[:, t:t + 1]) for t in range(T)], D ** -0.5, norm_ms)
            transposed("mem", MEMT, KT, "mem")
            transposed("h2", HT, KT, "ffn")

            def up_copy(u, end, f, tile):
                act.wait_ge(group_used, end)
                if tile.per or tile.base >= 2:
                    act.wait_ge(ffn_conv, tile.count(-1))
                act.activation(FC[:, f % 2, :], PS[:, 4 * (u.base % 2) + f, 0:S], ACT.Copy).then_inc(ffn_copied, 1)

            def silu(tile, f, blk):
                act.wait_ge(ffn_conv, tile.count(1))
                act.activation(FA[:, f, :], FY[:, f % 2, :], ACT.Silu).then_inc(ffn_silu, 1)

            def block_hi(blk, end):
                act.wait_ge(ffn_prod, blk.count(1))
                if end is not None:
                    act.wait_ge(group_used, end)
                act.activation(ACTT[:, :, 0, :], FP[:], ACT.Copy).then_inc(ffn_hi, 1)

            g0 = GROUP0["ffn"]
            for p in range(2 * GD):
                split(At(g0), p + RING)
                if 7 <= p <= 10:
                    up_copy(At(0), g0 + GD, p - 7, At(p - 7))
                if 8 <= p <= 11:
                    silu(At(p - 8), p - 8, None)
            for f in range(FT):
                up_copy(At(1), g0 + 2 * GD, f, At(FT + f))
            block_hi(At(0), None)
            with act.Fori(0, FB - 1) as b:
                g = At(g0 + 2 * GD, b, 3 * GD)
                for p in range(3 * GD):
                    split(g, p + RING)
                    if 7 <= p <= 10:
                        up_copy(At(2, b, 4), g.count(GD), p - 7, At(8 + p - 7, b, 8))
                    if 8 <= p <= 11:
                        silu(At(8 + p - 8, b, 8), p - 8, None)
                    if 15 <= p <= 18:
                        up_copy(At(3, b, 4), g.count(2 * GD), p - 15, At(12 + p - 15, b, 8))
                block_hi(At(1, b, 1), g.count(3 * GD))
            for p in range(GD):
                split(At(g0 + (3 * FB - 1) * GD), p + RING)

            act.wait_ge(x_done, 2)
            mean_squares([(X[:, t, :], MS[:, t:t + 1]) for t in range(T)], D ** -0.5, norm_ms)
            act.wait_ge(x_done, 3)
            mean_squares([(X[:, t, :], MS[:, t:t + 1]) for t in range(T)], D ** -0.5, norm_ms)
            act.dma_start(rows(x_scratch), X[:]).then_inc(x_stored, 16)
            project("mem", 2, lambda c: CKV[:, :, ds(c, CH)])
            transposed("h3", HT, KT, "norm2")
            act.wait_ge(x_stored, 16)
            project("c_proj", 2, lambda c: PB[:, :, ds(c, CH)])
            act.wait_ge(prod_free, 2 + PROD0["a_proj"])
            act.activation(PB[:, :, W:2 * W], PB[:, :, W:2 * W], ACT.Silu).then_inc(gate_ready, 1)

            def c_step(i, p):
                if p == 0:
                    head_squares(CMEM, At(C0 - NORM0, i, 1))
                st = head_steps(CMEM, At(C0, i, 1), At(8, i, 1), i, ("cq", "ck"))
                if p % 2 == 0 and p // 2 - 1 in st:
                    st[p // 2 - 1]()
            project("a_proj", 4, lambda c: PA[:, :, ds(c, CH)], c_step, 3)

            act.wait_ge(head_out, C0 + 4 + 1)
            act.wait_ge(bias_stored, 16 * 12)
            for g in range(4):
                act.dma_start(BIAS[32 * g:32 * g + 32, :, :].rearrange("p h (s k) -> p h s k", s=3),
                              bias_scratch[8 * g:8 * g + 8].rearrange("h s p k -> p h s k")).then_inc(bias_loaded, 16)
            act.wait_ge(prod_free, 2 + PROD0["b_proj"])
            act.activation(PA[:, :, 1536:2560], PA[:, :, 1536:2560], ACT.Silu).then_inc(gate_ready, 1)
            act.wait_ge(idx_tr, 2)
            act.activation(QKT[:, 1, 0, :], PS[:, 5, 0:S], ACT.Copy).then_inc(idx_ready, 1)

            def index_step(i, p):
                k = At(p // 4, i, 4)
                if p % 4 == 0:
                    act.wait_ge(idx_tr, k.count(3))
                    act.activation(QKT[:, 0, 0, :], PS[:, 4, 0:S], ACT.Copy).then_inc(idx_ready, 1)
                elif p % 4 == 1:
                    act.wait_ge(idx_dots, k.count(1))
                    act.wait_ge(idx_sum, k.count(1))
                    act.activation(SC[:, 0:CAUS], PS[:, 6, 0:CAUS], ACT.Relu)
                    act.activation(PR[:, 0:CAUS], PS[:, 7, 0:CAUS], ACT.Relu).then_inc(idx_relu, 1)
            project("b_proj", 2, lambda c: PB[:, :, ds(c, CH)], index_step)

            with act.Fori(0, 2) as kv:
                ch.enter(kv, 4 * 3)
                for r in range(4):
                    H = At(A0 + r, kv, 4)
                    head_squares(ASP, At(A0 - NORM0 + r, kv, 4))
                    for step in head_steps(ASP, H, At(12 + r, kv, 4), kv * 4 + r, ("aq", "ak")).values():
                        step()
            ch.leave(2)
            act.wait_ge(prod_free, 2 + PROD0["b_up"])
            act.activation(PB[:, :, 832:832 + W], PB[:, :, 832:832 + W], ACT.Silu).then_inc(gate_ready, 1)
            act.wait_ge(head_out, A0 + 8 + 1)
            for t in range(T):
                act.activation(PS[:, 4 + 2 * t, :], PB[:, t, 0:512], ACT.Square, scale=512 ** -0.5, accum_out=MS[:, t:t + 1])
                ins = act.activation(PS[:, 5 + 2 * t, 0:256], PB[:, t, 512:768], ACT.Square, scale=1 / 16.0,
                                     accum_out=MS[:, 2 + t:3 + t])
            ins.then_inc(lat_ms, 1)
            transposed("lat", LATT, 6, "lat")
            g0, n0 = GROUP0["b_up"], PROD0["b_up"]
            for p in range(10):
                split(At(g0), p + RING)
                if p < 6 and p % 2:
                    evacuate(At(n0 + p // 2), g0 + p + 1, QB[:, :, p // 2 * CH:(p // 2 + 1) * CH])
                if p >= 6:
                    evacuate(At(n0 + 3 + p - 6), g0 + p + 1, KVB[:, :, (p - 6) * CH:(p - 5) * CH])
            with act.Fori(0, 8) as h:
                ch.enter(h, 3)
                head_squares(BLA, At(B0 - NORM0, h, 1))
                for step in head_steps(BLA, At(B0, h, 1), At(20, h, 1), h).values():
                    step()
            ch.leave(8)
            act.wait_ge(head_out, HEADS + 1)
            act.dma_start(X[:], rows(x_scratch)).then_inc(x_back, 16)
            merge("merge2", NCH, 3)
            transposed("merged2", HT, KT, None)
            for p in range(4 * GD):
                if p + RING < 4 * GD:
                    split(At(GROUP0["out2"]), p + RING)
                if p % GD == GD - 1:
                    c = p // GD
                    act.wait_ge(out_ready, c + 1)
                    act.dma_start(rows(out)[:, :, c * CH:(c + 1) * CH], X[:, :, c * CH:(c + 1) * CH]).then_inc(out_stored, 16)
            act.wait_ge(out_stored, 16 * NCH)
            act.wait_ge(bias_stored, 16 * 12)

        @block.vector
        def _(dve):
            ch = Chain(dve.wait_ge, dve_chain)
            link = ch.link

            def split(g, j):
                dve.wait_ge(hi_split, g.count(j + 1))
                s = g.slot(j)
                dve.tensor_tensor(WL[:, s], RAW[:, s], WH[:, s].bitcast(F32), ALU.subtract).then_inc(lo_split, 1)

            def stream(name, iters, per, steps=None):
                with dve.Fori(0, iters) as i:
                    for p in range(per):
                        split(At(GROUP0[name], i, per), p + RING)
                        if steps:
                            steps(i, p)

            def norm_apply(n, src, dst, gain=None):
                dve.wait_ge(norm_rstd, n)
                for t in range(T):
                    if gain is None:
                        ins = dve.tensor_scalar(dst[:, t, :], src[:, t, :], MS[:, t:t + 1], None, ALU.mult)
                    else:
                        ins = dve.scalar_tensor_tensor(out=dst[:, t, :], in0=src[:, t, :], scalar=MS[:, t:t + 1],
                                                       in1=gain, op0=ALU.mult, op1=ALU.mult)
                return ins

            def transposed(name, dst, count, gain):
                for k in range(count):
                    dve.wait_ge(tr_hi, TR[name] + k + 1)
                    hi, ps = dst[:, k, 0, :].bitcast(F32), PS[:, 4 + k % 4, 0:S]
                    if gain:
                        ins = dve.scalar_tensor_tensor(out=dst[:, k, 1, :], in0=ps, scalar=par(gain, k), in1=hi,
                                                       op0=ALU.mult, op1=ALU.subtract)
                    else:
                        ins = dve.tensor_tensor(dst[:, k, 1, :], ps, hi, ALU.subtract)
                    ins.then_inc(tr_lo, 1)

            def head_scores(br, H, M, h):
                dve.wait_ge(scores, H.count(1))
                if br is RET:
                    dve.tensor_tensor(SC[:, 0:CAUS], PS[:, 6, 0:CAUS], DECAY[:, ds(h, 1), :].rearrange("p a n -> p (a n)"),
                                      ALU.mult).then_inc(probs, 1)
                    return
                if br["causal"]:
                    mask = BIAS[:, ds(h, 1), :].rearrange("p a n -> p (a n)") if br is ASP else con("mask")
                    link(dve.scalar_tensor_tensor(out=SC[:, 0:CAUS], in0=PS[:, 6, 0:CAUS], scalar=br["scale"], in1=mask,
                                                  op0=ALU.mult, op1=ALU.add))
                    cut, end = P, CAUS
                else:
                    link(dve.tensor_scalar(SC[:], PS[:, 6, :], br["scale"], None, ALU.mult))
                    cut, end = S, 2 * S
                dve.tensor_reduce(NM[:, 0:1], SC[:, 0:cut], AX_X, ALU.max, negate=True)
                dve.tensor_reduce(NM[:, 1:2], SC[:, cut:end], AX_X, ALU.max, negate=True).then_inc(maxima, 1)

            def head_values(br, H, gate):
                dv = br["dv"]
                if br is RET:
                    dve.wait_ge(o_rstd, At(H.base - RET0, H.i, H.per).count(1))
                    inv = MS
                else:
                    dve.wait_ge(probs, H.count(1))
                    link(dve.reciprocal(RI[:], RS[:]))
                    inv = RI
                dve.wait_ge(pv_done, H.count(1))
                for t in range(T):
                    o, ps = OF[:, t, 0:dv], PS[:, 4, t * dv:(t + 1) * dv]
                    if gate is None:
                        ins = dve.tensor_scalar(o, ps, inv[:, t:t + 1], None, ALU.mult)
                    else:
                        ins = dve.scalar_tensor_tensor(out=o, in0=ps, scalar=inv[:, t:t + 1], in1=gate(t),
                                                       op0=ALU.mult, op1=ALU.mult)
                ins.then_inc(o_rows, 1)

            def head_output(br, H, h):
                dve.wait_ge(ot_hi, H.count(1))
                nd = br["dv"] // P
                for c in range(nd):
                    u = U[br["u"]]
                    hi, lo = u[:, ds(h * nd + c, 1), 0, :].bitcast(F32), u[:, ds(h * nd + c, 1), 1, :]
                    ps = PS[:, 5:6, c * S:(c + 1) * S]
                    if br is RET:
                        ins = dve.scalar_tensor_tensor(out=lo, in0=ps, scalar=par("ret", h * nd + c), in1=hi,
                                                       op0=ALU.mult, op1=ALU.subtract)
                    else:
                        ins = dve.tensor_tensor(lo, ps, hi, ALU.subtract)
                ins.then_inc(head_out, 1)

            def head_steps(br, H, M, h, gate=None):
                return {1: lambda: head_scores(br, H, M, h), 4: lambda: head_values(br, H, gate),
                        6: lambda: head_output(br, H, h)}

            for s, n in ((head_out, 1), (dist_used, 1), (idx_sum, 1), (ffn_free, 2)):
                dve.sem_inc(s, n)

            dve.wait_ge(con_loaded, 16)
            dve.wait_ge(pos_loaded, 16)
            posf = RI
            link(dve.tensor_copy(posf[:], POSI[:]))
            for t in range(T):
                link(dve.tensor_scalar(ANG[:, 0, t], con("freq"), posf[:, t:t + 1], None, ALU.mult))
            ang = ANG[:, 0].rearrange("p t d -> p (t d)")
            mag = ANG[:, 1].rearrange("p t d -> p (t d)")
            turns_i = ANGI[:]
            turns = JK[:, 0:T * 32]
            link(dve.tensor_scalar(turns_i, ang, float(1 / (2 * np.pi)), None, ALU.mult))
            link(dve.tensor_copy(turns, turns_i))
            for part in (6.28125, 0.0019340515136718750, 1.2556659146770e-06):
                link(dve.scalar_tensor_tensor(out=ang, in0=turns, scalar=-part, in1=ang, op0=ALU.mult, op1=ALU.add))
            link(dve.tensor_scalar(ang, ang, 3.1415925, -3.1415925, ALU.min, ALU.max))
            dve.scalar_tensor_tensor(out=mag, in0=ang, scalar=-1.0, in1=ang, op0=ALU.mult, op1=ALU.max).then_inc(ang_ready, 1)

            norm_apply(1, X, PB).then_inc(norm_rows, 1)
            for j in range(RING):
                split(At(0), j)
            dve.wait_ge(par_loaded, 16)
            transposed("h1", HT, KT, "attn")
            stream("moba_proj", 3, 2 * GD)

            with dve.Fori(0, 4) as i:
                ch.enter(i, 4)
                for p in range(2 * GD):
                    split(At(GROUP0["ret_proj"], i, 2 * GD), p + RING)
                    for r in range(2):
                        st = head_steps(MOBA, At(MOBA0 + r, i, 2), At(r, i, 2), i * 2 + r)
                        if p - 8 * r in st:
                            st[p - 8 * r]()
            ch.leave(4)
            dve.wait_ge(gate_ready, 1)
            dve.wait_ge(decay_loaded, 16)
            with dve.Fori(0, 4) as h:
                for step in head_steps(RET, At(RET0, h, 1), None, h, lambda t: PA[:, t, ds(h * 256 + 3 * W, 256)]).values():
                    step()

            def merge(name, order, links, extra=None):
                per = order * (GD + GW)
                with dve.Fori(0, NCH) as i:
                    ch.enter(i, links)
                    g = At(GROUP0[name], i, per)
                    for p in range(per):
                        split(g, p + RING)
                        b, r = p // (GD + GW), p % (GD + GW)
                        if r == GD + GW - 1:
                            n = At(PROD0[name] + 2 * b + 1, i, 2 * order)
                            dve.wait_ge(prod_free, n.count(2))
                            dve.wait_ge(group_used, g.count(p + 1))
                            ps = PS[:, 2 * (n.base % 2):2 * (n.base % 2) + 2, :]
                            m = MERGED[:, :, ds(i * CH, CH)]
                            if b == 0:
                                dve.tensor_tensor(m, ps, SG[:], ALU.mult).then_inc(prod_free, 1)
                            else:
                                dve.tensor_tensor(TMP[:], ps, SG[:], ALU.mult).then_inc(prod_free, 1)
                                dve.wait_ge(prod_free, n.count(3))
                                link(dve.tensor_tensor(m, m, TMP[:], ALU.add))
                        if extra:
                            extra(i, p)
                ch.leave(NCH)
                dve.sem_inc(merged_ready, 1)

            def bias_step(i, p):
                if p % 8 != 2:
                    return
                k = At(p // 8, i, 3)
                dve.wait_ge(dist_ready, k.count(1))
                dve.wait_ge(bias_done, k.count(1))
                link(dve.tensor_scalar(M1[:], DI[:], con("lo"), None, ALU.is_ge))
                dve.scalar_tensor_tensor(out=OH[:], in0=DI[:], scalar=con("hi"), in1=M1[:], op0=ALU.is_lt,
                                         op1=ALU.mult).then_inc(onehot, 1)
                dve.wait_ge(onehot, k.count(1))
                dve.sem_inc(dist_used, 1)
            merge("merge1", 2, 1 + 3, bias_step)
            transposed("merged1", HT, KT, None)

            def residual(name):
                def steps(i, p):
                    if p % GD == GD - 1:
                        c = p // GD
                        n = At(PROD0[name] + c, i, 2)
                        dve.wait_ge(group_used, At(GROUP0[name], i, 2 * GD).count(p + 1))
                        o = X[:, :, ds(i * (2 * CH) + c * CH, CH)]
                        dve.tensor_tensor(o, PS[:, 2 * (n.base % 2):2 * (n.base % 2) + 2, :], o, ALU.add)\
                           .then_inc(prod_free, 1)
                return steps
            dve.wait_ge(x_loaded, 32)
            stream("out1", 2, 2 * GD, residual("out1"))
            dve.wait_ge(prod_free, 2 + PROD0["mem"])
            dve.sem_inc(x_done, 1)
            norm_apply(2, PB, PB).then_inc(norm_rows, 1)
            transposed("mem", MEMT, KT, "mem")
            norm_apply(3, X, PB).then_inc(norm_rows, 1)
            link(dve.memset(FU[:, :, 0:2], 0.0))
            transposed("h2", HT, KT, "ffn")

            def conv(u, f, tile, feature, silu_done):
                dve.wait_ge(ffn_copied, tile.count(1))
                z, y = FU[:, f % 2, :], FY[:, f % 2, :]
                ins = dve.tensor_tensor(z[:, 2:S + 2], PS[:, 4 * (u.base % 2) + f, S:2 * S], FC[:, f % 2, :], ALU.add)
                link(ins)
                if f == FT - 1:
                    dve.sem_inc(ffn_free, 1)
                if silu_done is not None:
                    dve.wait_ge(ffn_silu, silu_done)
                link(dve.tensor_scalar(y, z[:, 2:S + 2], par("conv", feature * 4 + 2), par("conv", feature * 4 + 3),
                                       ALU.mult, ALU.add))
                link(dve.scalar_tensor_tensor(out=y, in0=z[:, 1:S + 1], scalar=par("conv", feature * 4 + 1), in1=y,
                                              op0=ALU.mult, op1=ALU.add))
                return dve.scalar_tensor_tensor(out=y, in0=z[:, 0:S], scalar=par("conv", feature * 4), in1=y,
                                                op0=ALU.mult, op1=ALU.add)

            def a_tile(u, f, tile, feature, silu_done):
                conv(u, f, tile, feature, silu_done).then_inc(ffn_conv, 1)

            def b_tile(u, f, tile, feature, silu_done):
                conv(u, f, tile, feature, silu_done).then_inc(ffn_conv, 1)
                dve.wait_ge(ffn_conv, tile.count(1))
                ins = dve.tensor_tensor(FP[:, f, :], FA[:, f, :], FY[:, f % 2, :], ALU.mult)
                if f == FT - 1:
                    ins.then_inc(ffn_prod, 1)

            def block_lo(blk):
                dve.wait_ge(ffn_hi, blk.count(1))
                dve.tensor_tensor(ACTT[:, :, 1, :], FP[:], ACTT[:, :, 0, :].bitcast(F32), ALU.subtract).then_inc(ffn_lo, 1)

            def down_add(u, end):
                dve.wait_ge(group_used, end)
                half, c0 = 4 * (u.base % 2), 2 * (u.base % 2)
                for c in range(2):
                    o = X[:, :, (c0 + c) * CH:(c0 + c + 1) * CH]
                    ins = dve.tensor_tensor(o, PS[:, half + 2 * c:half + 2 * c + 2, :], o, ALU.add)
                ins.then_inc(ffn_free, 1)

            g0 = GROUP0["ffn"]
            for p in range(2 * GD):
                split(At(g0), p + RING)
                if 7 <= p <= 10:
                    f = p - 7
                    a_tile(At(0), f, At(f), f, f - 1 if f >= 2 else None)
            for f in range(FT):
                b_tile(At(1), f, At(FT + f), NFT // 2 + f, FT)
            block_lo(At(0))
            with dve.Fori(0, FB - 1) as b:
                ch.enter(b, 3 * 2 * FT)
                g = At(g0 + 2 * GD, b, 3 * GD)
                for p in range(3 * GD):
                    split(g, p + RING)
                    if 7 <= p <= 10:
                        f = p - 7
                        a_tile(At(2, b, 4), f, At(8 + f, b, 8), b * FT + (FT + f),
                               At(FT + f - 1, b, FT).count() if f >= 2 else None)
                    if 15 <= p <= 18:
                        f = p - 15
                        b_tile(At(3, b, 4), f, At(12 + f, b, 8), b * FT + (NFT // 2 + FT + f), At(2 * FT, b, FT).count())
                    if p == 19:
                        down_add(At(4, b, 4), g.count(2 * GD + 4))
                    if p == 23:
                        down_add(At(5, b, 4), g.count(3 * GD))
                block_lo(At(1, b, 1))
            ch.leave(FB - 1)
            for p in range(GD):
                split(At(g0 + (3 * FB - 1) * GD), p + RING)
                if p == 3:
                    down_add(At(4 * FB - 2), g0 + (3 * FB - 1) * GD + 4)
                if p == 7:
                    down_add(At(4 * FB - 1), g0 + 3 * FB * GD)
            dve.wait_ge(ffn_free, 2 + 4 * FB)
            dve.sem_inc(x_done, 1)
            dve.wait_ge(fw_loaded, 16)
            link(norm_apply(4, X, X, FINALW[:]))
            dve.sem_inc(x_done, 1)
            norm_apply(5, X, PB).then_inc(norm_rows, 2)
            stream("mem", 2, 2 * GD)
            transposed("h3", HT, KT, "norm2")
            stream("c_proj", 2, 2 * GD)

            dve.wait_ge(gate_ready, 2)
            with dve.Fori(0, 4) as i:
                ch.enter(i, 2)
                st = head_steps(CMEM, At(C0, i, 1), At(8, i, 1), i, lambda t: PB[:, t, ds(i * 256 + W, 256)])
                for p in range(2 * GD):
                    split(At(GROUP0["a_proj"], i, 2 * GD), p + RING)
                    if p % 2 == 0 and p // 2 - 1 in st:
                        st[p // 2 - 1]()
            ch.leave(4)

            link(dve.memset(PT[:, 0:CAUS], 0.0))
            dve.wait_ge(prod_free, 2 + PROD0["b_proj"])
            with dve.Fori(0, 2) as i:
                ch.enter(i, 4 * 2)
                for p in range(2 * GD):
                    split(At(GROUP0["b_proj"], i, 2 * GD), p + RING)
                    if p % 4 == 2:
                        k = At(p // 4, i, 4)
                        dve.wait_ge(idx_relu, k.count(2))
                        for j, src in enumerate((SC, PR)):
                            for t, cols in enumerate((slice(0, P), slice(P, CAUS))):
                                w = PA[:, t, ds(i * 8 + (3648 + 2 * (p // 4) + j), 1)]
                                ins = dve.scalar_tensor_tensor(out=PT[:, cols], in0=src[:, cols], scalar=w, in1=PT[:, cols],
                                                               op0=ALU.mult, op1=ALU.add)
                            link(ins)
                        dve.sem_inc(idx_sum, 1)
            ch.leave(2)

            masked, left = SC, OF[:].rearrange("p t d -> p (t d)")
            link(dve.tensor_tensor(masked[:, 0:CAUS], PT[:, 0:CAUS], con("mask"), ALU.add))
            src = masked
            for _ in range(8):
                for t, cols in enumerate((slice(0, P), slice(P, CAUS))):
                    ins = dve.max(M8[:, t, :], src[:, cols])
                link(ins)
                for t, cols in enumerate((slice(0, P), slice(P, CAUS))):
                    ins = dve.match_replace(left[:, cols], M8[:, t, :], src[:, cols], TAKEN)
                link(ins)
                src = left
            link(dve.tensor_scalar(left[:, 0:CAUS], left[:, 0:CAUS], TAKEN, -1.0, ALU.is_equal, ALU.add))
            link(dve.scalar_tensor_tensor(out=SC[:, 0:CAUS], in0=left[:, 0:CAUS], scalar=-NEG, in1=con("mask"),
                                          op0=ALU.mult, op1=ALU.add))
            dve.wait_ge(bias_loaded, 64)
            dve.tensor_tensor(BIAS[:], BIAS[:], SC[:, 0:CAUS].unsqueeze(1).broadcast_to([P, REL_HEADS, CAUS]),
                              ALU.add).then_inc(sel_ready, 1)

            dve.wait_ge(sel_ready, 1)
            dve.wait_ge(gate_ready, 3)
            with dve.Fori(0, 2) as kv:
                ch.enter(kv, 4 * 2)
                for r in range(4):
                    for step in head_steps(ASP, At(A0 + r, kv, 4), At(12 + r, kv, 4), kv * 4 + r,
                                           lambda t: PA[:, t, ds(kv * CH + (1536 + r * P), P)]).values():
                        step()
            ch.leave(2)
            dve.wait_ge(lat_rstd, 1)
            for t in range(T):
                dve.tensor_scalar(PB[:, t, 0:512], PB[:, t, 0:512], MS[:, t:t + 1], None, ALU.mult)
                ins = dve.tensor_scalar(PB[:, t, 512:768], PB[:, t, 512:768], MS[:, 2 + t:3 + t], None, ALU.mult)
            ins.then_inc(lat_rows, 1)
            transposed("lat", LATT, 6, "lat")
            for p in range(10):
                split(At(GROUP0["b_up"]), p + RING)
            dve.wait_ge(gate_ready, 4)
            with dve.Fori(0, 8) as h:
                ch.enter(h, 2)
                for step in head_steps(BLA, At(B0, h, 1), At(20, h, 1), h, lambda t: PB[:, t, ds(h * P + 832, P)]).values():
                    step()
            ch.leave(8)
            merge("merge2", 3, 2)
            transposed("merged2", HT, KT, None)
            dve.wait_ge(x_back, 16)
            for p in range(4 * GD):
                if p + RING < 4 * GD:
                    split(At(GROUP0["out2"]), p + RING)
                if p % GD == GD - 1:
                    c = p // GD
                    n = PROD0["out2"] + c
                    dve.wait_ge(group_used, GROUP0["out2"] + p + 1)
                    o = X[:, :, c * CH:(c + 1) * CH]
                    link(dve.tensor_tensor(o, PS[:, 2 * (n % 2):2 * (n % 2) + 2, :], o, ALU.add))
                    dve.sem_inc(prod_free, 1)
                    dve.sem_inc(out_ready, 1)


def groups_of(w):
    k, n = w.shape
    return w.reshape(k // (GK * P), GK, P, n // CH, CH).transpose(3, 0, 2, 1, 4).reshape(n // CH, -1, P, GK * CH)


def lay_out(x):
    w_in, w_in2 = x["w_in"][0], x["w_in_2"][0]
    stream = np.empty((GROUPS, P, GK * CH), np.float32)
    at = [0]

    def put(*parts):
        for c in range(len(parts[0])):
            for part in parts:
                stream[at[0]:at[0] + part.shape[1]] = part[c]
                at[0] += part.shape[1]

    def padded(w, n):
        return np.concatenate([w, np.zeros((w.shape[0], n - w.shape[1]), w.dtype)], 1)

    put(groups_of(w_in[:, 4 * W:7 * W]))
    put(groups_of(w_in[:, 0:4 * W]))
    gates = 7 * W
    put(groups_of(w_in[:, gates:gates + D]), groups_of(x["w_ret_up"][0]),
        groups_of(w_in[:, gates + D:gates + 2 * D]), groups_of(x["w_moba_up"][0]))
    put(groups_of(x["w_out"][0]))
    up, down = groups_of(x["w_ffn_up"][0]), x["w_ffn_down"][0]
    for b in range(FB + 1):
        if b < FB:
            put(up[b:b + 1])
            put(up[FB + b:FB + b + 1])
        if b:
            put(groups_of(down[(b - 1) * CH:b * CH]))
    put(groups_of(x["w_mem_kv_2"][0]))
    put(groups_of(w_in2[:, 5520:7568]))
    put(groups_of(padded(w_in2[:, 0:3664], 4096)))
    put(groups_of(padded(w_in2[:, 3664:5520], 2048)))
    put(groups_of(x["w_b_uq_2"][0]))
    put(groups_of(x["w_b_ukv_2"][0]))
    branch = x["w_branch_2"][0]
    parts = []
    for b in range(3):
        parts += [groups_of(w_in2[:, 7568 + b * D:7568 + (b + 1) * D]), groups_of(branch[b])]
    put(*parts)
    put(groups_of(x["w_out_2"][0]))
    assert at[0] == GROUPS

    pack = np.zeros((P, NPAR), np.float32)

    def par(name, value):
        o, n = PAR[name]
        pack[:, o:o + n] = value

    def columns(v):
        return v.reshape(-1, P).T

    par("attn", columns(x["attn_norm_w"]))
    par("ffn", columns(x["ffn_norm_w"]))
    par("norm2", columns(x["norm_g_2"]))
    par("mem", columns(x["mem_norm_g_2"]))
    par("ret", columns(x["ret_norm_w"]))
    par("aq", columns(x["a_q_norm_g_2"]))
    par("ak", columns(x["a_k_norm_g_2"]))
    par("lat", np.concatenate([columns(x["b_q_lat_norm_g_2"]), columns(x["b_kv_lat_norm_g_2"])], 1))
    par("cq", columns(x["c_q_norm_g_2"]))
    par("ck", columns(x["c_k_norm_g_2"]))
    par("bq", x["b_q_norm_g_2"])
    par("bk", x["b_k_norm_g_2"])
    taps = np.concatenate([x["conv_w"][0], x["conv_b"]], 0)
    par("conv", taps.reshape(4, NFT, P).transpose(2, 1, 0).reshape(P, -1))
    table = np.zeros((P, 32), np.float32)
    for g in range(4):
        table[32 * g:32 * g + 32, 8 * g:8 * g + 8] = x["rel_bias_2"]
    par("rel", table)

    pos = x["positions_2"].reshape(S)
    ints = np.zeros((P, POSN + 2), np.int32)
    for g in range(4):
        rows = slice(32 * g, 32 * g + 32)
        ints[rows, 0:32] = pos[32 * g:32 * g + 32]
        ints[rows, 32:64] = pos[P + 32 * g:P + 32 * g + 32]
    ints[:, 64:POSN] = pos
    ints[:, POSN:] = pos.reshape(T, P).T
    return stream, pack, ints


def kernel(**inputs):
    import concourse.bacc as bacc
    from concourse.bass_utils import run_bass_kernel_spmd

    x = {name: np.asarray(a) for name, a in inputs.items()}
    stream, pack, ints = lay_out(x)
    arrays = {"x_in": x["x"].reshape(S, D), "mem_in": x["mem_2"].reshape(S, D), "w_stream": stream, "params": pack,
              "final_w": x["final_norm_w"], "pos_pack": ints, "constants": make_constants()}
    arrays = {name: np.ascontiguousarray(a) for name, a in arrays.items()}
    nc = bacc.Bacc("TRN2", target_bir_lowering=False, num_devices=1)
    args = [nc.dram_tensor(name, a.shape, mybir.dt.from_np(a.dtype), kind="ExternalInput").ap() for name, a in arrays.items()]
    out = nc.dram_tensor("out", (S, D), F32, kind="ExternalOutput").ap()
    build(nc, *args, out)
    r = run_bass_kernel_spmd(nc, [arrays], core_ids=[0])
    return r.results[0]["out"].reshape(1, S, D)
```

```python
from contextlib import ExitStack

import concourse.bass as bass
import numpy as np
from concourse import mybir

F32 = mybir.dt.float32
F32R = mybir.dt.float32r
I32 = mybir.dt.int32
ALU = mybir.AluOpType
ACT = mybir.ActivationFunctionType
AX_X = mybir.AxisListType.X
ds = bass.ds

P = 128
D = 2048
S = 256
T = S // P
FF = 5632
CH = 512
GK = 2
KT = D // P
RING = 4
EPS = 1e-6
NEG = -1.0e30
TAKEN = -3.0e38
W = 1024
NCH = D // CH
GD = KT // GK
GW = W // P // GK
FB = FF // CH
FT = CH // P
NFT = 2 * FF // P
CAUS = 3 * P
BUCKETS, REL_HEADS = 32, 8
NBIAS = NCH * 3
POSN = 64 + S

PHASES = [
    ("moba_proj", 6 * GD, 6), ("ret_proj", 8 * GD, 8), ("merge_moba", NCH * (GD + GW), 2 * NCH),
    ("gates_ret", NCH * GD, NCH), ("up_ret", NCH * GW, NCH), ("out1", NCH * GD, NCH), ("ffn", FB * 3 * GD, 0),
    ("mem", NCH * GD, NCH), ("c_proj", 4 * GD, 4), ("a_proj", 8 * GD, 8), ("b_proj", 4 * GD, 4),
    ("merge_c", NCH * (GD + GW), 2 * NCH), ("b_up", 3 * 2 + 4, 7), ("merge_a", NCH * (GD + GW), 2 * NCH),
    ("gates_b", NCH * GD, NCH), ("up_b", NCH * GW, NCH), ("out2", NCH * GD, NCH)]
GROUP0, PROD0 = {}, {}
_g = _n = 0
for _name, _groups, _prods in PHASES:
    GROUP0[_name], PROD0[_name] = _g, _n
    _g, _n = _g + _groups, _n + _prods
GROUPS = _g

MOBA0, RET0, C0, A0, B0, HEADS = 0, 8, 12, 16, 24, 32

PAR = {}


def _columns(table, *widths):
    at = 0
    for name, n in widths:
        table[name] = (at, n)
        at += n
    return at


NPAR = _columns(PAR, ("attn", KT), ("ffn", KT), ("norm2", KT), ("mem", KT), ("ret", 8), ("aq", 1), ("ak", 1),
                ("lat", 6), ("cq", 2), ("ck", 2), ("bqn", 1), ("bkn", 1), ("brope", 128), ("conv", 4 * NFT), ("rel", 32))
CON = {}
NCON = _columns(CON, ("ident", P), ("mask", CAUS), ("rcos", S), ("rsin", S),
                ("mcos", 64), ("msin", 64), ("freq", 32), ("lo", 1), ("hi", 1), ("eps", 32), ("half", 32), ("hpi", 1))


def make_constants():
    c = np.zeros((P, NCON + 4 * CAUS), np.float32)

    def put(name, value):
        o, n = CON[name]
        c[:, o:o + n] = np.asarray(value, np.float32).reshape(-1, n)

    i = np.arange(P)
    tri = i[None, :] <= i[:, None]
    put("ident", np.eye(P))
    put("mask", np.concatenate([np.where(tri, 0, NEG), np.zeros((P, P)), np.where(tri, 0, NEG)], 1))
    decay = np.zeros((P, 4, CAUS))
    for h in range(4):
        lg = np.log1p(-np.exp2(-5.0 - h))
        own = np.where(tri, np.exp(lg * np.maximum(i[:, None] - i[None, :], 0)), 0)
        across = np.exp(lg * (i[:, None] + 1.0)) * np.exp(lg * (P - 1.0 - i[None, :]))
        decay[:, h] = np.concatenate([own, across, own], 1) / 16.0
    c[:, NCON:] = decay.reshape(P, -1)
    pos = np.arange(S, dtype=np.float32)

    def angles(theta, dim):
        inv = np.float32(theta) ** (-np.arange(0, dim, 2, dtype=np.float32) / np.float32(dim))
        return (pos[:, None] * inv[None, :].astype(np.float32)).astype(np.float32).astype(np.float64)

    a = angles(10000.0, 256).reshape(T, P, P).transpose(1, 0, 2)
    put("rcos", np.cos(a).reshape(P, -1))
    put("rsin", np.sin(a).reshape(P, -1))
    a = angles(500000.0, 32).reshape(T, P, 16).transpose(1, 0, 2).reshape(P, 1, -1).repeat(2, 1)
    put("mcos", np.cos(a).reshape(P, -1))
    put("msin", np.sin(a).reshape(P, -1))
    inv = (1.0 / (np.float32(10000.0) ** (np.arange(0, 64, 2, dtype=np.float32) / np.float32(64)))).astype(np.float32)
    put("freq", inv)
    n = np.arange(1, 4096)
    large = 16 + (np.log(n.astype(np.float32) / np.float32(16)) / np.float32(np.log(8.0)) * np.float32(16)).astype(np.int32)
    bucket = np.where(n < 16, n, np.minimum(large, 31))
    low = np.array([-3.0e9] + [n[bucket >= b][0] for b in range(1, 32)], np.float32)
    high = np.append(low[1:], np.float32(3.0e9))
    put("lo", np.tile(low, 4)[:, None])
    put("hi", np.tile(high, 4)[:, None])
    put("eps", np.full(32, EPS))
    put("half", np.full(32, -0.5))
    put("hpi", np.pi / 2)
    return c


class At:

    def __init__(self, base, i=0, per=0):
        self.base, self.i, self.per = base, i, per

    def count(self, k=0):
        return self.base + k + self.i * self.per if self.per else self.base + k

    def slot(self, k):
        return (self.base + k) % RING

    def turn(self, k):
        n = (self.base + k) // RING
        return n + self.i * (self.per // RING) if self.per else n


class Chain:

    def __init__(self, wait, sem):
        self.wait, self.sem, self.total, self.k, self.i, self.per = wait, sem, 0, 0, 0, 0

    def link(self, ins):
        self.k += 1
        ins.then_inc(self.sem, 1)
        self.wait(self.sem, self.total + self.k + self.i * self.per if self.per else self.total + self.k)

    def enter(self, i, per):
        self.total, self.k, self.i, self.per = self.total + self.k, 0, i, per

    def leave(self, n):
        assert self.k == self.per, (self.k, self.per)
        self.total, self.k, self.i, self.per = self.total + n * self.per, 0, 0, 0


def build(nc, x_in, mem_in, w_stream, params, final_w, pos_pack, constants, out):
    with ExitStack() as ctx:
        def sem(name):
            return ctx.enter_context(nc.semaphore(name))

        START = 16512
        cursor = [START]

        def take(nbytes):
            at = cursor[0]
            cursor[0] += nbytes
            return at

        def sb(name, shape, dt, at):
            return nc.alloc_sbuf_tensor_at(name, shape, dt, offset=at)

        KB = 1024
        at_x, at_ht, at_pa, at_pb, at_u2 = take(16 * KB), take(32 * KB), take(36 * KB), take(16 * KB), take(16 * KB)
        at_u0, at_u1 = take(16 * KB), take(16 * KB)
        X = sb("X", [P, T, D], F32, at_x)
        HT = sb("HT", [P, KT, 2, S], F32R, at_ht)
        PA = sb("PA", [P, T, 4096], F32, at_pa)
        PAC = sb("PAC", [P, 8, T, CH], F32, at_pa)
        PB = sb("PB", [P, T, D], F32, at_pb)
        ROWS = sb("ROWS", [P, T, D], F32, at_pa)
        MEMR = sb("MEMR", [P, T, D], F32, at_pa + 16 * KB)
        MEMT = sb("MEMT", [P, KT, 2, S], F32R, at_pb)
        MQKV = sb("MQKV", [P, T, 3 * W], F32, at_pb)
        MERGED = {"merged1": sb("MERGED1", [P, T, D], F32, at_pb), "merged2": sb("MERGED2", [P, T, D], F32, at_pa + 20 * KB)}
        SGX = sb("SGX", [P, T, D], F32, at_pa)
        QB = sb("QB", [P, T, 1536], F32, at_pa)
        KVB = sb("KVB", [P, T, 2048], F32, at_u0)
        U = [sb("U0", [P, 8, 2, S], F32R, at_u0), sb("U1", [P, 8, 2, S], F32R, at_u1),
             sb("U2", [P, 8, 2, S], F32R, at_u2)]
        ACTT = sb("ACTT", [P, FT, 2, S], F32R, at_u0)
        FINALW = sb("FINALW", [P, D], F32, at_u0 + 8 * KB)
        FU = sb("FU", [P, 2, S + 2], F32, at_u1)
        FC = sb("FC", [P, 2, S], F32, at_u1 + 2112)
        FY = sb("FY", [P, 2, S], F32, at_u1 + 2112 + 2 * KB)
        FA = sb("FA", [P, FT, S], F32, at_u1 + 2112 + 4 * KB)
        FP = sb("FP", [P, FT, S], F32, at_u1 + 2112 + 8 * KB)
        DECAY = sb("DECAY", [P, 4, CAUS], F32, at_u2 + 8 * KB)
        CKV = sb("CKV", [P, T, 2 * W], F32, at_u1)
        JUNK = sb("JUNK", [P, T, D], F32, at_u1)
        BIAS = sb("BIAS", [P, REL_HEADS, CAUS], F32, at_u2)
        LATT = sb("LATT", [P, 6, 2, S], F32R, at_u2)
        SG = {"merge_moba": sb("SG_MOBA", [P, T, CH], F32, at_u2), "merge_c": sb("SG_C", [P, T, CH], F32, at_u2 + 12 * KB),
              "merge_a": sb("SG_A", [P, T, CH], F32, at_pa + 12 * KB)}
        TMP = sb("TMP", [P, T, CH], F32, at_pa + 16 * KB)
        SQQ = sb("SQQ", [P, T, 1536], F32, at_x)
        SQK = sb("SQK", [P, T, 8, P], F32, at_pa + 12 * KB)
        QK = sb("QK", [P, 2, T, 256], F32, at_x)
        QKT = sb("QKT", [P, 2, 2, S], F32, at_x + 4 * KB)
        SC = sb("SC", [P, 512], F32, at_x + 8 * KB)
        PR = sb("PR", [P, 512], F32, at_x + 10 * KB)
        PT = sb("PT", [P, 512], F32, at_x + 12 * KB)
        OF = sb("OF", [P, T, 256], F32, at_x + 14 * KB)
        POSB = sb("POSB", [P, POSN], I32, at_u2 + 4 * KB)
        ANG = sb("ANG", [P, 2, T, 32], F32, at_u1)
        ANGI = sb("ANGI", [P, T * 32], I32, at_u1 + KB)
        DI = sb("DI", [P, 8, P], I32, at_x)
        M1 = sb("M1", [P, 8, P], F32, at_x + 4 * KB)
        OH = sb("OH", [P, 8, P], F32, at_x + 8 * KB)
        BE = sb("BE", [32, 8, P], F32, at_x + 12 * KB)
        RAW = sb("RAW", [P, RING, GK, CH], F32, take(16 * KB))
        WH = sb("WH", [P, RING, GK, CH], F32R, take(16 * KB))
        WL = sb("WL", [P, RING, GK, CH], F32R, take(16 * KB))
        CONST = sb("CONST", [P, NCON], F32, take(4 * NCON // 32 * 32 + 32))
        PARAM = sb("PARAM", [P, NPAR], F32, take(4 * NPAR // 32 * 32 + 32))
        POSI = sb("POSI", [P, 2], I32, take(32))
        ROPE = sb("ROPE", [P, 2, 2, T, 32], F32, take(1024))
        JK = sb("JK", [P, 256], F32, take(1024))
        MS = sb("MS", [P, 8], F32, take(32))
        MSC = sb("MSC", [P, T, NCH], F32, take(32))
        MST = sb("MST", [P, 2, T, 8], F32, take(128))
        NM = sb("NM", [P, 2], F32, take(32))
        RS = sb("RS", [P, 2], F32, take(32))
        RI = sb("RI", [P, 2], F32, take(32))
        M8 = sb("M8", [P, T, 8], F32, take(64))
        assert cursor[0] <= nc.sbuf_usable_end
        PS = ctx.enter_context(nc.psum_tensor("PS", [P, 8, 512], F32))

        bias_scratch = nc.dram_tensor("bias_scratch", (32, 3, 32, P), F32, kind="Internal").ap()
        x_scratch = nc.dram_tensor("x_scratch", (S, D), F32, kind="Internal").ap()

        def con(name, rows=P):
            o, n = CON[name]
            return CONST[0:rows, o:o + n]

        def par(name, k=0, n=1):
            o = k + PAR[name][0]
            return PARAM[:, ds(o, n)]

        ident = con("ident")

        def rows(dram):
            return dram.rearrange("(t p) d -> p t d", p=P)

        raw_landed = [sem(f"raw_landed{s}") for s in range(RING)]
        hi_split = sem("hi_split")
        lo_split = sem("lo_split")
        group_used = sem("group_used")
        prod_free = sem("prod_free")
        ffn_free = sem("ffn_free")
        ffn_copied = sem("ffn_copied")
        ffn_conv = sem("ffn_conv")
        ffn_silu = sem("ffn_silu")
        ffn_prod = sem("ffn_prod")
        ffn_hi = sem("ffn_hi")
        ffn_lo = sem("ffn_lo")
        x_first = [sem(f"x_first{t}") for t in range(T)]
        x_loaded = sem("x_loaded")
        con_loaded = sem("con_loaded")
        decay_loaded = sem("decay_loaded")
        par_loaded = sem("par_loaded")
        pos_loaded = sem("pos_loaded")
        norm_ms = sem("norm_ms")
        norm_rstd = sem("norm_rstd")
        norm_rows = sem("norm_rows")
        x_sq = sem("x_sq")
        tr_done = sem("tr_done")
        tr_hi = sem("tr_hi")
        tr_lo = sem("tr_lo")
        qk_raw = sem("qk_raw")
        qk_ms = sem("qk_ms")
        qk_fixed = sem("qk_fixed")
        qk_tr = sem("qk_tr")
        qkt_ready = sem("qkt_ready")
        scores = sem("scores")
        maxima = sem("maxima")
        probs = sem("probs")
        pt_done = sem("pt_done")
        pt_ready = sem("pt_ready")
        pv_done = sem("pv_done")
        o_ms = sem("o_ms")
        o_rstd = sem("o_rstd")
        o_rows = sem("o_rows")
        ot_done = sem("ot_done")
        ot_hi = sem("ot_hi")
        head_out = sem("head_out")
        gate_ready = sem("gate_ready")
        merged_ready = sem("merged_ready")
        dist_ready = sem("dist_ready")
        dist_used = sem("dist_used")
        onehot = sem("onehot")
        bias_done = sem("bias_done")
        bias_copied = sem("bias_copied")
        bias_stored = sem("bias_stored")
        bias_loaded = sem("bias_loaded")
        ang_ready = sem("ang_ready")
        rope_ready = sem("rope_ready")
        mem_loaded = sem("mem_loaded")
        fw_loaded = sem("fw_loaded")
        x_done = sem("x_done")
        x_stored = sem("x_stored")
        x_back = sem("x_back")
        idx_fixed = sem("idx_fixed")
        idx_tr = sem("idx_tr")
        idx_ready = sem("idx_ready")
        idx_dots = sem("idx_dots")
        idx_relu = sem("idx_relu")
        idx_sum = sem("idx_sum")
        sel_ready = sem("sel_ready")
        a_ms = sem("a_ms")
        bq_sq = sem("bq_sq")
        bk_sq = sem("bk_sq")
        b_ms = sem("b_ms")
        lat_ms = sem("lat_ms")
        lat_rstd = sem("lat_rstd")
        lat_rows = sem("lat_rows")
        out_ready = sem("out_ready")
        out_stored = sem("out_stored")
        dve_chain = sem("dve_chain")
        pool_chain = sem("pool_chain")
        act_chain = sem("act_chain")
        pool_held = sem("pool_held")

        block = ctx.enter_context(nc.Block())

        MOBA = dict(h0=MOBA0, sm0=0, d=[128], causal=True, dv=128, scale=128 ** -0.5, u=1)
        RET = dict(h0=RET0, sm0=None, d=[128, 128], causal=True, dv=256, scale=None, u=0)
        CMEM = dict(h0=C0, sm0=8, d=[128, 128], causal=False, dv=256, scale=256 ** -0.5, u=0)
        ASP = dict(h0=A0, sm0=12, d=[128], causal=True, dv=128, scale=128 ** -0.5, u=1)
        BLA = dict(h0=B0, sm0=20, d=[128, 64], causal=True, dv=128, scale=192 ** -0.5, u=2)
        NORM0 = C0

        TR = {"h1": 0, "merged1": 16, "mem": 32, "h2": 48, "h3": 64, "lat": 80, "merged2": 86}
        BIAS_AT = (1, 3, 6, 9, 11, 14)

        def pairs_ahead(q):
            return [k for k in range(2 * q + 2 if q else 0, 2 * q + 4) if k < KT]

        def merged_tiles(p):
            c, r = p // GW - 1, p % GW
            return [4 * c + 2 * (r - 1), 4 * c + 2 * (r - 1) + 1] if r in (1, 2) and c >= 0 else []

        @block.sync
        def _(sp):
            for t in range(T):
                sp.dma_start(X[:, t], rows(x_in)[:, t]).then_inc(x_first[t], 16)
            stream = w_stream.rearrange("g p (k n) -> g p k n", k=GK)

            def load(g, g_index, slot):
                sp.dma_start(RAW[:, slot], stream[g_index].rearrange("g p k n -> (g p) k n")).then_inc(raw_landed[slot], 16)

            for g in range(RING):
                load(g, ds(g, 1), g)
            with sp.Fori(1, GROUPS // RING) as r:
                for s in range(RING):
                    sp.wait_ge(lo_split, r * RING + (s + 1 - RING))
                    load(None, ds(r * RING + s, 1), s)
            for g in range(GROUPS // RING * RING, GROUPS):
                sp.wait_ge(lo_split, g + 1 - RING)
                load(g, ds(g, 1), g % RING)

        @block.gpsimd
        def _(pool):
            def hold(sem, value):
                pool.wait_ge(sem, value)
                pool.sem_inc(pool_held, 1)

            ch = Chain(hold, pool_chain)
            link = ch.link

            def rstd(n, ready, done_sem, value):
                hold(ready, value)
                link(pool.tensor_tensor(MS[:, 0:n], MS[:, 0:n], con("eps")[:, 0:n], ALU.add))
                ins = pool.tensor_tensor(MS[:, 0:n], MS[:, 0:n], con("half")[:, 0:n], ALU.pow)
                if done_sem is None:
                    link(ins)
                else:
                    ins.then_inc(done_sem, 1)

            def rotate(x1, x2, cos, sin, t1, t2, last_sem):
                link(pool.tensor_tensor(t1, x2, sin, ALU.mult))
                link(pool.tensor_tensor(t2, x1, sin, ALU.mult))
                link(pool.tensor_tensor(x1, x1, cos, ALU.mult))
                link(pool.tensor_tensor(x2, x2, cos, ALU.mult))
                link(pool.tensor_tensor(x1, x1, t1, ALU.subtract))
                pool.tensor_tensor(x2, x2, t2, ALU.add).then_inc(last_sem, 1)

            hold(con_loaded, 16)
            rstd(2, norm_ms, norm_rstd, 1)

            hold(prod_free, 2 + 6)
            with pool.Fori(0, 8) as h:
                ch.enter(h, 7)
                H = At(MOBA0, h, 1)
                hold(qk_tr, H.count(1))
                link(pool.tensor_copy(QK[:, 0, :, 0:P], MQKV[:, :, ds(h * P, P)]))
                link(pool.tensor_copy(QK[:, 1, :, 0:P], MQKV[:, :, ds(h * P + W, P)]))
                v = JK[:, 0:128].rearrange("p (z a t d) -> p z a t d", z=2, a=2, t=T)
                tab = [con(n).rearrange("p (a t d) -> p a t d", a=2, t=T) for n in ("mcos", "msin")]
                rotate(QK[:, :, :, 0:16], QK[:, :, :, 16:32], tab[0], tab[1], v[:, 0], v[:, 1], qk_fixed)
            ch.leave(8)

            hold(prod_free, 2 + 6 + 8)
            cos = con("rcos").rearrange("p (t d) -> p t d", t=T)
            sin = con("rsin").rearrange("p (t d) -> p t d", t=T)
            tmp = JK[:, 0:256].rearrange("p (t d) -> p t d", t=T)
            with pool.Fori(0, 4) as h:
                ch.enter(h, 2 * 5 + 1 + 1)
                H = At(RET0, h, 1)
                hold(qk_tr, H.count(1))
                for a in range(2):
                    x1 = PA[:, :, ds(h * 256 + a * W, P)]
                    x2 = PA[:, :, ds(h * 256 + (a * W + P), P)]
                    y1, y2 = QK[:, a, :, 0:P], QK[:, a, :, P:256]
                    link(pool.tensor_tensor(y1, x1, cos, ALU.mult))
                    link(pool.tensor_tensor(tmp, x2, sin, ALU.mult))
                    link(pool.tensor_tensor(y1, y1, tmp, ALU.subtract))
                    link(pool.tensor_tensor(y2, x2, cos, ALU.mult))
                    link(pool.tensor_tensor(tmp, x1, sin, ALU.mult))
                    ins = pool.tensor_tensor(y2, y2, tmp, ALU.add)
                    if a:
                        ins.then_inc(qk_fixed, 1)
                    else:
                        link(ins)
                hold(o_ms, At(0, h, 1).count(1))
                link(pool.tensor_tensor(MS[:, 0:2], MS[:, 0:2], con("eps")[:, 0:2], ALU.add))
                pool.tensor_tensor(MS[:, 0:2], MS[:, 0:2], con("half")[:, 0:2], ALU.pow).then_inc(o_rstd, 1)
            ch.leave(4)

            hold(head_out, RET0 + 4 + 1)
            hold(pos_loaded, 32)
            with pool.Fori(0, NCH) as i:
                for seg in range(3):
                    hold(dist_used, At(seg + 1, i, 3).count())
                    q = POSB[:, ds(i * 8 + (32 if seg else 0), 8)].unsqueeze(2).broadcast_to([P, 8, P])
                    k = POSB[:, 64 + (P if seg == 2 else 0):64 + (P if seg == 2 else 0) + P].unsqueeze(1).broadcast_to([P, 8, P])
                    pool.tensor_tensor(DI[:], q, k, ALU.subtract).then_inc(dist_ready, 1)

            rstd(2, norm_ms, norm_rstd, 2)
            rstd(2, norm_ms, norm_rstd, 3)
            rstd(2, norm_ms, norm_rstd, 4)
            rstd(2, norm_ms, norm_rstd, 5)

            hold(x_stored, 16)
            hold(prod_free, 2 + PROD0["a_proj"])
            with pool.Fori(0, 4) as h:
                ch.enter(h, 3)
                hold(qk_tr, At(C0, h, 1).count(1))
                link(pool.tensor_copy(QK[:, 0], PB[:, :, ds(h * 256, 256)]))
                pool.tensor_copy(QK[:, 1], CKV[:, :, ds(h * 256, 256)]).then_inc(qk_raw, 1)
                rstd(4, qk_ms, None, At(0, h, 1).count(1))
                f = QK[:].rearrange("p a t d -> p (a t) d")
                pool.tensor_tensor(f, f, MS[:, 0:4].unsqueeze(2).broadcast_to([P, 4, 256]), ALU.mult).then_inc(qk_fixed, 1)
            ch.leave(4)

            hold(prod_free, 2 + PROD0["b_proj"])
            hold(head_out, C0 + 4 + 1)
            link(pool.tensor_copy(QK[:, 1, :, 0:64], PAC[:, 7, :, 0:64]))
            pool.tensor_copy(QK[:, 1, :, 64:P], PAC[:, 7, :, 0:64]).then_inc(idx_fixed, 1)
            with pool.Fori(0, 2) as i:
                for p in range(4):
                    hold(idx_tr, At(2 + p, i, 4).count())
                    src = PAC[:, ds(i + 5, 1), :, p * P:(p + 1) * P].rearrange("p a t d -> p (a t) d")
                    pool.tensor_copy(QK[:, 0, :, 0:P], src).then_inc(idx_fixed, 1)

            def inverse_roots(ms):
                eps, half = [con(n)[:, 0:ms.shape[1] * ms.shape[2]].rearrange("p (t h) -> p t h", t=ms.shape[1])
                             for n in ("eps", "half")]
                link(pool.tensor_tensor(ms, ms, eps, ALU.add))
                link(pool.tensor_tensor(ms, ms, half, ALU.pow))

            hold(lat_ms, 1)
            link(pool.tensor_tensor(MS[:, 0:4], MS[:, 0:4], con("eps")[:, 0:4], ALU.add))
            pool.tensor_tensor(MS[:, 0:4], MS[:, 0:4], con("half")[:, 0:4], ALU.pow).then_inc(lat_rstd, 1)

            hold(a_ms, 1)
            inverse_roots(MST[:, 0])
            inverse_roots(MST[:, 1, :, 0:2])
            hold(sel_ready, 1)
            with pool.Fori(0, 2) as kv:
                for r in range(4):
                    hold(qk_tr, At(A0 + r, kv, 4).count(1))
                    q = PAC[:, ds(kv, 1), :, r * P:(r + 1) * P].rearrange("p a t d -> p (a t) d")
                    pool.tensor_tensor(QK[:, 0, :, 0:P], q, MST[:, 0, :, ds(kv * 4 + r, 1)].broadcast_to([P, T, P]), ALU.mult)
                    pool.tensor_tensor(QK[:, 1, :, 0:P], PAC[:, 2, :, ds(kv * P, P)],
                                       MST[:, 1, :, ds(kv, 1)].broadcast_to([P, T, P]), ALU.mult).then_inc(qk_fixed, 1)

            hold(b_ms, 1)
            hold(rope_ready, 1)
            link(pool.tensor_tensor(MST[:, 1], MST[:, 1], MS[:, 4:6].unsqueeze(2).broadcast_to([P, T, 8]), ALU.add))
            inverse_roots(MST[:, 0])
            inverse_roots(MST[:, 1])
            with pool.Fori(0, 8) as h:
                ch.enter(h, 1 + 1 + 5)
                hold(qk_tr, At(B0, h, 1).count(1))
                q_rms, k_rms = MST[:, 0, :, ds(h, 1)], MST[:, 1, :, ds(h, 1)]
                pool.tensor_tensor(QK[:, 0, :, 0:192], QB[:, :, ds(h * 192, 192)], q_rms.broadcast_to([P, T, 192]), ALU.mult)
                pool.tensor_tensor(QK[:, 1, :, 0:P], KVB[:, :, ds(h * 256, P)], k_rms.broadcast_to([P, T, P]), ALU.mult)
                link(pool.tensor_tensor(QK[:, 1, :, P:192], PB[:, :, 768:832], k_rms.broadcast_to([P, T, 64]), ALU.mult))
                f = QK[:, :, :, P:192]
                gains = par("brope", 0, 128).rearrange("p (a d) -> p a d", a=2).unsqueeze(2).broadcast_to([P, 2, T, 64])
                link(pool.tensor_tensor(f, f, gains, ALU.mult))
                t = JK[:, 0:256].rearrange("p (z a t d) -> p z a t d", z=2, a=2, t=T)
                rotate(QK[:, :, :, P:P + 32], QK[:, :, :, P + 32:P + 64], ROPE[:, 0], ROPE[:, 1], t[:, 0], t[:, 1], qk_fixed)
            ch.leave(8)

        @block.tensor
        def _(pe):
            def group(g, j, body):
                pe.wait_ge(lo_split, g.count(j + 1))
                body(g.slot(j)).then_inc(group_used, 1)

            def rows_product(g, n, j, q, nq, left):
                pair = 2 * (n % 2)

                def body(slot):
                    for kk in range(GK):
                        k = q * GK + kk
                        for t in range(T):
                            hi, lo = left[:, k, 0, t * P:(t + 1) * P], left[:, k, 1, t * P:(t + 1) * P]
                            o = PS[:, pair + t, :]
                            pe.matmul(o, hi, WH[:, slot, kk, :], start=k == 0, stop=False)
                            pe.matmul(o, hi, WL[:, slot, kk, :], start=False, stop=False)
                            ins = pe.matmul(o, lo, WH[:, slot, kk, :], start=False, stop=k == nq * GK - 1)
                    return ins
                group(g, j, body)

            def product(g, n, j, nq, left, steps=None, before=None):
                pe.wait_ge(prod_free, n.count(1))
                for q in range(nq):
                    if before:
                        before(j + q)
                    rows_product(g, n.base, j + q, q, nq, left)
                    if steps:
                        steps(j + q)

            def products(name, parts, i, steps=None, before=None):
                per = sum(nq for nq, _ in parts)
                j = 0
                for m, (nq, left) in enumerate(parts):
                    g, n = At(GROUP0[name], i, per), At(PROD0[name] + m, i, len(parts))
                    product(g, n, j, nq, left, (lambda p: steps(i, p)) if steps else None, before)
                    j += nq

            def product_loop(name, iters, parts, steps=None, first=0):
                with pe.Fori(first, iters) as i:
                    products(name, parts, i, steps)

            def straight(name, count, nq, left, steps=None, before=None):
                for m in range(count):
                    product(At(GROUP0[name]), At(PROD0[name] + m), m * nq, nq, left, steps, before)

            def transposes(name, src, ks):
                for k in ks:
                    at = TR[name] + k
                    if at >= 4:
                        pe.wait_ge(tr_lo, at - 3)
                    for t in range(T):
                        ins = pe.transpose(PS[:, 4 + at % 4, t * P:(t + 1) * P], src[:, t, k * P:(k + 1) * P], ident)
                    ins.then_inc(tr_done, 1)

            def as_it_arrives(name, src, rows_before):
                def before(q):
                    if q in (0, 3):
                        pe.wait_ge(norm_rows, rows_before + (2 if q else 1))
                    transposes(name, src, pairs_ahead(q))
                    pe.wait_ge(tr_lo, TR[name] + 2 * q + 2)
                return before

            def head_transpose(br, H):
                pe.wait_ge(qk_fixed, H.count(1))
                pe.wait_ge(head_out, H.count(1))
                for a in range(2):
                    for c, n in enumerate(br["d"]):
                        for t in range(T):
                            ins = pe.transpose(PS[0:n, 4 + a, c * S + t * P:c * S + (t + 1) * P],
                                               QK[:, a, t, c * P:c * P + n], ident)
                ins.then_inc(qk_tr, 1)

            def head_scores(br, H):
                pe.wait_ge(qkt_ready, H.count(1))
                last = len(br["d"]) - 1
                col = 0
                for t in range(T):
                    keys = (t + 1) * P if br["causal"] else S
                    for c, n in enumerate(br["d"]):
                        ins = pe.matmul(PS[:, 6, col:col + keys], QKT[0:n, 0, c, t * P:(t + 1) * P],
                                        QKT[0:n, 1, c, 0:keys], start=c == 0, stop=c == last)
                    col += keys
                ins.then_inc(scores, 1)

            def head_probs(br, H):
                pe.wait_ge(probs, H.count(1))
                src = SC if br is RET else PR
                for b in range(3 if br["causal"] else 4):
                    ins = pe.transpose(PS[:, 7, b * P:(b + 1) * P], src[:, b * P:(b + 1) * P], ident)
                ins.then_inc(pt_done, 1)

            def head_values(br, H, v):
                pe.wait_ge(pt_ready, H.count(1))
                dv = br["dv"]
                blocks = ([[0], [1, 2]] if br["causal"] else [[0, 1], [2, 3]])
                for t in range(T):
                    for s, b in enumerate(blocks[t]):
                        ins = pe.matmul(PS[:, 4, t * dv:(t + 1) * dv], PT[:, b * P:(b + 1) * P], v(s),
                                        start=s == 0, stop=s == len(blocks[t]) - 1)
                ins.then_inc(pv_done, 1)

            def head_output(br, H):
                pe.wait_ge(o_rows, H.count(1))
                for c in range(br["dv"] // P):
                    for t in range(T):
                        ins = pe.transpose(PS[:, 5, c * S + t * P:c * S + (t + 1) * P], OF[:, t, c * P:(c + 1) * P], ident)
                ins.then_inc(ot_done, 1)

            def head_steps(br, H, v, at=(0, 1, 3, 4, 6)):
                return dict(zip(at, (lambda: head_transpose(br, H), lambda: head_scores(br, H), lambda: head_probs(br, H),
                                     lambda: head_values(br, H, v), lambda: head_output(br, H))))

            pe.wait_ge(con_loaded, 16)
            pe.sem_inc(qk_tr, 1)
            pe.sem_inc(idx_tr, 1)
            pe.sem_inc(bias_done, 1)
            arriving = as_it_arrives("h1", ROWS, 0)
            products("moba_proj", [(GD, HT)] * 2, 0, None, lambda p: arriving(p) if p < GD else None)
            product_loop("moba_proj", 3, [(GD, HT)] * 2, first=1)

            def moba_step(i, p):
                for r in range(2):
                    h = i * 2 + r
                    st = head_steps(MOBA, At(MOBA0 + r, i, 2), lambda s: MQKV[:, s, ds(h * P + 2 * W, P)])
                    if p - 8 * r in st:
                        st[p - 8 * r]()
            product_loop("ret_proj", 4, [(GD, HT)] * 2, moba_step)

            def ret_step(i, p):
                st = head_steps(RET, At(RET0, i, 1), lambda s: PA[:, s, ds(i * 256 + 2 * W, 256)], (0, 2, 4, 6, 9))
                if p in st:
                    st[p]()
            product_loop("merge_moba", NCH, [(GD, HT), (GW, U[1])], ret_step)

            def bias_step(i, p):
                if p not in BIAS_AT:
                    return
                k = At(BIAS_AT.index(p), i, len(BIAS_AT))
                pe.wait_ge(onehot, k.count(1))
                pe.wait_ge(bias_copied, k.count(1))
                for b in range(2):
                    ins = pe.matmul(PS[0:32, 4 + b, :], par("rel", 0, 32),
                                    OH[:, 4 * b:4 * b + 4, :].rearrange("p q s -> p (q s)"), start=True, stop=True)
                ins.then_inc(bias_done, 1)
            pe.wait_ge(head_out, RET0 + 4 + 1)
            product_loop("gates_ret", 2, [(GD, HT)] * 2, bias_step)
            pe.wait_ge(bias_copied, NBIAS + 1)

            def up_steps(name, chunks_before):
                def steps(p):
                    if merged_tiles(p):
                        pe.wait_ge(merged_ready, chunks_before + p // GW)
                        transposes(name, MERGED[name], merged_tiles(p))
                return steps

            def out_steps(name, chunks_before):
                def steps(p):
                    if p in (1, 2):
                        pe.wait_ge(merged_ready, chunks_before + NCH)
                        transposes(name, MERGED[name], merged_tiles(NCH * GW + p))

                def before(p):
                    if p in (0, 6):
                        pe.wait_ge(tr_lo, TR[name] + (12 if p == 0 else KT))
                return steps, before
            straight("up_ret", NCH, GW, U[0], up_steps("merged1", 0))
            steps, before = out_steps("merged1", 0)

            def out1_steps(p):
                steps(p)
                if 4 <= p < 4 + KT:
                    pe.wait_ge(norm_rows, 3)
                    transposes("mem", MEMR, [p - 4])
            straight("out1", NCH, GD, HT, out1_steps, before)

            def ffn_up(g, u, j, before=None):
                half = 4 * (u.base % 2)
                pe.wait_ge(ffn_free, u.count(1))
                for q in range(GD):
                    if before:
                        before(q)

                    def body(slot):
                        for kk in range(GK):
                            k = q * GK + kk
                            for f in range(FT):
                                pe.matmul(PS[:, half + f, :], WH[:, slot, kk, f * P:(f + 1) * P], HT[:, k, :, :],
                                          start=k == 0, stop=False, skip_group_check=True)
                                ins = pe.matmul(PS[:, half + f, 0:S], WL[:, slot, kk, f * P:(f + 1) * P], HT[:, k, 0, :],
                                                start=False, stop=k == KT - 1, skip_group_check=True)
                        return ins
                    group(g, j + q, body)

            def ffn_down(g, u, j, blk):
                for c in range(NCH):
                    v = At(u.base + c // 2, u.i, u.per)
                    if c % 2 == 0:
                        pe.wait_ge(ffn_free, v.count(1))
                    if c == 0:
                        pe.wait_ge(ffn_lo, blk.count(1))
                    for q in range(2):
                        def body(slot):
                            for kk in range(GK):
                                k = q * GK + kk
                                for t in range(T):
                                    hi, lo = ACTT[:, k, 0, t * P:(t + 1) * P], ACTT[:, k, 1, t * P:(t + 1) * P]
                                    o = PS[:, 4 * (v.base % 2) + 2 * (c % 2) + t, :]
                                    pe.matmul(o, hi, WH[:, slot, kk, :], start=k == 0, stop=False)
                                    pe.matmul(o, hi, WL[:, slot, kk, :], start=False, stop=False)
                                    ins = pe.matmul(o, lo, WH[:, slot, kk, :], start=False, stop=k == FT - 1)
                            return ins
                        group(g, j + 2 * c + q, body)

            g0 = GROUP0["ffn"]
            ffn_up(At(g0), At(0), 0, as_it_arrives("h2", ROWS, 3))
            ffn_up(At(g0), At(1), GD)
            with pe.Fori(0, FB - 1) as b:
                g = At(g0 + 2 * GD, b, 3 * GD)
                ffn_up(g, At(2, b, 4), 0)
                ffn_up(g, At(3, b, 4), GD)
                ffn_down(g, At(4, b, 4), 2 * GD, At(0, b, 1))
            ffn_down(At(g0 + (3 * FB - 1) * GD), At(4 * FB - 2), 0, At(FB - 1))
            pe.wait_ge(ffn_free, 2 + 4 * FB - 1)

            def h3_steps(p):
                if 12 <= p < 12 + KT:
                    pe.wait_ge(norm_rows, 7)
                    transposes("h3", ROWS, [p - 12])
            straight("mem", NCH, GD, MEMT, h3_steps)
            pe.wait_ge(tr_lo, TR["h3"] + KT)
            product_loop("c_proj", 2, [(GD, HT)] * 2)

            def c_step(i, p):
                st = head_steps(CMEM, At(C0, i, 1), lambda s: CKV[:, s, ds(i * 256 + W, 256)])
                if p % 2 == 0 and p // 2 - 1 in st:
                    st[p // 2 - 1]()
            product_loop("a_proj", 4, [(GD, HT)] * 2, c_step)

            pe.wait_ge(idx_fixed, 1)
            for t in range(T):
                ins = pe.transpose(PS[:, 5, t * P:(t + 1) * P], QK[:, 1, t, 0:P], ident)
            ins.then_inc(idx_tr, 1)

            def index_step(i, p):
                r = p // 4
                k = At(r, i, 4)
                if p % 4 == 0:
                    pe.wait_ge(idx_fixed, k.count(2))
                    for t in range(T):
                        ins = pe.transpose(PS[:, 4, t * P:(t + 1) * P], QK[:, 0, t, 0:P], ident)
                    ins.then_inc(idx_tr, 1)
                elif p % 4 == 1:
                    pe.wait_ge(idx_ready, k.count(2))
                    pe.wait_ge(idx_relu, k.count(1))
                    for j in range(2):
                        q = slice(64 * j, 64 * j + 64)
                        pe.matmul(PS[:, 6 + j, 0:P], QKT[q, 0, 0, 0:P], QKT[q, 1, 0, 0:P], start=True, stop=True)
                        ins = pe.matmul(PS[:, 6 + j, P:CAUS], QKT[q, 0, 0, P:S], QKT[q, 1, 0, :], start=True, stop=True)
                    ins.then_inc(idx_dots, 1)
            product_loop("b_proj", 2, [(GD, HT)] * 2, index_step)

            def a_step(i, p):
                r = p // 6
                st = head_steps(ASP, At(A0 + r, i, 4), lambda s: PAC[:, 2, s, ds(i * P + 256, P)], (0, 1, 3, 4, 5))
                if p - 6 * r in st:
                    st[p - 6 * r]()
            product_loop("merge_c", 2, [(GD, HT), (GW, U[0])] * 2, a_step)
            pe.wait_ge(lat_rows, 1)
            pe.wait_ge(head_out, A0 + 8 + 1)
            transposes("lat", PB, range(6))
            pe.wait_ge(tr_lo, TR["lat"] + 6)
            g0, n0 = GROUP0["b_up"], PROD0["b_up"]
            for c in range(3):
                product(At(g0), At(n0 + c), 2 * c, 2, LATT)
            for c in range(4):
                product(At(g0), At(n0 + 3 + c), 6 + c, 1, LATT[:, 4:6])

            def b_step(i, p):
                r = p // 6
                h = i * 2 + r
                st = head_steps(BLA, At(B0 + r, i, 2), lambda s: KVB[:, s, ds(h * 256 + P, P)], (0, 1, 3, 4, 5))
                if p - 6 * r in st:
                    st[p - 6 * r]()
            product_loop("merge_a", NCH, [(GD, HT), (GW, U[1])], b_step)
            product_loop("gates_b", 2, [(GD, HT)] * 2)
            pe.wait_ge(head_out, HEADS + 1)
            straight("up_b", NCH, GW, U[2], up_steps("merged2", NCH))
            steps, before = out_steps("merged2", NCH)
            straight("out2", NCH, GD, HT, steps, before)

        @block.scalar
        def _(act):
            ch = Chain(act.wait_ge, act_chain)
            link = ch.link

            def split(g, j):
                act.wait_ge(raw_landed[g.slot(j)], g.turn(j) * 16 + 16)
                if g.per or g.base + j >= RING:
                    act.wait_ge(group_used, g.count(j + 1 - RING))
                act.activation(WH[:, g.slot(j)], RAW[:, g.slot(j)], ACT.Copy).then_inc(hi_split, 1)

            def evacuate(n, end, dst):
                act.wait_ge(group_used, end)
                pair = 2 * (n.base % 2)
                act.activation(dst, PS[:, pair:pair + 2, :], ACT.Copy).then_inc(prod_free, 1)

            def evacuations(name, g, i, p, per_iter, dst, func=ACT.Copy):
                if p % GD == GD - 1:
                    c = p // GD
                    n = At(PROD0[name] + c, i, per_iter)
                    act.wait_ge(group_used, g.count(p + 1))
                    pair = 2 * (n.base % 2)
                    act.activation(dst(i * (per_iter * CH) + c * CH if n.per else c * CH), PS[:, pair:pair + 2, :],
                                   func).then_inc(prod_free, 1)

            def project(name, iters, dst, steps=None, links=0, first=0, func=ACT.Copy):
                with act.Fori(first, iters) as i:
                    ch.enter(i, links)
                    g = At(GROUP0[name], i, 2 * GD)
                    for p in range(2 * GD):
                        split(g, p + RING)
                        evacuations(name, g, i, p, 2, dst, func)
                        if steps:
                            steps(i, p)
                ch.leave(iters - first)

            def mean_squares(pairs, scale, done, junk=None):
                for n, (src, acc) in enumerate(pairs):
                    o = junk if junk is not None else PS[:, 4:8, :].rearrange("p b n -> p (b n)")
                    ins = act.activation(o, src, ACT.Square, scale=scale, accum_out=acc)
                    if n + 1 < len(pairs):
                        link(ins)
                ins.then_inc(done, 1)

            def transposed(name, dst, ks, gain):
                for k in ks:
                    at = TR[name] + k
                    act.wait_ge(tr_done, at + 1)
                    act.activation(dst[:, k, 0, :], PS[:, 4 + at % 4, 0:S], ACT.Copy,
                                   scale=par(gain, k) if gain else 1.0).then_inc(tr_hi, 1)

            def head_transpose(br, H, gains):
                act.wait_ge(qk_tr, H.count(2))
                for a in range(2):
                    whole = len(set(br["d"])) == 1 and not gains
                    for c, n in enumerate([P] if whole else br["d"]):
                        w = S * len(br["d"]) if whole else S
                        dst = QKT[:, a].rearrange("p c s -> p (c s)")[0:n, c * S:c * S + w]
                        ins = act.activation(dst, PS[0:n, 4 + a, c * S:c * S + w], ACT.Copy,
                                             scale=par(gains[a], c) if gains and c < PAR[gains[a]][1] else 1.0)
                ins.then_inc(qkt_ready, 1)

            def head_exp(br, H, M):
                act.wait_ge(maxima, M.count(1))
                cut = P if br["causal"] else S
                end = CAUS if br["causal"] else 2 * S
                act.activation(PR[:, 0:cut], SC[:, 0:cut], ACT.Exp, bias=NM[:, 0:1], accum_out=RS[:, 0:1])
                act.activation(PR[:, cut:end], SC[:, cut:end], ACT.Exp, bias=NM[:, 1:2], accum_out=RS[:, 1:2]).then_inc(probs, 1)

            def head_probs(br, H):
                act.wait_ge(pt_done, H.count(1))
                n = CAUS if br["causal"] else 512
                act.activation(PT[:, 0:n], PS[:, 7, 0:n], ACT.Copy).then_inc(pt_ready, 1)

            def head_output(br, H, h):
                act.wait_ge(ot_done, H.count(1))
                nd = br["dv"] // P
                for c in range(nd):
                    dst = U[br["u"]][:, ds(h * nd + c, 1), 0, :]
                    ins = act.activation(dst, PS[:, 5:6, c * S:(c + 1) * S], ACT.Copy,
                                         scale=par("ret", h * nd + c) if br is RET else 1.0)
                ins.then_inc(ot_hi, 1)

            def head_squares(br, N):
                act.wait_ge(qk_raw, N.count(1))
                d = sum(br["d"])
                mean_squares([(QK[:, a, t, 0:d], MS[:, 2 * a + t:2 * a + t + 1]) for a in range(2) for t in range(T)],
                             float(d) ** -0.5, qk_ms, JK[:, 0:d])

            def head_steps(br, H, M, h, gains=None, at=(0, 1, 3, 6)):
                return dict(zip(at, (lambda: head_transpose(br, H, gains), lambda: head_exp(br, H, M),
                                     lambda: head_probs(br, H), lambda: head_output(br, H, h))))

            act.dma_start(CONST[:], constants[:, 0:NCON]).then_inc(con_loaded, 16)
            act.dma_start(DECAY[:].rearrange("p h n -> p (h n)"), constants[:, NCON:]).then_inc(decay_loaded, 16)
            act.dma_start(PARAM[:], params).then_inc(par_loaded, 16)
            act.dma_start(POSI[:], pos_pack[:, POSN:POSN + 2]).then_inc(pos_loaded, 16)
            act.sem_inc(prod_free, 2)
            act.sem_inc(bias_copied, 1)
            act.sem_inc(idx_relu, 1)

            act.wait_ge(ang_ready, 1)
            act.wait_ge(con_loaded, 16)
            for a in range(2):
                act.activation(ROPE[:, 1, a], ANG[:, 0], ACT.Sin)
                ins = act.activation(ROPE[:, 0, a], ANG[:, 1], ACT.Sin, scale=-1.0, bias=con("hpi"))
            ins.then_inc(rope_ready, 1)

            for t in range(T):
                act.wait_ge(x_first[t], 16)
                ins = act.activation(PS[:, 4 * t:4 * t + 4, :].rearrange("p b n -> p (b n)"), X[:, t, :], ACT.Square,
                                     scale=D ** -0.5, accum_out=MS[:, t:t + 1])
            ins.then_inc(norm_ms, 1)
            act.wait_ge(par_loaded, 16)
            for j in range(RING):
                split(At(0), j)
            g = At(GROUP0["moba_proj"])
            for p in range(2 * GD):
                if p < GD:
                    transposed("h1", HT, pairs_ahead(p), "attn")
                split(g, p + RING)
                evacuations("moba_proj", g, 0, p, 2, lambda c: MQKV[:, :, ds(c, CH)])
            project("moba_proj", 3, lambda c: MQKV[:, :, ds(c, CH)], first=1)

            def moba_step(i, p):
                for r in range(2):
                    st = head_steps(MOBA, At(MOBA0 + r, i, 2), At(r, i, 2), i * 2 + r)
                    if p - 8 * r in st:
                        st[p - 8 * r]()
            project("ret_proj", 4, lambda c: PA[:, :, ds(c, CH)], moba_step)

            act.wait_ge(prod_free, 2 + PROD0["merge_moba"])
            act.activation(PA[:, :, 3 * W:4 * W], PA[:, :, 3 * W:4 * W], ACT.Silu).then_inc(gate_ready, 1)

            def merge(name, iters, chunks, links=0, steps=None):
                per = chunks * (GD + GW)
                with act.Fori(0, iters) as i:
                    ch.enter(i, links)
                    g = At(GROUP0[name], i, per)
                    for p in range(per):
                        split(g, p + RING)
                        b, r = p // (GD + GW), p % (GD + GW)
                        if r == GD - 1:
                            n = At(PROD0[name] + 2 * b, i, 2 * chunks)
                            act.wait_ge(group_used, g.count(p + 1))
                            act.wait_ge(prod_free, n.count(2))
                            pair = 2 * (n.base % 2)
                            act.activation(SG[name][:], PS[:, pair:pair + 2, :], ACT.Sigmoid).then_inc(prod_free, 1)
                        if steps:
                            steps(i, p)
                ch.leave(iters)

            def ret_step(i, p):
                H = At(RET0, i, 1)
                if p == 0:
                    head_transpose(RET, H, None)
                elif p == 4:
                    head_probs(RET, H)
                elif p == 6:
                    act.wait_ge(pv_done, H.count(1))
                    mean_squares([(PS[:, 4, t * 256:(t + 1) * 256], MS[:, t:t + 1]) for t in range(T)], 1 / 16.0, o_ms, JK[:])
                elif p == 9:
                    head_output(RET, H, i)
            merge("merge_moba", NCH, 1, 1, ret_step)

            def bias_step(i, p):
                if p not in BIAS_AT:
                    return
                s = BIAS_AT.index(p)
                k = At(s, i, len(BIAS_AT))
                act.wait_ge(bias_done, k.count(2))
                if s:
                    act.wait_ge(bias_stored, k.count() * 16)
                act.activation(BE[:].rearrange("p (b q) s -> p b (q s)", b=2), PS[0:32, 4:6, :], ACT.Copy).then_inc(bias_copied, 1)
                act.wait_ge(bias_copied, k.count(2))
                act.dma_start(bias_scratch[:, s % 3, ds(i * 16 + s // 3 * 8, 8), :], BE[:]).then_inc(bias_stored, 16)
                if s == len(BIAS_AT) - 1:
                    act.wait_ge(bias_stored, k.count(1) * 16)

            act.wait_ge(head_out, RET0 + 4 + 1)
            act.dma_start(POSB[:], pos_pack[:, 0:POSN]).then_inc(pos_loaded, 16)
            act.dma_start(MEMR[:], rows(mem_in)).then_inc(mem_loaded, 16)
            project("gates_ret", 2, lambda c: SGX[:, :, ds(c, CH)], bias_step, func=ACT.Sigmoid)

            act.dma_start(X[:], rows(x_in)).then_inc(x_loaded, 16)
            for p in range(NCH * GW):
                split(At(GROUP0["up_ret"]), p + RING)
                transposed("merged1", HT, merged_tiles(p), None)
                if p == 3:
                    act.wait_ge(mem_loaded, 16)
                    for t in range(T):
                        ins = act.activation(JUNK[:, t, :], MEMR[:, t, :], ACT.Square, scale=D ** -0.5, accum_out=MS[:, t:t + 1])
                    ins.then_inc(norm_ms, 1)

            def chunk_squares(c):
                act.wait_ge(prod_free, 2 + PROD0["out1"] + c + 1)
                if c == 0:
                    act.wait_ge(norm_ms, 2)
                for t in range(T):
                    ins = act.activation(JUNK[:, t, c * CH:(c + 1) * CH], X[:, t, c * CH:(c + 1) * CH], ACT.Square,
                                         scale=D ** -0.5, accum_out=MSC[:, t, c:c + 1])
                return ins
            for p in range(NCH * GD):
                split(At(GROUP0["out1"]), p + RING)
                if p in (1, 2):
                    transposed("merged1", HT, merged_tiles(NCH * GW + p), None)
                if p == 3:
                    act.dma_start(FINALW[:], final_w.partition_broadcast(P)).then_inc(fw_loaded, 16)
                if 4 <= p < 4 + KT:
                    transposed("mem", MEMT, [p - 4], "mem")
                if p % GD == 1 and p > GD:
                    chunk_squares(p // GD - 1)
            chunk_squares(NCH - 1).then_inc(x_sq, 1)

            def up_copy(u, end, f, tile):
                act.wait_ge(group_used, end)
                if tile.per or tile.base >= 2:
                    act.wait_ge(ffn_conv, tile.count(-1))
                act.activation(FC[:, f % 2, :], PS[:, 4 * (u.base % 2) + f, 0:S], ACT.Copy).then_inc(ffn_copied, 1)

            def silu(tile, f, blk):
                act.wait_ge(ffn_conv, tile.count(1))
                act.activation(FA[:, f, :], FY[:, f % 2, :], ACT.Silu).then_inc(ffn_silu, 1)

            def block_hi(blk, end):
                act.wait_ge(ffn_prod, blk.count(1))
                if end is not None:
                    act.wait_ge(group_used, end)
                act.activation(ACTT[:, :, 0, :], FP[:], ACT.Copy).then_inc(ffn_hi, 1)

            g0 = GROUP0["ffn"]
            for p in range(2 * GD):
                if p < GD:
                    transposed("h2", HT, pairs_ahead(p), "ffn")
                split(At(g0), p + RING)
                if 7 <= p <= 10:
                    up_copy(At(0), g0 + GD, p - 7, At(p - 7))
                if 8 <= p <= 11:
                    silu(At(p - 8), p - 8, None)
            for f in range(FT):
                up_copy(At(1), g0 + 2 * GD, f, At(FT + f))
            block_hi(At(0), None)
            with act.Fori(0, FB - 1) as b:
                g = At(g0 + 2 * GD, b, 3 * GD)
                for p in range(3 * GD):
                    split(g, p + RING)
                    if 7 <= p <= 10:
                        up_copy(At(2, b, 4), g.count(GD), p - 7, At(8 + p - 7, b, 8))
                    if 8 <= p <= 11:
                        silu(At(8 + p - 8, b, 8), p - 8, None)
                    if 15 <= p <= 18:
                        up_copy(At(3, b, 4), g.count(2 * GD), p - 15, At(12 + p - 15, b, 8))
                block_hi(At(1, b, 1), g.count(3 * GD))
            for p in range(GD):
                split(At(g0 + (3 * FB - 1) * GD), p + RING)

            for p in range(NCH * GD):
                g = At(GROUP0["mem"])
                split(g, p + RING)
                if p in (0, 4):
                    act.wait_ge(x_done, 1 + p // 4)
                    mean_squares([(X[:, t, :], MS[:, t:t + 1]) for t in range(T)], D ** -0.5, norm_ms)
                if p == 4:
                    act.dma_start(rows(x_scratch), X[:]).then_inc(x_stored, 16)
                if 12 <= p < 12 + KT:
                    transposed("h3", HT, [p - 12], "norm2")
                evacuations("mem", g, 0, p, NCH, lambda c: CKV[:, :, ds(c, CH)])
            act.wait_ge(x_stored, 16)
            project("c_proj", 2, lambda c: PB[:, :, ds(c, CH)])
            act.wait_ge(prod_free, 2 + PROD0["a_proj"])
            act.activation(PB[:, :, W:2 * W], PB[:, :, W:2 * W], ACT.Silu).then_inc(gate_ready, 1)

            def c_step(i, p):
                if p == 0:
                    head_squares(CMEM, At(0, i, 1))
                st = head_steps(CMEM, At(C0, i, 1), At(8, i, 1), i, ("cq", "ck"))
                if p % 2 == 0 and p // 2 - 1 in st:
                    st[p // 2 - 1]()
            with act.Fori(0, 4) as i:
                ch.enter(i, 3)
                g = At(GROUP0["a_proj"], i, 2 * GD)
                for p in range(2 * GD):
                    split(g, p + RING)
                    if p % GD == GD - 1:
                        c = p // GD
                        dst = PAC[:, ds(i * 2 + c, 1)].rearrange("p a t n -> p (a t) n")
                        evacuate(At(PROD0["a_proj"] + c, i, 2), g.count(p + 1), dst)
                    c_step(i, p)
            ch.leave(4)

            act.wait_ge(head_out, C0 + 4 + 1)
            act.wait_ge(bias_stored, 16 * NBIAS)
            for g in range(4):
                act.dma_start(BIAS[32 * g:32 * g + 32, :, :].rearrange("p h (s k) -> p h s k", s=3),
                              bias_scratch[8 * g:8 * g + 8].rearrange("h s p k -> p h s k")).then_inc(bias_loaded, 16)
            act.wait_ge(prod_free, 2 + PROD0["b_proj"])
            act.activation(PAC[:, 3:5], PAC[:, 3:5], ACT.Silu).then_inc(gate_ready, 1)
            act.wait_ge(idx_tr, 2)
            act.activation(QKT[:, 1, 0, :], PS[:, 5, 0:S], ACT.Copy).then_inc(idx_ready, 1)

            def index_step(i, p):
                k = At(p // 4, i, 4)
                if p % 4 == 0:
                    act.wait_ge(idx_tr, k.count(3))
                    act.activation(QKT[:, 0, 0, :], PS[:, 4, 0:S], ACT.Copy).then_inc(idx_ready, 1)
                elif p % 4 == 1:
                    act.wait_ge(idx_dots, k.count(1))
                    act.wait_ge(idx_sum, k.count(1))
                    act.activation(SC[:, 0:CAUS], PS[:, 6, 0:CAUS], ACT.Relu)
                    act.activation(PR[:, 0:CAUS], PS[:, 7, 0:CAUS], ACT.Relu).then_inc(idx_relu, 1)
                elif p % 4 == 3:
                    r = p // 4
                    for t in range(T):
                        q = PAC[:, ds(i, 1), t, r * P:(r + 1) * P].rearrange("p a d -> p (a d)")
                        link(act.activation(JK[:, 0:P], q, ACT.Square, scale=P ** -0.5, accum_out=MST[:, 0, t, ds(i * 4 + r, 1)]))
                    if r == 3:
                        for t in range(T):
                            link(act.activation(JK[:, 0:P], PAC[:, 2, t, ds(i * P, P)], ACT.Square, scale=P ** -0.5,
                                                accum_out=MST[:, 1, t, ds(i, 1)]))
            project("b_proj", 2, lambda c: PB[:, :, ds(c, CH)], index_step, 4 * T + T)
            act.sem_inc(a_ms, 1)

            act.wait_ge(prod_free, 2 + PROD0["merge_c"])
            for t in range(T):
                act.activation(PS[:, 4 + 2 * t, :], PB[:, t, 0:512], ACT.Square, scale=512 ** -0.5, accum_out=MS[:, t:t + 1])
                act.activation(PS[:, 5 + 2 * t, 0:256], PB[:, t, 512:768], ACT.Square, scale=1 / 16.0, accum_out=MS[:, 2 + t:3 + t])
                ins = act.activation(PS[:, 5 + 2 * t, 256:320], PB[:, t, 768:832], ACT.Square, scale=192 ** -0.5,
                                     accum_out=MS[:, 4 + t:5 + t])
            ins.then_inc(lat_ms, 1)
            act.activation(PB[:, :, 832:832 + W], PB[:, :, 832:832 + W], ACT.Silu).then_inc(gate_ready, 1)

            def a_step(i, p):
                r = p // 6
                st = head_steps(ASP, At(A0 + r, i, 4), At(12 + r, i, 4), i * 4 + r, ("aq", "ak"), (0, 1, 3, 5))
                if p - 6 * r in st:
                    st[p - 6 * r]()
            merge("merge_c", 2, 2, 0, a_step)

            act.wait_ge(head_out, A0 + 8 + 1)
            transposed("lat", LATT, range(6), "lat")
            g0, n0 = GROUP0["b_up"], PROD0["b_up"]
            scale = 192 ** -0.5

            def square_q(c):
                act.wait_ge(prod_free, 2 + n0 + c + 1)
                cols = slice(c * CH, (c + 1) * CH)
                return act.activation(SQQ[:, :, cols], QB[:, :, cols], ACT.Square, scale=scale)

            def square_k(c):
                act.wait_ge(prod_free, 2 + n0 + 3 + c + 1)
                src = KVB[:, :, c * CH:(c + 1) * CH].rearrange("p t (h d) -> p t h d", h=2)[:, :, :, 0:P]
                return act.activation(SQK[:, :, 2 * c:2 * c + 2, :], src, ACT.Square, scale=scale)
            for p in range(10):
                split(At(g0), p + RING)
                if p < 6 and p % 2:
                    evacuate(At(n0 + p // 2), g0 + p + 1, QB[:, :, p // 2 * CH:(p // 2 + 1) * CH])
                if p in (2, 4):
                    square_q(p // 2 - 1)
                if p >= 6:
                    evacuate(At(n0 + 3 + p - 6), g0 + p + 1, KVB[:, :, (p - 6) * CH:(p - 5) * CH])
                if p == 6:
                    square_q(2).then_inc(bq_sq, 1)
                if p > 6:
                    square_k(p - 7)
            square_k(3).then_inc(bk_sq, 1)

            def b_step(i, p):
                r = p // 6
                st = head_steps(BLA, At(B0 + r, i, 2), At(20 + r, i, 2), i * 2 + r, ("bqn", "bkn"), (0, 1, 3, 5))
                if p - 6 * r in st:
                    st[p - 6 * r]()
            merge("merge_a", NCH, 1, 0, b_step)
            act.wait_ge(head_out, HEADS + 1)
            act.dma_start(X[:], rows(x_scratch)).then_inc(x_back, 16)
            act.wait_ge(prod_free, 2 + PROD0["gates_b"])
            project("gates_b", 2, lambda c: SGX[:, :, ds(c, CH)], func=ACT.Sigmoid)
            for p in range(NCH * GW):
                split(At(GROUP0["up_b"]), p + RING)
                transposed("merged2", HT, merged_tiles(p), None)
            for p in range(NCH * GD):
                if p + RING < NCH * GD:
                    split(At(GROUP0["out2"]), p + RING)
                if p in (1, 2):
                    transposed("merged2", HT, merged_tiles(NCH * GW + p), None)
                if p % GD == GD - 1:
                    c = p // GD
                    act.wait_ge(out_ready, c + 1)
                    act.dma_start(rows(out)[:, :, c * CH:(c + 1) * CH], X[:, :, c * CH:(c + 1) * CH]).then_inc(out_stored, 16)
            act.wait_ge(out_stored, 16 * NCH)
            act.wait_ge(bias_stored, 16 * NBIAS)

        @block.vector
        def _(dve):
            ch = Chain(dve.wait_ge, dve_chain)
            link = ch.link

            def split(g, j):
                dve.wait_ge(hi_split, g.count(j + 1))
                s = g.slot(j)
                dve.tensor_tensor(WL[:, s], RAW[:, s], WH[:, s].bitcast(F32), ALU.subtract).then_inc(lo_split, 1)

            def stream(name, iters, per, steps=None, first=0):
                with dve.Fori(first, iters) as i:
                    for p in range(per):
                        split(At(GROUP0[name], i, per), p + RING)
                        if steps:
                            steps(i, p)

            def scaled_rows(dst, src, t, gain=None, cols=slice(0, D)):
                if gain is None:
                    return dve.tensor_scalar(dst[:, t, cols], src[:, t, cols], MS[:, t:t + 1], None, ALU.mult)
                return dve.scalar_tensor_tensor(out=dst[:, t, cols], in0=src[:, t, cols], scalar=MS[:, t:t + 1],
                                                in1=gain, op0=ALU.mult, op1=ALU.mult)

            def rows_by_halves(n):
                dve.wait_ge(norm_rstd, n)
                for cols in (slice(0, D // 2), slice(D // 2, D)):
                    for t in range(T):
                        ins = scaled_rows(ROWS, X, t, cols=cols)
                    ins.then_inc(norm_rows, 1)

            def transposed(name, dst, ks, gain):
                for k in ks:
                    at = TR[name] + k
                    dve.wait_ge(tr_hi, at + 1)
                    hi, ps = dst[:, k, 0, :].bitcast(F32), PS[:, 4 + at % 4, 0:S]
                    if gain:
                        ins = dve.scalar_tensor_tensor(out=dst[:, k, 1, :], in0=ps, scalar=par(gain, k), in1=hi,
                                                       op0=ALU.mult, op1=ALU.subtract)
                    else:
                        ins = dve.tensor_tensor(dst[:, k, 1, :], ps, hi, ALU.subtract)
                    ins.then_inc(tr_lo, 1)

            def head_scores(br, H, M, h):
                dve.wait_ge(scores, H.count(1))
                if br is RET:
                    dve.tensor_tensor(SC[:, 0:CAUS], PS[:, 6, 0:CAUS], DECAY[:, ds(h, 1), :].rearrange("p a n -> p (a n)"),
                                      ALU.mult).then_inc(probs, 1)
                    return
                if br["causal"]:
                    mask = BIAS[:, ds(h, 1), :].rearrange("p a n -> p (a n)") if br is ASP else con("mask")
                    link(dve.scalar_tensor_tensor(out=SC[:, 0:CAUS], in0=PS[:, 6, 0:CAUS], scalar=br["scale"], in1=mask,
                                                  op0=ALU.mult, op1=ALU.add))
                    cut, end = P, CAUS
                else:
                    link(dve.tensor_scalar(SC[:], PS[:, 6, :], br["scale"], None, ALU.mult))
                    cut, end = S, 2 * S
                dve.tensor_reduce(NM[:, 0:1], SC[:, 0:cut], AX_X, ALU.max, negate=True)
                dve.tensor_reduce(NM[:, 1:2], SC[:, cut:end], AX_X, ALU.max, negate=True).then_inc(maxima, 1)

            def head_values(br, H, gate):
                dv = br["dv"]
                if br is RET:
                    dve.wait_ge(o_rstd, At(H.base - RET0, H.i, H.per).count(1))
                    inv = MS
                else:
                    dve.wait_ge(probs, H.count(1))
                    link(dve.reciprocal(RI[:], RS[:]))
                    inv = RI
                dve.wait_ge(pv_done, H.count(1))
                for t in range(T):
                    o, ps = OF[:, t, 0:dv], PS[:, 4, t * dv:(t + 1) * dv]
                    if gate is None:
                        ins = dve.tensor_scalar(o, ps, inv[:, t:t + 1], None, ALU.mult)
                    else:
                        ins = dve.scalar_tensor_tensor(out=o, in0=ps, scalar=inv[:, t:t + 1], in1=gate(t),
                                                       op0=ALU.mult, op1=ALU.mult)
                ins.then_inc(o_rows, 1)

            def head_output(br, H, h):
                dve.wait_ge(ot_hi, H.count(1))
                nd = br["dv"] // P
                for c in range(nd):
                    u = U[br["u"]]
                    hi, lo = u[:, ds(h * nd + c, 1), 0, :].bitcast(F32), u[:, ds(h * nd + c, 1), 1, :]
                    ps = PS[:, 5:6, c * S:(c + 1) * S]
                    if br is RET:
                        ins = dve.scalar_tensor_tensor(out=lo, in0=ps, scalar=par("ret", h * nd + c), in1=hi,
                                                       op0=ALU.mult, op1=ALU.subtract)
                    else:
                        ins = dve.tensor_tensor(lo, ps, hi, ALU.subtract)
                ins.then_inc(head_out, 1)

            def head_steps(br, H, M, h, gate=None, at=(1, 4, 6)):
                return dict(zip(at, (lambda: head_scores(br, H, M, h), lambda: head_values(br, H, gate),
                                     lambda: head_output(br, H, h))))

            for s, n in ((head_out, 1), (dist_used, 1), (idx_sum, 1), (ffn_free, 2)):
                dve.sem_inc(s, n)

            dve.wait_ge(con_loaded, 16)
            dve.wait_ge(pos_loaded, 16)
            posf = RI
            link(dve.tensor_copy(posf[:], POSI[:]))
            for t in range(T):
                link(dve.tensor_scalar(ANG[:, 0, t], con("freq"), posf[:, t:t + 1], None, ALU.mult))
            ang = ANG[:, 0].rearrange("p t d -> p (t d)")
            mag = ANG[:, 1].rearrange("p t d -> p (t d)")
            turns_i = ANGI[:]
            turns = JK[:, 0:T * 32]
            link(dve.tensor_scalar(turns_i, ang, float(1 / (2 * np.pi)), None, ALU.mult))
            link(dve.tensor_copy(turns, turns_i))
            for part in (6.28125, 0.0019340515136718750, 1.2556659146770e-06):
                link(dve.scalar_tensor_tensor(out=ang, in0=turns, scalar=-part, in1=ang, op0=ALU.mult, op1=ALU.add))
            link(dve.tensor_scalar(ang, ang, 3.1415925, -3.1415925, ALU.min, ALU.max))
            dve.scalar_tensor_tensor(out=mag, in0=ang, scalar=-1.0, in1=ang, op0=ALU.mult, op1=ALU.max).then_inc(ang_ready, 1)

            rows_by_halves(1)
            for j in range(RING):
                split(At(0), j)
            dve.wait_ge(par_loaded, 16)
            for p in range(2 * GD):
                if p < GD:
                    transposed("h1", HT, pairs_ahead(p), "attn")
                split(At(GROUP0["moba_proj"]), p + RING)
            stream("moba_proj", 3, 2 * GD, first=1)

            with dve.Fori(0, 4) as i:
                ch.enter(i, 4)
                for p in range(2 * GD):
                    split(At(GROUP0["ret_proj"], i, 2 * GD), p + RING)
                    for r in range(2):
                        st = head_steps(MOBA, At(MOBA0 + r, i, 2), At(r, i, 2), i * 2 + r)
                        if p - 8 * r in st:
                            st[p - 8 * r]()
            ch.leave(4)
            dve.wait_ge(gate_ready, 1)
            dve.wait_ge(decay_loaded, 16)

            def merge(name, iters, chunks, merged, links=0, steps=None):
                add = name == "merge_a"
                per = chunks * (GD + GW)
                with dve.Fori(0, iters) as i:
                    ch.enter(i, links)
                    g = At(GROUP0[name], i, per)
                    for p in range(per):
                        split(g, p + RING)
                        b, r = p // (GD + GW), p % (GD + GW)
                        if r == GD + GW - 1:
                            n = At(PROD0[name] + 2 * b + 1, i, 2 * chunks)
                            dve.wait_ge(prod_free, n.count(2))
                            dve.wait_ge(group_used, g.count(p + 1))
                            ps = PS[:, 2 * (n.base % 2):2 * (n.base % 2) + 2, :]
                            m = merged[:, :, ds(i * (chunks * CH) + b * CH, CH)]
                            dve.tensor_tensor(TMP[:] if add else m, ps, SG[name][:], ALU.mult).then_inc(prod_free, 1)
                            if add:
                                dve.wait_ge(prod_free, n.count(3))
                                dve.tensor_tensor(m, m, TMP[:], ALU.add)
                        if steps:
                            steps(i, p)
                ch.leave(iters)

            def ret_step(i, p):
                st = head_steps(RET, At(RET0, i, 1), None, i, lambda t: PA[:, t, ds(i * 256 + 3 * W, 256)], (2, 7, 9))
                if p in st:
                    st[p]()
            merge("merge_moba", NCH, 1, MERGED["merged1"], 0, ret_step)

            def bias_step(i, p):
                if p + 1 not in BIAS_AT:
                    return
                k = At(BIAS_AT.index(p + 1), i, len(BIAS_AT))
                dve.wait_ge(dist_ready, k.count(1))
                dve.wait_ge(bias_done, k.count(1))
                link(dve.tensor_scalar(M1[:], DI[:], con("lo"), None, ALU.is_ge))
                dve.scalar_tensor_tensor(out=OH[:], in0=DI[:], scalar=con("hi"), in1=M1[:], op0=ALU.is_lt,
                                         op1=ALU.mult).then_inc(onehot, 1)
                dve.wait_ge(onehot, k.count(1))
                dve.sem_inc(dist_used, 1)
            with dve.Fori(0, 2) as i:
                ch.enter(i, len(BIAS_AT))
                for p in range(2 * GD):
                    split(At(GROUP0["gates_ret"], i, 2 * GD), p + RING)
                    bias_step(i, p)
            ch.leave(2)

            def up_chunk(name, merged, c):
                n, end = PROD0[name] + c, GROUP0[name] + (c + 1) * GW
                cols = slice(c * CH, (c + 1) * CH)
                dve.wait_ge(group_used, end)
                ps = PS[:, 2 * (n % 2):2 * (n % 2) + 2, :]
                dve.tensor_tensor(SGX[:, :, cols], ps, SGX[:, :, cols], ALU.mult).then_inc(prod_free, 1)
                dve.wait_ge(prod_free, 2 + n + 1)
                dve.tensor_tensor(merged[:, :, cols], merged[:, :, cols], SGX[:, :, cols], ALU.add).then_inc(merged_ready, 1)

            dve.wait_ge(prod_free, 2 + PROD0["up_ret"])
            for p in range(NCH * GW):
                split(At(GROUP0["up_ret"]), p + RING)
                transposed("merged1", HT, merged_tiles(p), None)
                if p % GW == GW - 1:
                    up_chunk("up_ret", MERGED["merged1"], p // GW)
                if p in (8, 12):
                    dve.wait_ge(norm_rstd, 2)
                    ins = scaled_rows(MEMR, MEMR, p // 4 - 2)
                    if p == 12:
                        ins.then_inc(norm_rows, 1)

            def residual(name, p):
                c = p // GD
                n = PROD0[name] + c
                dve.wait_ge(group_used, GROUP0[name] + p + 1)
                o = X[:, :, c * CH:(c + 1) * CH]
                return dve.tensor_tensor(o, PS[:, 2 * (n % 2):2 * (n % 2) + 2, :], o, ALU.add)
            dve.wait_ge(x_loaded, 16)
            for p in range(NCH * GD):
                split(At(GROUP0["out1"]), p + RING)
                if p in (1, 2):
                    transposed("merged1", HT, merged_tiles(NCH * GW + p), None)
                if 4 <= p < 4 + KT:
                    transposed("mem", MEMT, [p - 4], "mem")
                if p % GD == GD - 1:
                    residual("out1", p).then_inc(prod_free, 1)
            dve.wait_ge(x_sq, 1)
            dve.tensor_reduce(MS[:, 0:T], MSC[:], AX_X, ALU.add).then_inc(norm_ms, 1)
            link(dve.memset(FU[:, :, 0:2], 0.0))
            rows_by_halves(3)

            def conv(u, f, tile, feature, silu_done):
                dve.wait_ge(ffn_copied, tile.count(1))
                z, y = FU[:, f % 2, :], FY[:, f % 2, :]
                ins = dve.tensor_tensor(z[:, 2:S + 2], PS[:, 4 * (u.base % 2) + f, S:2 * S], FC[:, f % 2, :], ALU.add)
                link(ins)
                if f == FT - 1:
                    dve.sem_inc(ffn_free, 1)
                if silu_done is not None:
                    dve.wait_ge(ffn_silu, silu_done)
                link(dve.tensor_scalar(y, z[:, 2:S + 2], par("conv", feature * 4 + 2), par("conv", feature * 4 + 3),
                                       ALU.mult, ALU.add))
                link(dve.scalar_tensor_tensor(out=y, in0=z[:, 1:S + 1], scalar=par("conv", feature * 4 + 1), in1=y,
                                              op0=ALU.mult, op1=ALU.add))
                return dve.scalar_tensor_tensor(out=y, in0=z[:, 0:S], scalar=par("conv", feature * 4), in1=y,
                                                op0=ALU.mult, op1=ALU.add)

            def a_tile(u, f, tile, feature, silu_done):
                conv(u, f, tile, feature, silu_done).then_inc(ffn_conv, 1)

            def b_tile(u, f, tile, feature, silu_done):
                conv(u, f, tile, feature, silu_done).then_inc(ffn_conv, 1)
                dve.wait_ge(ffn_conv, tile.count(1))
                ins = dve.tensor_tensor(FP[:, f, :], FA[:, f, :], FY[:, f % 2, :], ALU.mult)
                if f == FT - 1:
                    ins.then_inc(ffn_prod, 1)

            def block_lo(blk):
                dve.wait_ge(ffn_hi, blk.count(1))
                dve.tensor_tensor(ACTT[:, :, 1, :], FP[:], ACTT[:, :, 0, :].bitcast(F32), ALU.subtract).then_inc(ffn_lo, 1)

            def down_add(u, end):
                dve.wait_ge(group_used, end)
                half, c0 = 4 * (u.base % 2), 2 * (u.base % 2)
                for c in range(2):
                    o = X[:, :, (c0 + c) * CH:(c0 + c + 1) * CH]
                    ins = dve.tensor_tensor(o, PS[:, half + 2 * c:half + 2 * c + 2, :], o, ALU.add)
                ins.then_inc(ffn_free, 1)

            g0 = GROUP0["ffn"]
            for p in range(2 * GD):
                if p < GD:
                    transposed("h2", HT, pairs_ahead(p), "ffn")
                split(At(g0), p + RING)
                if 7 <= p <= 10:
                    f = p - 7
                    a_tile(At(0), f, At(f), f, f - 1 if f >= 2 else None)
            for f in range(FT):
                b_tile(At(1), f, At(FT + f), NFT // 2 + f, FT)
            block_lo(At(0))
            with dve.Fori(0, FB - 1) as b:
                ch.enter(b, 3 * 2 * FT)
                g = At(g0 + 2 * GD, b, 3 * GD)
                for p in range(3 * GD):
                    split(g, p + RING)
                    if 7 <= p <= 10:
                        f = p - 7
                        a_tile(At(2, b, 4), f, At(8 + f, b, 8), b * FT + (FT + f),
                               At(FT + f - 1, b, FT).count() if f >= 2 else None)
                    if 15 <= p <= 18:
                        f = p - 15
                        b_tile(At(3, b, 4), f, At(12 + f, b, 8), b * FT + (NFT // 2 + FT + f), At(2 * FT, b, FT).count())
                    if p == 19:
                        down_add(At(4, b, 4), g.count(2 * GD + 4))
                    if p == 23:
                        down_add(At(5, b, 4), g.count(3 * GD))
                block_lo(At(1, b, 1))
            ch.leave(FB - 1)
            for p in range(GD):
                split(At(g0 + (3 * FB - 1) * GD), p + RING)
                if p == 3:
                    down_add(At(4 * FB - 2), g0 + (3 * FB - 1) * GD + 4)
                if p == 7:
                    down_add(At(4 * FB - 1), g0 + 3 * FB * GD)
            dve.wait_ge(ffn_free, 2 + 4 * FB)
            dve.sem_inc(x_done, 1)

            dve.wait_ge(fw_loaded, 16)
            for p in range(NCH * GD):
                split(At(GROUP0["mem"]), p + RING)
                if p in (2, 3):
                    dve.wait_ge(norm_rstd, 4)
                    ins = scaled_rows(X, X, p - 2, FINALW[:])
                    if p == 3:
                        ins.then_inc(x_done, 1)
                if p in (6, 7):
                    dve.wait_ge(norm_rstd, 5)
                    scaled_rows(ROWS, X, p - 6).then_inc(norm_rows, 1)
                if 12 <= p < 12 + KT:
                    transposed("h3", HT, [p - 12], "norm2")
            stream("c_proj", 2, 2 * GD)

            dve.wait_ge(gate_ready, 2)
            with dve.Fori(0, 4) as i:
                ch.enter(i, 2)
                st = head_steps(CMEM, At(C0, i, 1), At(8, i, 1), i, lambda t: PB[:, t, ds(i * 256 + W, 256)])
                for p in range(2 * GD):
                    split(At(GROUP0["a_proj"], i, 2 * GD), p + RING)
                    if p % 2 == 0 and p // 2 - 1 in st:
                        st[p // 2 - 1]()
            ch.leave(4)

            link(dve.memset(PT[:, 0:CAUS], 0.0))
            dve.wait_ge(prod_free, 2 + PROD0["b_proj"])
            with dve.Fori(0, 2) as i:
                ch.enter(i, 4 * 2)
                for p in range(2 * GD):
                    split(At(GROUP0["b_proj"], i, 2 * GD), p + RING)
                    if p % 4 == 2:
                        k = At(p // 4, i, 4)
                        dve.wait_ge(idx_relu, k.count(2))
                        for j, src in enumerate((SC, PR)):
                            for t, cols in enumerate((slice(0, P), slice(P, CAUS))):
                                w = PAC[:, 7, t, ds(i * 8 + (64 + 2 * (p // 4) + j), 1)]
                                ins = dve.scalar_tensor_tensor(out=PT[:, cols], in0=src[:, cols], scalar=w, in1=PT[:, cols],
                                                               op0=ALU.mult, op1=ALU.add)
                            link(ins)
                        dve.sem_inc(idx_sum, 1)
            ch.leave(2)

            masked, left = SC, OF[:].rearrange("p t d -> p (t d)")
            link(dve.tensor_tensor(masked[:, 0:CAUS], PT[:, 0:CAUS], con("mask"), ALU.add))
            src = masked
            for _ in range(8):
                for t, cols in enumerate((slice(0, P), slice(P, CAUS))):
                    ins = dve.max(M8[:, t, :], src[:, cols])
                link(ins)
                for t, cols in enumerate((slice(0, P), slice(P, CAUS))):
                    ins = dve.match_replace(left[:, cols], M8[:, t, :], src[:, cols], TAKEN)
                link(ins)
                src = left
            link(dve.tensor_scalar(left[:, 0:CAUS], left[:, 0:CAUS], TAKEN, -1.0, ALU.is_equal, ALU.add))
            link(dve.scalar_tensor_tensor(out=SC[:, 0:CAUS], in0=left[:, 0:CAUS], scalar=-NEG, in1=con("mask"),
                                          op0=ALU.mult, op1=ALU.add))
            dve.wait_ge(bias_loaded, 64)
            dve.tensor_tensor(BIAS[:], BIAS[:], SC[:, 0:CAUS].unsqueeze(1).broadcast_to([P, REL_HEADS, CAUS]),
                              ALU.add).then_inc(sel_ready, 1)

            dve.wait_ge(sel_ready, 1)
            dve.wait_ge(gate_ready, 3)
            dve.wait_ge(lat_rstd, 1)
            for t in range(T):
                dve.tensor_scalar(PB[:, t, 0:512], PB[:, t, 0:512], MS[:, t:t + 1], None, ALU.mult)
                ins = dve.tensor_scalar(PB[:, t, 512:768], PB[:, t, 512:768], MS[:, 2 + t:3 + t], None, ALU.mult)
            ins.then_inc(lat_rows, 1)

            def a_step(i, p):
                r = p // 6

                def gate(t):
                    return PAC[:, ds(i + 3, 1), t, r * P:(r + 1) * P].rearrange("p a d -> p (a d)")
                st = head_steps(ASP, At(A0 + r, i, 4), At(12 + r, i, 4), i * 4 + r, gate, (1, 4, 5))
                if p - 6 * r in st:
                    st[p - 6 * r]()
            merge("merge_c", 2, 2, MERGED["merged2"], 4 * 2, a_step)
            transposed("lat", LATT, range(6), "lat")
            for p in range(10):
                split(At(GROUP0["b_up"]), p + RING)
                if p == 8:
                    dve.wait_ge(bq_sq, 1)
                    dve.tensor_reduce(MST[:, 0].rearrange("p t h -> p (t h)"), SQQ[:].rearrange("p t (h d) -> p (t h) d", d=192),
                                      AX_X, ALU.add)
            dve.wait_ge(bk_sq, 1)
            dve.tensor_reduce(MST[:, 1].rearrange("p t h -> p (t h)"), SQK[:].rearrange("p t h d -> p (t h) d"),
                              AX_X, ALU.add).then_inc(b_ms, 1)
            dve.wait_ge(gate_ready, 4)

            def b_step(i, p):
                r = p // 6
                h = i * 2 + r
                st = head_steps(BLA, At(B0 + r, i, 2), At(20 + r, i, 2), h, lambda t: PB[:, t, ds(h * P + 832, P)], (1, 4, 5))
                if p - 6 * r in st:
                    st[p - 6 * r]()
            merge("merge_a", NCH, 1, MERGED["merged2"], 2 * 2, b_step)
            stream("gates_b", 2, 2 * GD)
            dve.wait_ge(prod_free, 2 + PROD0["up_b"])
            for p in range(NCH * GW):
                split(At(GROUP0["up_b"]), p + RING)
                transposed("merged2", HT, merged_tiles(p), None)
                if p % GW == GW - 1:
                    up_chunk("up_b", MERGED["merged2"], p // GW)
            dve.wait_ge(x_back, 16)
            for p in range(NCH * GD):
                if p + RING < NCH * GD:
                    split(At(GROUP0["out2"]), p + RING)
                if p in (1, 2):
                    transposed("merged2", HT, merged_tiles(NCH * GW + p), None)
                if p % GD == GD - 1:
                    link(residual("out2", p))
                    dve.sem_inc(prod_free, 1)
                    dve.sem_inc(out_ready, 1)


def groups_of(w):
    k, n = w.shape
    return w.reshape(k // (GK * P), GK, P, n // CH, CH).transpose(3, 0, 2, 1, 4).reshape(n // CH, -1, P, GK * CH)


def lay_out(x):
    w_in, w_in2 = x["w_in"][0], x["w_in_2"][0]
    stream = np.empty((GROUPS, P, GK * CH), np.float32)
    at = [0]

    def put(*parts):
        for c in range(len(parts[0])):
            for part in parts:
                stream[at[0]:at[0] + part.shape[1]] = part[c]
                at[0] += part.shape[1]

    def padded(w, n):
        return np.concatenate([w, np.zeros((w.shape[0], n - w.shape[1]), w.dtype)], 1)

    put(groups_of(w_in[:, 4 * W:7 * W]))
    put(groups_of(w_in[:, 0:4 * W]))
    gates = 7 * W
    put(groups_of(w_in[:, gates + D:gates + 2 * D]), groups_of(x["w_moba_up"][0]))
    put(groups_of(w_in[:, gates:gates + D]))
    put(groups_of(x["w_ret_up"][0]))
    put(groups_of(x["w_out"][0]))
    up, down = groups_of(x["w_ffn_up"][0]), x["w_ffn_down"][0]
    for b in range(FB + 1):
        if b < FB:
            put(up[b:b + 1])
            put(up[FB + b:FB + b + 1])
        if b:
            put(groups_of(down[(b - 1) * CH:b * CH]))
    put(groups_of(x["w_mem_kv_2"][0]))
    put(groups_of(w_in2[:, 5520:7568]))
    put(groups_of(padded(w_in2[:, 0:3664], 4096)))
    put(groups_of(padded(w_in2[:, 3664:5520], 2048)))
    branch = x["w_branch_2"][0]
    a_gate, b_gate, c_gate = [groups_of(w_in2[:, 7568 + b * D:7568 + (b + 1) * D]) for b in range(3)]
    put(c_gate, groups_of(branch[2]))
    put(groups_of(x["w_b_uq_2"][0]))
    put(groups_of(x["w_b_ukv_2"][0]))
    put(a_gate, groups_of(branch[0]))
    put(b_gate)
    put(groups_of(branch[1]))
    put(groups_of(x["w_out_2"][0]))
    assert at[0] == GROUPS

    pack = np.zeros((P, NPAR), np.float32)

    def par(name, value):
        o, n = PAR[name]
        pack[:, o:o + n] = value

    def columns(v):
        return v.reshape(-1, P).T

    par("attn", columns(x["attn_norm_w"]))
    par("ffn", columns(x["ffn_norm_w"]))
    par("norm2", columns(x["norm_g_2"]))
    par("mem", columns(x["mem_norm_g_2"]))
    par("ret", columns(x["ret_norm_w"]))
    par("aq", columns(x["a_q_norm_g_2"]))
    par("ak", columns(x["a_k_norm_g_2"]))
    par("lat", np.concatenate([columns(x["b_q_lat_norm_g_2"]), columns(x["b_kv_lat_norm_g_2"])], 1))
    par("cq", columns(x["c_q_norm_g_2"]))
    par("ck", columns(x["c_k_norm_g_2"]))
    par("bqn", x["b_q_norm_g_2"][:, 0:P].T)
    par("bkn", x["b_k_norm_g_2"][:, 0:P].T)
    par("brope", np.concatenate([x["b_q_norm_g_2"][:, P:], x["b_k_norm_g_2"][:, P:]], 1))
    taps = np.concatenate([x["conv_w"][0], x["conv_b"]], 0)
    par("conv", taps.reshape(4, NFT, P).transpose(2, 1, 0).reshape(P, -1))
    table = np.zeros((P, 32), np.float32)
    for g in range(4):
        table[32 * g:32 * g + 32, 8 * g:8 * g + 8] = x["rel_bias_2"]
    par("rel", table)

    pos = x["positions_2"].reshape(S)
    ints = np.zeros((P, POSN + 2), np.int32)
    for g in range(4):
        rows = slice(32 * g, 32 * g + 32)
        ints[rows, 0:32] = pos[32 * g:32 * g + 32]
        ints[rows, 32:64] = pos[P + 32 * g:P + 32 * g + 32]
    ints[:, 64:POSN] = pos
    ints[:, POSN:] = pos.reshape(T, P).T
    return stream, pack, ints


def kernel(**inputs):
    import concourse.bacc as bacc
    from concourse.bass_utils import run_bass_kernel_spmd

    x = {name: np.asarray(a) for name, a in inputs.items()}
    stream, pack, ints = lay_out(x)
    arrays = {"x_in": x["x"].reshape(S, D), "mem_in": x["mem_2"].reshape(S, D), "w_stream": stream, "params": pack,
              "final_w": x["final_norm_w"], "pos_pack": ints, "constants": make_constants()}
    arrays = {name: np.ascontiguousarray(a) for name, a in arrays.items()}
    nc = bacc.Bacc("TRN2", target_bir_lowering=False, num_devices=1)
    args = [nc.dram_tensor(name, a.shape, mybir.dt.from_np(a.dtype), kind="ExternalInput").ap() for name, a in arrays.items()]
    out = nc.dram_tensor("out", (S, D), F32, kind="ExternalOutput").ap()
    build(nc, *args, out)
    r = run_bass_kernel_spmd(nc, [arrays], core_ids=[0])
    return r.results[0]["out"].reshape(1, S, D)
```

```python
from contextlib import ExitStack

import concourse.bass as bass
import numpy as np
from concourse import mybir

F32 = mybir.dt.float32
F32R = mybir.dt.float32r
I32 = mybir.dt.int32
ALU = mybir.AluOpType
ACT = mybir.ActivationFunctionType
AX_X = mybir.AxisListType.X
ds = bass.ds

P = 128
D = 2048
S = 256
T = S // P
FF = 5632
CH = 512
GK = 2
KT = D // P
RING = 4
EPS = 1e-6
DMA_SCRATCH = 1024
NEG = -1.0e30
TAKEN = -3.0e38
W = 1024
NCH = D // CH
GD = KT // GK
GW = W // P // GK
FB = FF // CH
FT = CH // P
NFT = 2 * FF // P
CAUS = 3 * P
BUCKETS, REL_HEADS = 32, 8
NBIAS = NCH * 3
POSN = 64 + S

PHASES = [
    ("moba_proj", 6 * GD, 6), ("ret_proj", 8 * GD, 8), ("merge_moba", NCH * (GD + GW), 2 * NCH),
    ("gates_ret", NCH * GD, NCH), ("up_ret", NCH * GW, NCH), ("out1", NCH * GD, NCH), ("mem0", GD, 1),
    ("ffn", (FB * 3 - 1) * GD, 0), ("mem1", GD, 1), ("ffn_down", GD, 0), ("mem2", 2 * GD, 2),
    ("c_proj", 4 * GD, 4), ("a_proj", 8 * GD, 8), ("b_proj", 3 * GD, 3),
    ("gates_b0", GD, 1), ("merge_c", NCH * (GD + GW), 2 * NCH), ("b_up", 3 * 2 + 4, 7), ("gates_b1", GD, 1),
    ("merge_a", NCH * (GD + GW), 2 * NCH), ("gates_b", 2 * GD, 2), ("up_b", NCH * GW, NCH), ("out2", NCH * GD, NCH)]
GROUP0, PROD0 = {}, {}
_g = _n = 0
for _name, _groups, _prods in PHASES:
    GROUP0[_name], PROD0[_name] = _g, _n
    _g, _n = _g + _groups, _n + _prods
GROUPS = _g

MOBA0, RET0, C0, A0, B0, HEADS = 0, 8, 12, 16, 24, 32

PAR = {}


def _columns(table, *widths):
    at = 0
    for name, n in widths:
        table[name] = (at, n)
        at += n
    return at


NPAR = _columns(PAR, ("attn", KT), ("ffn", KT), ("norm2", KT), ("mem", KT), ("ret", 8), ("aq", 1), ("ak", 1),
                ("lat", 6), ("cq", 2), ("ck", 2), ("bqn", 1), ("bkn", 1), ("brope", 128), ("conv", 4 * NFT), ("rel", 32))
CON = {}
NFIRST = P + 32 + 32
NCON = _columns(CON, ("ident", P), ("eps", 32), ("half", 32), ("mask", CAUS), ("rcos", S), ("rsin", S),
                ("mcos", 64), ("msin", 64), ("freq", 32), ("lo", 1), ("hi", 1), ("hpi", 1))


def make_constants():
    c = np.zeros((P, NCON + 4 * CAUS), np.float32)

    def put(name, value):
        o, n = CON[name]
        c[:, o:o + n] = np.asarray(value, np.float32).reshape(-1, n)

    i = np.arange(P)
    tri = i[None, :] <= i[:, None]
    put("ident", np.eye(P))
    put("mask", np.concatenate([np.where(tri, 0, NEG), np.zeros((P, P)), np.where(tri, 0, NEG)], 1))
    decay = np.zeros((P, 4, CAUS))
    for h in range(4):
        lg = np.log1p(-np.exp2(-5.0 - h))
        own = np.where(tri, np.exp(lg * np.maximum(i[:, None] - i[None, :], 0)), 0)
        across = np.exp(lg * (i[:, None] + 1.0)) * np.exp(lg * (P - 1.0 - i[None, :]))
        decay[:, h] = np.concatenate([own.T, across.T, own.T], 1) / 16.0
    c[:, NCON:] = decay.reshape(P, -1)
    pos = np.arange(S, dtype=np.float32)

    def angles(theta, dim):
        inv = np.float32(theta) ** (-np.arange(0, dim, 2, dtype=np.float32) / np.float32(dim))
        return (pos[:, None] * inv[None, :].astype(np.float32)).astype(np.float32).astype(np.float64)

    a = angles(10000.0, 256).reshape(T, P, P).transpose(1, 0, 2)
    put("rcos", np.cos(a).reshape(P, -1))
    put("rsin", np.sin(a).reshape(P, -1))
    a = angles(500000.0, 32).reshape(T, P, 16).transpose(1, 0, 2).reshape(P, 1, -1).repeat(2, 1)
    put("mcos", np.cos(a).reshape(P, -1))
    put("msin", np.sin(a).reshape(P, -1))
    inv = (1.0 / (np.float32(10000.0) ** (np.arange(0, 64, 2, dtype=np.float32) / np.float32(64)))).astype(np.float32)
    put("freq", inv)
    n = np.arange(1, 4096)
    large = 16 + (np.log(n.astype(np.float32) / np.float32(16)) / np.float32(np.log(8.0)) * np.float32(16)).astype(np.int32)
    bucket = np.where(n < 16, n, np.minimum(large, 31))
    low = np.array([-3.0e9] + [n[bucket >= b][0] for b in range(1, 32)], np.float32)
    high = np.append(low[1:], np.float32(3.0e9))
    put("lo", np.tile(low, 4)[:, None])
    put("hi", np.tile(high, 4)[:, None])
    put("eps", np.full(32, EPS))
    put("half", np.full(32, -0.5))
    put("hpi", np.pi / 2)
    return c


class At:

    def __init__(self, base, i=0, per=0):
        self.base, self.i, self.per = base, i, per

    def count(self, k=0):
        return self.base + k + self.i * self.per if self.per else self.base + k

    def slot(self, k):
        return (self.base + k) % RING

    def turn(self, k):
        n = (self.base + k) // RING
        return n + self.i * (self.per // RING) if self.per else n


class Chain:

    def __init__(self, wait, sem):
        self.wait, self.sem, self.total, self.k, self.i, self.per = wait, sem, 0, 0, 0, 0

    def link(self, ins):
        self.k += 1
        ins.then_inc(self.sem, 1)
        self.wait(self.sem, self.total + self.k + self.i * self.per if self.per else self.total + self.k)

    def enter(self, i, per):
        self.total, self.k, self.i, self.per = self.total + self.k, 0, i, per

    def leave(self, n):
        assert self.k == self.per, (self.k, self.per)
        self.total, self.k, self.i, self.per = self.total + n * self.per, 0, 0, 0


def build(nc, x_in, mem_in, w_stream, params, final_w, pos_pack, constants, out):
    with ExitStack() as ctx:
        def sem(name):
            return ctx.enter_context(nc.semaphore(name))

        START = DMA_SCRATCH + P
        cursor = [START]

        def take(nbytes):
            at = cursor[0]
            cursor[0] += nbytes
            return at

        def sb(name, shape, dt, at):
            return nc.alloc_sbuf_tensor_at(name, shape, dt, offset=at)

        KB = 1024
        at_x, at_ht, at_pa, at_pb, at_u2 = take(16 * KB), take(32 * KB), take(36 * KB), take(16 * KB), take(16 * KB)
        at_u0, at_u1 = take(16 * KB), take(16 * KB)
        X = sb("X", [P, T, D], F32, at_x)
        HT = sb("HT", [P, KT, 2, S], F32R, at_ht)
        PA = sb("PA", [P, T, 4096], F32, at_pa)
        PAC = sb("PAC", [P, 8, T, CH], F32, at_pa)
        PB = sb("PB", [P, T, D], F32, at_pb)
        ROWS = sb("ROWS", [P, T, D], F32, at_pa)
        MEMR = sb("MEMR", [P, T, D], F32, at_pa + 16 * KB)
        MEMT = sb("MEMT", [P, KT, 2, S], F32R, at_pb)
        MQKV = sb("MQKV", [P, T, 3 * W], F32, at_pb)
        MERGED = {"merged1": sb("MERGED1", [P, T, D], F32, at_pb), "merged2": sb("MERGED2", [P, T, D], F32, at_pa + 20 * KB)}
        at_sgx = take(16 * KB)
        SGX = sb("SGX", [P, NCH * T * CH], F32, at_sgx)
        QB = sb("QB", [P, T, 1536], F32, at_pa)
        KVB = sb("KVB", [P, T, 2048], F32, at_u0)
        U = [sb("U0", [P, 8, 2, S], F32R, at_u0), sb("U1", [P, 8, 2, S], F32R, at_u1),
             sb("U2", [P, 8, 2, S], F32R, at_u2)]
        ACTT = sb("ACTT", [P, FT, 2, S], F32R, at_u0)
        FINALW = sb("FINALW", [P, D], F32, at_u0 + 8 * KB)
        FU = sb("FU", [P, FT, S + 2], F32, at_u1)
        FC = sb("FC", [P, FT, S], F32, at_u1 + 4160)
        FY = sb("FY", [P, 2, S], F32, at_u1 + 4160 + 4 * KB)
        FA = sb("FA", [P, FT, S], F32, at_pa + 16 * KB)
        FP = sb("FP", [P, FT, S], F32, at_pa + 20 * KB)
        DECAY = sb("DECAY", [P, 4, CAUS], F32, at_u2 + 8 * KB)
        CKV = sb("CKV", [P, T, 2 * W], F32, at_sgx)
        JUNK = sb("JUNK", [P, T, D], F32, at_u1)
        BIAS = sb("BIAS", [P, REL_HEADS, CAUS], F32, at_u2)
        LATT = sb("LATT", [P, 6, 2, S], F32R, at_sgx + 4 * KB)
        SG = {"merge_moba": sb("SG_MOBA", [P, T, CH], F32, at_u2), "merge_c": sb("SG_C", [P, T, CH], F32, at_u2 + 12 * KB),
              "merge_a": sb("SG_A", [P, T, CH], F32, at_pa + 12 * KB)}
        TMP = sb("TMP", [P, T, CH], F32, at_pa + 16 * KB)
        SQQ = sb("SQQ", [P, T, 1536], F32, at_x)
        SQK = sb("SQK", [P, T, 8, P], F32, at_pa + 12 * KB)
        QK = sb("QK", [P, 2, T, 256], F32, at_x)
        QKT = sb("QKT", [P, 2, 2, S], F32, at_x + 4 * KB)
        SC = sb("SC", [P, 512], F32, at_x + 8 * KB)
        PR = sb("PR", [P, 512], F32, at_x + 10 * KB)
        PT = sb("PT", [P, 512], F32, at_x + 12 * KB)
        OF = sb("OF", [P, T, 256], F32, at_x + 14 * KB)
        POSB = sb("POSB", [P, POSN], I32, at_u2 + 4 * KB)
        ANG = sb("ANG", [P, 2, T, 32], F32, at_u1)
        ANGI = sb("ANGI", [P, T * 32], I32, at_u1 + KB)
        DI = sb("DI", [P, 8, P], I32, at_x)
        OH = sb("OH", [P, 2, 8, P], F32R, at_x + 4 * KB)
        BE = sb("BE", [32, 8, P], F32, at_x + 12 * KB)
        RAW = sb("RAW", [P, RING, GK, CH], F32, take(16 * KB))
        WH = sb("WH", [P, RING, GK, CH], F32R, take(16 * KB))
        WL = sb("WL", [P, RING, GK, CH], F32R, take(16 * KB))
        CONST = sb("CONST", [P, NCON], F32, take(4 * NCON // 32 * 32 + 32))
        PARAM = sb("PARAM", [P, NPAR], F32, take(4 * NPAR // 32 * 32 + 32))
        POSI = sb("POSI", [P, 2], I32, take(32))
        ROPE = sb("ROPE", [P, 2, 2, T, 32], F32, take(1024))
        JK = sb("JK", [P, 256], F32, take(1024))
        REL = sb("REL", [P, 2, 32], F32R, take(256))
        MS = sb("MS", [P, 8], F32, take(32))
        MSC = sb("MSC", [P, T, NCH], F32, take(32))
        MST = sb("MST", [P, 2, T, 8], F32, take(128))
        NM = sb("NM", [P, 2], F32, take(32))
        RS = sb("RS", [P, 2], F32, take(32))
        RI = sb("RI", [P, 2], F32, take(32))
        M8 = sb("M8", [P, T, 8], F32, take(64))
        assert cursor[0] <= nc.sbuf_usable_end
        PS = ctx.enter_context(nc.psum_tensor("PS", [P, 8, 512], F32))

        bias_scratch = nc.dram_tensor("bias_scratch", (32, 3, 32, P), F32, kind="Internal").ap()
        x_scratch = nc.dram_tensor("x_scratch", (S, D), F32, kind="Internal").ap()

        def con(name, rows=P):
            o, n = CON[name]
            return CONST[0:rows, o:o + n]

        def par(name, k=0, n=1):
            o = k + PAR[name][0]
            return PARAM[:, ds(o, n)]

        def gate_chunk(col):
            return SGX[:, ds(col * T, T * CH)].rearrange("p (t n) -> p t n", t=T)

        ident = con("ident")
        IK, IW, KV_LAT, KPE = slice(0, 64), 64, slice(80, 336), slice(336, 400)
        PB_KV, PB_Z, PB_KPE = slice(512, 768), 768, slice(768 + W, 768 + W + 64)

        def rows(dram):
            return dram.rearrange("(t p) d -> p t d", p=P)

        raw_landed = [sem(f"raw_landed{s}") for s in range(RING)]
        hi_split = sem("hi_split")
        lo_split = sem("lo_split")
        group_used = sem("group_used")
        prod_free = sem("prod_free")
        ffn_free = sem("ffn_free")
        ffn_copied = sem("ffn_copied")
        ffn_sum = sem("ffn_sum")
        ffn_conv = sem("ffn_conv")
        ffn_silu = sem("ffn_silu")
        ffn_prod = sem("ffn_prod")
        ffn_hi = sem("ffn_hi")
        ffn_lo = sem("ffn_lo")
        x_first = [sem(f"x_first{t}") for t in range(T)]
        x_loaded = sem("x_loaded")
        con_loaded = sem("con_loaded")
        tables_loaded = sem("tables_loaded")
        decay_loaded = sem("decay_loaded")
        par_loaded = sem("par_loaded")
        pos_loaded = sem("pos_loaded")
        norm_ms = sem("norm_ms")
        norm_rstd = sem("norm_rstd")
        norm_rows = sem("norm_rows")
        x_sq = sem("x_sq")
        tr_done = sem("tr_done")
        tr_hi = sem("tr_hi")
        tr_lo = sem("tr_lo")
        qk_raw = sem("qk_raw")
        qk_ms = sem("qk_ms")
        qk_fixed = sem("qk_fixed")
        qk_tr = sem("qk_tr")
        qkt_ready = sem("qkt_ready")
        scores = sem("scores")
        maxima = sem("maxima")
        probs = sem("probs")
        pt_done = sem("pt_done")
        pt_ready = sem("pt_ready")
        pv_done = sem("pv_done")
        o_ms = sem("o_ms")
        o_rstd = sem("o_rstd")
        o_rows = sem("o_rows")
        ot_done = sem("ot_done")
        ot_hi = sem("ot_hi")
        head_out = sem("head_out")
        gate_ready = sem("gate_ready")
        merged_ready = sem("merged_ready")
        rel_hi = sem("rel_hi")
        rel_lo = sem("rel_lo")
        dist_ready = sem("dist_ready")
        dist_used = sem("dist_used")
        onehot = sem("onehot")
        bias_done = sem("bias_done")
        bias_copied = sem("bias_copied")
        bias_stored = sem("bias_stored")
        bias_loaded = sem("bias_loaded")
        ang_ready = sem("ang_ready")
        rope_ready = sem("rope_ready")
        mem_loaded = sem("mem_loaded")
        fw_loaded = sem("fw_loaded")
        x_done = sem("x_done")
        x_stored = sem("x_stored")
        x_back = sem("x_back")
        idx_fixed = sem("idx_fixed")
        idx_tr = sem("idx_tr")
        idx_ready = sem("idx_ready")
        idx_dots = sem("idx_dots")
        idx_relu = sem("idx_relu")
        idx_sum = sem("idx_sum")
        sel_ready = sem("sel_ready")
        a_ms = sem("a_ms")
        bq_sq = sem("bq_sq")
        bk_sq = sem("bk_sq")
        b_ms = sem("b_ms")
        lat_ms = sem("lat_ms")
        lat_rstd = sem("lat_rstd")
        lat_rows = sem("lat_rows")
        out_ready = sem("out_ready")
        out_stored = sem("out_stored")
        dve_chain = sem("dve_chain")
        pool_chain = sem("pool_chain")
        act_chain = sem("act_chain")
        pool_held = sem("pool_held")

        block = ctx.enter_context(nc.Block())

        MOBA = dict(d=[128], causal=True, dv=128, scale=128 ** -0.5, u=1)
        RET = dict(d=[128, 128], causal=True, dv=256, scale=None, u=0)
        CMEM = dict(d=[128, 128], causal=False, dv=256, scale=256 ** -0.5, u=0)
        ASP = dict(d=[128], causal=True, dv=128, scale=128 ** -0.5, u=1)
        BLA = dict(d=[128, 64], causal=True, dv=128, scale=192 ** -0.5, u=2)

        TR = {"h1": 0, "merged1": 16, "mem": 32, "h2": 48, "h3": 64, "lat": 80, "merged2": 86}
        BIAS_AT = (2, 4, 7, 10, 12, 15)

        def pairs_ahead(q):
            return [k for k in range(2 * q + 2 if q else 0, 2 * q + 4) if k < KT]

        PAIRS = 8
        TOPK_AT = 2 * PAIRS + 2

        def h3_tiles(p):
            return range(3 * (p - 9), min(3 * (p - 8), KT)) if p >= 9 else ()

        def merged_tiles(p):
            c, r = p // GW - 1, p % GW
            return [4 * c + 2 * (r - 1), 4 * c + 2 * (r - 1) + 1] if r in (1, 2) and c >= 0 else []

        @block.sync
        def _(sp):
            for t in range(T):
                sp.dma_start(X[:, t], rows(x_in)[:, t]).then_inc(x_first[t], 16)
            stream = w_stream.rearrange("g p (k n) -> g p k n", k=GK)

            def load(g, g_index, slot):
                sp.dma_start(RAW[:, slot], stream[g_index].rearrange("g p k n -> (g p) k n")).then_inc(raw_landed[slot], 16)

            for g in range(RING):
                load(g, ds(g, 1), g)
            with sp.Fori(1, GROUPS // RING) as r:
                for s in range(RING):
                    sp.wait_ge(lo_split, r * RING + (s + 1 - RING))
                    load(None, ds(r * RING + s, 1), s)
            for g in range(GROUPS // RING * RING, GROUPS):
                sp.wait_ge(lo_split, g + 1 - RING)
                load(g, ds(g, 1), g % RING)

        @block.gpsimd
        def _(pool):
            def hold(sem, value):
                pool.wait_ge(sem, value)
                pool.sem_inc(pool_held, 1)

            ch = Chain(hold, pool_chain)
            link = ch.link

            def rstd(n, ready, done_sem, value, ms=MS):
                hold(ready, value)
                link(pool.tensor_tensor(ms[:, 0:n], ms[:, 0:n], con("eps")[:, 0:n], ALU.add))
                ins = pool.tensor_tensor(ms[:, 0:n], ms[:, 0:n], con("half")[:, 0:n], ALU.pow)
                if done_sem is None:
                    link(ins)
                else:
                    ins.then_inc(done_sem, 1)

            def rotate(x1, x2, cos, sin, t1, t2, last_sem):
                link(pool.tensor_tensor(t1, x2, sin, ALU.mult))
                link(pool.tensor_tensor(t2, x1, sin, ALU.mult))
                link(pool.tensor_tensor(x1, x1, cos, ALU.mult))
                link(pool.tensor_tensor(x2, x2, cos, ALU.mult))
                link(pool.tensor_tensor(x1, x1, t1, ALU.subtract))
                pool.tensor_tensor(x2, x2, t2, ALU.add).then_inc(last_sem, 1)

            hold(con_loaded, 16)
            rstd(2, norm_ms, norm_rstd, 1)

            hold(tables_loaded, 16)
            hold(prod_free, 2 + 6)
            with pool.Fori(0, 8) as h:
                ch.enter(h, 7)
                H = At(MOBA0, h, 1)
                hold(qk_tr, H.count(1))
                link(pool.tensor_copy(QK[:, 0, :, 0:P], MQKV[:, :, ds(h * P, P)]))
                link(pool.tensor_copy(QK[:, 1, :, 0:P], MQKV[:, :, ds(h * P + W, P)]))
                v = JK[:, 0:128].rearrange("p (z a t d) -> p z a t d", z=2, a=2, t=T)
                tab = [con(n).rearrange("p (a t d) -> p a t d", a=2, t=T) for n in ("mcos", "msin")]
                rotate(QK[:, :, :, 0:16], QK[:, :, :, 16:32], tab[0], tab[1], v[:, 0], v[:, 1], qk_fixed)
            ch.leave(8)

            hold(prod_free, 2 + 6 + 8)
            cos = con("rcos").rearrange("p (t d) -> p t d", t=T)
            sin = con("rsin").rearrange("p (t d) -> p t d", t=T)
            tmp = JK[:, 0:256].rearrange("p (t d) -> p t d", t=T)
            with pool.Fori(0, 4) as h:
                ch.enter(h, 2 * 5 + 1 + 1)
                H = At(RET0, h, 1)
                hold(qk_tr, H.count(1))
                for a in range(2):
                    x1 = PA[:, :, ds(h * 256 + a * W, P)]
                    x2 = PA[:, :, ds(h * 256 + (a * W + P), P)]
                    y1, y2 = QK[:, a, :, 0:P], QK[:, a, :, P:256]
                    link(pool.tensor_tensor(y1, x1, cos, ALU.mult))
                    link(pool.tensor_tensor(tmp, x2, sin, ALU.mult))
                    link(pool.tensor_tensor(y1, y1, tmp, ALU.subtract))
                    link(pool.tensor_tensor(y2, x2, cos, ALU.mult))
                    link(pool.tensor_tensor(tmp, x1, sin, ALU.mult))
                    ins = pool.tensor_tensor(y2, y2, tmp, ALU.add)
                    if a:
                        ins.then_inc(qk_fixed, 1)
                    else:
                        link(ins)
                hold(o_ms, At(0, h, 1).count(1))
                link(pool.tensor_tensor(MS[:, 0:2], MS[:, 0:2], con("eps")[:, 0:2], ALU.add))
                pool.tensor_tensor(MS[:, 0:2], MS[:, 0:2], con("half")[:, 0:2], ALU.pow).then_inc(o_rstd, 1)
            ch.leave(4)

            hold(head_out, RET0 + 4 + 1)
            hold(pos_loaded, 32)
            with pool.Fori(0, NCH) as i:
                for seg in range(3):
                    hold(dist_used, At(seg + 1, i, 3).count())
                    q = POSB[:, ds(i * 8 + (32 if seg else 0), 8)].unsqueeze(2).broadcast_to([P, 8, P])
                    k = POSB[:, 64 + (P if seg == 2 else 0):64 + (P if seg == 2 else 0) + P].unsqueeze(1).broadcast_to([P, 8, P])
                    pool.tensor_tensor(DI[:], q, k, ALU.subtract).then_inc(dist_ready, 1)

            rstd(2, norm_ms, norm_rstd, 2)
            rstd(2, norm_ms, norm_rstd, 3)
            rstd(2, norm_ms, norm_rstd, 4)
            rstd(2, norm_ms, norm_rstd, 5, MST[:, 0, 0])

            hold(x_stored, 16 * NCH)
            hold(prod_free, 2 + PROD0["a_proj"])
            with pool.Fori(0, 4) as h:
                ch.enter(h, 3)
                hold(qk_tr, At(C0, h, 1).count(1))
                link(pool.tensor_copy(QK[:, 0], PB[:, :, ds(h * 256, 256)]))
                pool.tensor_copy(QK[:, 1], CKV[:, :, ds(h * 256, 256)]).then_inc(qk_raw, 1)
                rstd(4, qk_ms, None, At(0, h, 1).count(1))
                f = QK[:].rearrange("p a t d -> p (a t) d")
                pool.tensor_tensor(f, f, MS[:, 0:4].unsqueeze(2).broadcast_to([P, 4, 256]), ALU.mult).then_inc(qk_fixed, 1)
            ch.leave(4)

            hold(prod_free, 2 + PROD0["b_proj"])
            hold(head_out, C0 + 4 + 1)
            link(pool.tensor_copy(QK[:, 1, :, 0:64], PAC[:, 7, :, IK]))
            pool.tensor_copy(QK[:, 1, :, 64:P], PAC[:, 7, :, IK]).then_inc(idx_fixed, 1)
            with pool.Fori(0, 2) as i:
                for p in range(4):
                    hold(idx_tr, At(2 + p, i, 4).count())
                    src = PAC[:, ds(i + 5, 1), :, p * P:(p + 1) * P].rearrange("p a t d -> p (a t) d")
                    pool.tensor_copy(QK[:, 0, :, 0:P], src).then_inc(idx_fixed, 1)

            def inverse_roots(ms):
                eps, half = [con(n)[:, 0:ms.shape[1] * ms.shape[2]].rearrange("p (t h) -> p t h", t=ms.shape[1])
                             for n in ("eps", "half")]
                link(pool.tensor_tensor(ms, ms, eps, ALU.add))
                link(pool.tensor_tensor(ms, ms, half, ALU.pow))

            hold(lat_ms, 1)
            link(pool.tensor_tensor(MS[:, 0:4], MS[:, 0:4], con("eps")[:, 0:4], ALU.add))
            pool.tensor_tensor(MS[:, 0:4], MS[:, 0:4], con("half")[:, 0:4], ALU.pow).then_inc(lat_rstd, 1)

            hold(a_ms, 1)
            inverse_roots(MST[:, 0])
            inverse_roots(MST[:, 1, :, 0:2])
            hold(sel_ready, 2)
            with pool.Fori(0, 2) as kv:
                for r in range(4):
                    hold(qk_tr, At(A0 + r, kv, 4).count(1))
                    q = PAC[:, ds(kv, 1), :, r * P:(r + 1) * P].rearrange("p a t d -> p (a t) d")
                    if r == 0:
                        pool.tensor_tensor(QK[:, 1, :, 0:P], PAC[:, 2, :, ds(kv * P, P)],
                                           MST[:, 1, :, ds(kv, 1)].broadcast_to([P, T, P]), ALU.mult)
                    pool.tensor_tensor(QK[:, 0, :, 0:P], q, MST[:, 0, :, ds(kv * 4 + r, 1)].broadcast_to([P, T, P]),
                                       ALU.mult).then_inc(qk_fixed, 1)

            hold(b_ms, 1)
            hold(rope_ready, 1)
            link(pool.tensor_tensor(MST[:, 1], MST[:, 1], MS[:, 4:6].unsqueeze(2).broadcast_to([P, T, 8]), ALU.add))
            inverse_roots(MST[:, 0])
            inverse_roots(MST[:, 1])
            with pool.Fori(0, 8) as h:
                ch.enter(h, 1 + 1 + 5)
                hold(qk_tr, At(B0, h, 1).count(1))
                q_rms, k_rms = MST[:, 0, :, ds(h, 1)], MST[:, 1, :, ds(h, 1)]
                pool.tensor_tensor(QK[:, 0, :, 0:192], QB[:, :, ds(h * 192, 192)], q_rms.broadcast_to([P, T, 192]), ALU.mult)
                pool.tensor_tensor(QK[:, 1, :, 0:P], KVB[:, :, ds(h * 256, P)], k_rms.broadcast_to([P, T, P]), ALU.mult)
                link(pool.tensor_tensor(QK[:, 1, :, P:192], PB[:, :, PB_KPE], k_rms.broadcast_to([P, T, 64]), ALU.mult))
                f = QK[:, :, :, P:192]
                gains = par("brope", 0, 128).rearrange("p (a d) -> p a d", a=2).unsqueeze(2).broadcast_to([P, 2, T, 64])
                link(pool.tensor_tensor(f, f, gains, ALU.mult))
                t = JK[:, 0:256].rearrange("p (z a t d) -> p z a t d", z=2, a=2, t=T)
                rotate(QK[:, :, :, P:P + 32], QK[:, :, :, P + 32:P + 64], ROPE[:, 0], ROPE[:, 1], t[:, 0], t[:, 1], qk_fixed)
            ch.leave(8)

        @block.tensor
        def _(pe):
            def group(g, j, body):
                pe.wait_ge(lo_split, g.count(j + 1))
                body(g.slot(j)).then_inc(group_used, 1)

            def rows_product(g, n, j, q, nq, left):
                pair = 2 * (n % 2)

                def body(slot):
                    for kk in range(GK):
                        k = q * GK + kk
                        for t in range(T):
                            hi, lo = left[:, k, 0, t * P:(t + 1) * P], left[:, k, 1, t * P:(t + 1) * P]
                            o = PS[:, pair + t, :]
                            pe.matmul(o, hi, WH[:, slot, kk, :], start=k == 0, stop=False)
                            pe.matmul(o, hi, WL[:, slot, kk, :], start=False, stop=False)
                            ins = pe.matmul(o, lo, WH[:, slot, kk, :], start=False, stop=k == nq * GK - 1)
                    return ins
                group(g, j, body)

            def product(g, n, j, nq, left, steps=None, before=None):
                pe.wait_ge(prod_free, n.count(1))
                for q in range(nq):
                    if before:
                        before(j + q)
                    rows_product(g, n.base, j + q, q, nq, left)
                    if steps:
                        steps(j + q)

            def products(name, parts, i, steps=None, before=None):
                per = sum(nq for nq, _ in parts)
                j = 0
                for m, (nq, left) in enumerate(parts):
                    g, n = At(GROUP0[name], i, per), At(PROD0[name] + m, i, len(parts))
                    product(g, n, j, nq, left, (lambda p: steps(i, p)) if steps else None, before)
                    j += nq

            def product_loop(name, iters, parts, steps=None, first=0):
                with pe.Fori(first, iters) as i:
                    products(name, parts, i, steps)

            def straight(name, count, nq, left, steps=None, before=None):
                for m in range(count):
                    product(At(GROUP0[name]), At(PROD0[name] + m), m * nq, nq, left, steps, before)

            def transposes(name, src, ks):
                for k in ks:
                    at = TR[name] + k
                    if at >= 4:
                        pe.wait_ge(tr_lo, at - 3)
                    for t in range(T):
                        ins = pe.transpose(PS[:, 4 + at % 4, t * P:(t + 1) * P], src[:, t, k * P:(k + 1) * P], ident)
                    ins.then_inc(tr_done, 1)

            def as_it_arrives(name, src, rows_before):
                def before(q):
                    if q in (0, 3):
                        pe.wait_ge(norm_rows, rows_before + (2 if q else 1))
                    transposes(name, src, pairs_ahead(q))
                    pe.wait_ge(tr_lo, TR[name] + 2 * q + 2)
                return before

            def head_transpose(br, H, parts):
                pe.wait_ge(qk_fixed, H.count(1))
                pe.wait_ge(head_out, H.count(1))
                for a in range(parts):
                    for c, n in enumerate(br["d"]):
                        for t in range(T):
                            ins = pe.transpose(PS[0:n, 4 + a, c * S + t * P:c * S + (t + 1) * P],
                                               QK[:, a, t, c * P:c * P + n], ident)
                ins.then_inc(qk_tr, 1)

            def head_scores(br, H):
                pe.wait_ge(qkt_ready, H.count(1))
                last = len(br["d"]) - 1
                if br is RET:
                    for s, cols in enumerate((slice(0, S), slice(S, CAUS))):
                        for c in range(2):
                            ins = pe.matmul(PS[:, 6, cols], QKT[:, 1, c, s * P:(s + 1) * P], QKT[:, 0, c, s * P:S],
                                            start=c == 0, stop=c == last)
                    ins.then_inc(scores, 1)
                    pe.sem_inc(pt_done, 1)
                    return
                col = 0
                for t in range(T):
                    keys = (t + 1) * P if br["causal"] else S
                    for c, n in enumerate(br["d"]):
                        ins = pe.matmul(PS[:, 6, col:col + keys], QKT[0:n, 0, c, t * P:(t + 1) * P],
                                        QKT[0:n, 1, c, 0:keys], start=c == 0, stop=c == last)
                    col += keys
                ins.then_inc(scores, 1)

            def head_probs(br, H):
                pe.wait_ge(probs, H.count(1))
                for b in range(3 if br["causal"] else 4):
                    ins = pe.transpose(PS[:, 7, b * P:(b + 1) * P], PR[:, b * P:(b + 1) * P], ident)
                ins.then_inc(pt_done, 1)

            def head_values(br, H, v):
                pe.wait_ge(pt_ready, H.count(1))
                dv = br["dv"]
                blocks = ([[0], [1, 2]] if br["causal"] else [[0, 1], [2, 3]])
                for t in range(T):
                    for s, b in enumerate(blocks[t]):
                        ins = pe.matmul(PS[:, 4, t * dv:(t + 1) * dv], PT[:, b * P:(b + 1) * P], v(s),
                                        start=s == 0, stop=s == len(blocks[t]) - 1)
                ins.then_inc(pv_done, 1)

            def head_output(br, H):
                pe.wait_ge(o_rows, H.count(1))
                for c in range(br["dv"] // P):
                    for t in range(T):
                        ins = pe.transpose(PS[:, 5, c * S + t * P:c * S + (t + 1) * P], OF[:, t, c * P:(c + 1) * P], ident)
                ins.then_inc(ot_done, 1)

            def head_steps(br, H, v, at=(0, 1, 3, 4, 6), parts=2):
                return dict(zip(at, (lambda: head_transpose(br, H, parts), lambda: head_scores(br, H), lambda: head_probs(br, H),
                                     lambda: head_values(br, H, v), lambda: head_output(br, H))))

            pe.wait_ge(con_loaded, 16)
            pe.sem_inc(qk_tr, 1)
            pe.sem_inc(idx_tr, 1)
            pe.sem_inc(bias_done, 2)
            arriving = as_it_arrives("h1", ROWS, 0)
            products("moba_proj", [(GD, HT)] * 2, 0, None, lambda p: arriving(p) if p < GD else None)
            product_loop("moba_proj", 3, [(GD, HT)] * 2, first=1)

            def moba_step(i, p):
                for r in range(2):
                    h = i * 2 + r
                    st = head_steps(MOBA, At(MOBA0 + r, i, 2), lambda s: MQKV[:, s, ds(h * P + 2 * W, P)], (2, 3, 5, 6, 7))
                    if p - 8 * r in st:
                        st[p - 8 * r]()
            product_loop("ret_proj", 4, [(GD, HT)] * 2, moba_step)

            def ret_step(i, p):
                st = head_steps(RET, At(RET0, i, 1), lambda s: PA[:, s, ds(i * 256 + 2 * W, 256)], (4, 5, None, 7, 10))
                if p in st:
                    st[p]()
            product_loop("merge_moba", NCH, [(GD, HT), (GW, U[1])], ret_step)

            def bias_step(i, p):
                if p not in BIAS_AT:
                    return
                k = At(BIAS_AT.index(p), i, len(BIAS_AT))
                pe.wait_ge(onehot, k.count(1))
                pe.wait_ge(bias_copied, k.count(1))
                for b in range(2):
                    for part in range(2):
                        ins = pe.matmul(PS[0:32, 4 + b, :], REL[:, part, :],
                                        OH[:, k.base % 2, 4 * b:4 * b + 4, :].rearrange("p q s -> p (q s)"), start=part == 0, stop=part == 1)
                ins.then_inc(bias_done, 1)
            pe.wait_ge(rel_lo, 1)
            product_loop("gates_ret", 2, [(GD, HT)] * 2, bias_step)
            pe.wait_ge(head_out, RET0 + 4 + 1)
            pe.wait_ge(bias_copied, NBIAS + 1)

            def up_steps(name, chunks_before):
                def steps(p):
                    if merged_tiles(p):
                        pe.wait_ge(merged_ready, chunks_before + p // GW)
                        transposes(name, MERGED[name], merged_tiles(p))
                return steps

            def out_steps(name, chunks_before):
                def steps(p):
                    if p in (1, 2):
                        pe.wait_ge(merged_ready, chunks_before + NCH)
                        transposes(name, MERGED[name], merged_tiles(NCH * GW + p))

                def before(p):
                    if p in (0, 6):
                        pe.wait_ge(tr_lo, TR[name] + (12 if p == 0 else KT))
                return steps, before
            straight("up_ret", NCH, GW, U[0], up_steps("merged1", 0))
            steps, before = out_steps("merged1", 0)

            def mem0_steps(p):
                if p >= 4:
                    pe.wait_ge(norm_rows, 4)
                    transposes("h2", ROWS, [2 * p - 8, 2 * p - 7])

            def out1_steps(p):
                steps(p)
                if 4 <= p < 4 + KT:
                    pe.wait_ge(norm_rows, 3)
                    transposes("mem", MEMR, [p - 4])
            straight("out1", NCH, GD, HT, out1_steps, before)
            pe.wait_ge(tr_lo, TR["mem"] + KT)
            straight("mem0", 1, GD, MEMT, mem0_steps)

            def ffn_up(g, u, j, before=None):
                half = 4 * (u.base % 2)
                pe.wait_ge(ffn_free, u.count(1))
                for q in range(GD):
                    if before:
                        before(q)

                    def body(slot):
                        for kk in range(GK):
                            k = q * GK + kk
                            for f in range(FT):
                                pe.matmul(PS[:, half + f, :], WH[:, slot, kk, f * P:(f + 1) * P], HT[:, k, :, :],
                                          start=k == 0, stop=False, skip_group_check=True)
                                ins = pe.matmul(PS[:, half + f, 0:S], WL[:, slot, kk, f * P:(f + 1) * P], HT[:, k, 0, :],
                                                start=False, stop=k == KT - 1, skip_group_check=True)
                        return ins
                    group(g, j + q, body)

            def ffn_down(g, u, j, blk, products_before=None):
                for c in range(NCH):
                    v = At(u.base + c // 2, u.i, u.per)
                    if c % 2 == 0:
                        pe.wait_ge(ffn_free, v.count(1))
                    if c == 0:
                        pe.wait_ge(ffn_lo, blk.count(1))
                    if c == 1 and products_before:
                        pe.wait_ge(prod_free, 2 + products_before)
                    for q in range(2):
                        def body(slot):
                            for kk in range(GK):
                                k = q * GK + kk
                                for t in range(T):
                                    hi, lo = ACTT[:, k, 0, t * P:(t + 1) * P], ACTT[:, k, 1, t * P:(t + 1) * P]
                                    o = PS[:, 4 * (v.base % 2) + 2 * (c % 2) + t, :]
                                    pe.matmul(o, hi, WH[:, slot, kk, :], start=k == 0, stop=False)
                                    pe.matmul(o, hi, WL[:, slot, kk, :], start=False, stop=False)
                                    ins = pe.matmul(o, lo, WH[:, slot, kk, :], start=False, stop=k == FT - 1)
                            return ins
                        group(g, j + 2 * c + q, body)

            g0 = GROUP0["ffn"]

            def h2_rest(q):
                if q < 4:
                    pe.wait_ge(norm_rows, 5)
                    transposes("h2", ROWS, [8 + 2 * q, 9 + 2 * q])
                pe.wait_ge(tr_lo, TR["h2"] + 2 * q + 2)
            pe.wait_ge(prod_free, 2 + PROD0["mem1"])
            ffn_up(At(g0), At(0), 0, h2_rest)
            ffn_up(At(g0), At(1), GD)
            with pe.Fori(0, FB - 1) as b:
                g = At(g0 + 2 * GD, b, 3 * GD)
                ffn_up(g, At(2, b, 4), 0)
                ffn_up(g, At(3, b, 4), GD)
                ffn_down(g, At(4, b, 4), 2 * GD, At(0, b, 1))
            pe.wait_ge(ffn_free, 4 * FB - 1)
            straight("mem1", 1, GD, MEMT)
            ffn_down(At(GROUP0["ffn_down"]), At(4 * FB - 2), 0, At(FB - 1), PROD0["mem2"])
            pe.wait_ge(ffn_free, 2 + 4 * FB - 1)

            def h3_steps(p):
                if p == 9:
                    pe.wait_ge(norm_rows, 7)
                transposes("h3", ROWS, h3_tiles(p))
            straight("mem2", 2, GD, MEMT, h3_steps)
            pe.wait_ge(tr_lo, TR["h3"] + KT)
            product_loop("c_proj", 2, [(GD, HT)] * 2)

            def c_step(i, p):
                st = head_steps(CMEM, At(C0, i, 1), lambda s: CKV[:, s, ds(i * 256 + W, 256)], (4, 6, 9, 11, 14))
                if p in st:
                    st[p]()
            product_loop("a_proj", 4, [(GD, HT)] * 2, c_step)

            def index_step(_, p):
                if p == 0:
                    pe.wait_ge(idx_fixed, 1)
                    for t in range(T):
                        ins = pe.transpose(PS[:, 5, t * P:(t + 1) * P], QK[:, 1, t, 0:P], ident)
                    ins.then_inc(idx_tr, 1)
                elif p % 2 and p // 2 < PAIRS:
                    pe.wait_ge(idx_fixed, p // 2 + 2)
                    for t in range(T):
                        ins = pe.transpose(PS[:, 4, t * P:(t + 1) * P], QK[:, 0, t, 0:P], ident)
                    ins.then_inc(idx_tr, 1)
                elif p % 2 == 0 and p // 2 <= PAIRS:
                    k = p // 2 - 1
                    pe.wait_ge(idx_ready, k + 2)
                    pe.wait_ge(idx_relu, k + 1)
                    for j in range(2):
                        q = slice(64 * j, 64 * j + 64)
                        pe.matmul(PS[:, 6 + j, 0:P], QKT[q, 0, 0, 0:P], QKT[q, 1, 0, 0:P], start=True, stop=True)
                        ins = pe.matmul(PS[:, 6 + j, P:CAUS], QKT[q, 0, 0, P:S], QKT[q, 1, 0, :], start=True, stop=True)
                    ins.then_inc(idx_dots, 1)
            products("b_proj", [(GD, HT)] * 3, 0, index_step)

            def latent_tiles(_, p):
                if 4 <= p < 7:
                    pe.wait_ge(lat_rows, 1)
                    transposes("lat", PB, [2 * p - 8, 2 * p - 7])

            def a_step(i, p):
                r = p // 6
                st = head_steps(ASP, At(A0 + r, i, 4), lambda s: PAC[:, 2, s, ds(i * P + 256, P)], (0, 1, 3, 4, 5),
                                1 if r else 2)
                if p - 6 * r in st:
                    st[p - 6 * r]()
            products("gates_b0", [(GD, HT)], 0, latent_tiles)
            pe.wait_ge(tr_lo, TR["lat"] + 6)
            product_loop("merge_c", 2, [(GD, HT), (GW, U[0])] * 2, a_step)
            g0, n0 = GROUP0["b_up"], PROD0["b_up"]
            for c in range(3):
                product(At(g0), At(n0 + c), 2 * c, 2, LATT)
            for c in range(4):
                product(At(g0), At(n0 + 3 + c), 6 + c, 1, LATT[:, 4:6])

            def b_step(i, p):
                r = p // 6
                h = i * 2 + r
                st = head_steps(BLA, At(B0 + r, i, 2), lambda s: KVB[:, s, ds(h * 256 + P, P)], (0, 1, 3, 4, 5))
                if p - 6 * r in st:
                    st[p - 6 * r]()
            products("gates_b1", [(GD, HT)], 0)
            product_loop("merge_a", NCH, [(GD, HT), (GW, U[1])], b_step)
            products("gates_b", [(GD, HT)] * 2, 0)
            pe.wait_ge(head_out, HEADS + 1)
            straight("up_b", NCH, GW, U[2], up_steps("merged2", NCH))
            steps, before = out_steps("merged2", NCH)
            straight("out2", NCH, GD, HT, steps, before)

        @block.scalar
        def _(act):
            ch = Chain(act.wait_ge, act_chain)
            link = ch.link

            def split(g, j):
                act.wait_ge(raw_landed[g.slot(j)], g.turn(j) * 16 + 16)
                if g.per or g.base + j >= RING:
                    act.wait_ge(group_used, g.count(j + 1 - RING))
                act.activation(WH[:, g.slot(j)], RAW[:, g.slot(j)], ACT.Copy).then_inc(hi_split, 1)

            def evacuate(n, end, dst):
                act.wait_ge(group_used, end)
                pair = 2 * (n.base % 2)
                act.activation(dst, PS[:, pair:pair + 2, :], ACT.Copy).then_inc(prod_free, 1)

            def evacuations(name, g, i, p, per_iter, dst, func=ACT.Copy):
                if p % GD == GD - 1:
                    c = p // GD
                    n = At(PROD0[name] + c, i, per_iter)
                    act.wait_ge(group_used, g.count(p + 1))
                    pair = 2 * (n.base % 2)
                    act.activation(dst(i * (per_iter * CH) + c * CH if n.per else c * CH), PS[:, pair:pair + 2, :],
                                   func).then_inc(prod_free, 1)

            def project(name, iters, dst, steps=None, links=0, first=0, func=ACT.Copy):
                with act.Fori(first, iters) as i:
                    ch.enter(i, links)
                    g = At(GROUP0[name], i, 2 * GD)
                    for p in range(2 * GD):
                        split(g, p + RING)
                        evacuations(name, g, i, p, 2, dst, func)
                        if steps:
                            steps(i, p)
                ch.leave(iters - first)

            def mean_squares(pairs, scale, done, junk=None):
                for n, (src, acc) in enumerate(pairs):
                    o = junk if junk is not None else PS[:, 4:8, :].rearrange("p b n -> p (b n)")
                    ins = act.activation(o, src, ACT.Square, scale=scale, accum_out=acc)
                    if n + 1 < len(pairs):
                        link(ins)
                ins.then_inc(done, 1)

            def transposed(name, dst, ks, gain):
                for k in ks:
                    at = TR[name] + k
                    act.wait_ge(tr_done, at + 1)
                    act.activation(dst[:, k, 0, :], PS[:, 4 + at % 4, 0:S], ACT.Copy,
                                   scale=par(gain, k) if gain else 1.0).then_inc(tr_hi, 1)

            def head_transpose(br, H, gains, parts=2):
                act.wait_ge(qk_tr, H.count(2))
                for a in range(parts):
                    whole = len(set(br["d"])) == 1 and not gains
                    for c, n in enumerate([P] if whole else br["d"]):
                        w = S * len(br["d"]) if whole else S
                        dst = QKT[:, a].rearrange("p c s -> p (c s)")[0:n, c * S:c * S + w]
                        ins = act.activation(dst, PS[0:n, 4 + a, c * S:c * S + w], ACT.Copy,
                                             scale=par(gains[a], c) if gains and c < PAR[gains[a]][1] else 1.0)
                ins.then_inc(qkt_ready, 1)

            def head_exp(br, H, M):
                act.wait_ge(maxima, M.count(1))
                cut = P if br["causal"] else S
                end = CAUS if br["causal"] else 2 * S
                act.activation(PR[:, 0:cut], SC[:, 0:cut], ACT.Exp, bias=NM[:, 0:1], accum_out=RS[:, 0:1])
                act.activation(PR[:, cut:end], SC[:, cut:end], ACT.Exp, bias=NM[:, 1:2], accum_out=RS[:, 1:2]).then_inc(probs, 1)

            def head_probs(br, H):
                act.wait_ge(pt_done, H.count(1))
                n = CAUS if br["causal"] else 512
                act.activation(PT[:, 0:n], PS[:, 7, 0:n], ACT.Copy).then_inc(pt_ready, 1)

            def head_output(br, H, h):
                act.wait_ge(ot_done, H.count(1))
                nd = br["dv"] // P
                for c in range(nd):
                    dst = U[br["u"]][:, ds(h * nd + c, 1), 0, :]
                    ins = act.activation(dst, PS[:, 5:6, c * S:(c + 1) * S], ACT.Copy,
                                         scale=par("ret", h * nd + c) if br is RET else 1.0)
                ins.then_inc(ot_hi, 1)

            def head_squares(br, N):
                act.wait_ge(qk_raw, N.count(1))
                d = sum(br["d"])
                mean_squares([(QK[:, a, t, 0:d], MS[:, 2 * a + t:2 * a + t + 1]) for a in range(2) for t in range(T)],
                             float(d) ** -0.5, qk_ms, JK[:, 0:d])

            def head_steps(br, H, M, h, gains=None, at=(0, 1, 3, 6), parts=2):
                return dict(zip(at, (lambda: head_transpose(br, H, gains, parts), lambda: head_exp(br, H, M),
                                     lambda: head_probs(br, H), lambda: head_output(br, H, h))))

            act.dma_start(CONST[:, 0:NFIRST], constants[:, 0:NFIRST]).then_inc(con_loaded, 16)
            act.dma_start(PARAM[:], params).then_inc(par_loaded, 16)
            act.sem_inc(prod_free, 2)
            act.sem_inc(bias_copied, 1)
            act.sem_inc(bias_stored, 16)
            act.sem_inc(idx_relu, 1)

            for t in range(T):
                act.wait_ge(x_first[t], 16)
                ins = act.activation(PS[:, 4 * t:4 * t + 4, :].rearrange("p b n -> p (b n)"), X[:, t, :], ACT.Square,
                                     scale=D ** -0.5, accum_out=MS[:, t:t + 1])
            ins.then_inc(norm_ms, 1)
            act.dma_start(CONST[:, NFIRST:NCON], constants[:, NFIRST:NCON]).then_inc(tables_loaded, 16)
            act.dma_start(POSI[:], pos_pack[:, POSN:POSN + 2]).then_inc(pos_loaded, 16)
            act.dma_start(DECAY[:].rearrange("p h n -> p (h n)"), constants[:, NCON:]).then_inc(decay_loaded, 16)
            act.wait_ge(par_loaded, 16)
            split(At(0), 0)
            transposed("h1", HT, pairs_ahead(0), "attn")
            for j in range(1, RING):
                split(At(0), j)
            g = At(GROUP0["moba_proj"])
            for p in range(2 * GD):
                if 0 < p < GD:
                    transposed("h1", HT, pairs_ahead(p), "attn")
                split(g, p + RING)
                evacuations("moba_proj", g, 0, p, 2, lambda c: MQKV[:, :, ds(c, CH)])
            act.activation(REL[:, 0, :], par("rel", 0, 32), ACT.Copy).then_inc(rel_hi, 1)

            act.wait_ge(ang_ready, 1)
            act.wait_ge(tables_loaded, 16)
            for a in range(2):
                act.activation(ROPE[:, 1, a], ANG[:, 0], ACT.Sin)
                ins = act.activation(ROPE[:, 0, a], ANG[:, 1], ACT.Sin, scale=-1.0, bias=con("hpi"))
            ins.then_inc(rope_ready, 1)

            project("moba_proj", 3, lambda c: MQKV[:, :, ds(c, CH)], first=1)

            def moba_step(i, p):
                for r in range(2):
                    st = head_steps(MOBA, At(MOBA0 + r, i, 2), At(r, i, 2), i * 2 + r, None, (2, 3, 5, 7))
                    if p - 8 * r in st:
                        st[p - 8 * r]()
            project("ret_proj", 4, lambda c: PA[:, :, ds(c, CH)], moba_step)

            act.wait_ge(prod_free, 2 + PROD0["merge_moba"])
            act.activation(PA[:, :, 3 * W:4 * W], PA[:, :, 3 * W:4 * W], ACT.Silu).then_inc(gate_ready, 1)

            def merge(name, iters, chunks, links=0, steps=None):
                per = chunks * (GD + GW)
                with act.Fori(0, iters) as i:
                    ch.enter(i, links)
                    g = At(GROUP0[name], i, per)
                    for p in range(per):
                        split(g, p + RING)
                        if steps:
                            steps(i, p)
                        b, r = p // (GD + GW), p % (GD + GW)
                        if r == GD - 1:
                            n = At(PROD0[name] + 2 * b, i, 2 * chunks)
                            act.wait_ge(group_used, g.count(p + 1))
                            act.wait_ge(prod_free, n.count(2))
                            pair = 2 * (n.base % 2)
                            act.activation(SG[name][:], PS[:, pair:pair + 2, :], ACT.Sigmoid).then_inc(prod_free, 1)
                ch.leave(iters)

            def ret_step(i, p):
                H = At(RET0, i, 1)
                if p == 4:
                    head_transpose(RET, H, None)
                elif p == 7:
                    act.wait_ge(pv_done, H.count(1))
                    mean_squares([(PS[:, 4, t * 256:(t + 1) * 256], MS[:, t:t + 1]) for t in range(T)], 1 / 16.0, o_ms, JK[:])
                elif p == 10:
                    head_output(RET, H, i)
            act.wait_ge(head_out, RET0 + 1)
            act.dma_start(POSB[:], pos_pack[:, 0:POSN]).then_inc(pos_loaded, 16)
            merge("merge_moba", NCH, 1, 1, ret_step)

            def bias_step(i, p):
                if p not in BIAS_AT:
                    return
                s = BIAS_AT.index(p)
                k = At(s, i, len(BIAS_AT))
                act.wait_ge(bias_done, k.count(3))
                act.wait_ge(bias_stored, k.count(1) * 16)
                act.activation(BE[:].rearrange("p (b q) s -> p b (q s)", b=2), PS[0:32, 4:6, :], ACT.Copy).then_inc(bias_copied, 1)
                act.wait_ge(bias_copied, k.count(2))
                act.dma_start(bias_scratch[:, s % 3, ds(i * 16 + s // 3 * 8, 8), :], BE[:]).then_inc(bias_stored, 16)

            act.wait_ge(head_out, RET0 + 4 + 1)
            act.dma_start(MEMR[:], rows(mem_in)).then_inc(mem_loaded, 16)
            project("gates_ret", 2, gate_chunk, bias_step, func=ACT.Sigmoid)

            for p in range(NCH * GW):
                split(At(GROUP0["up_ret"]), p + RING)
                if p == 1:
                    act.wait_ge(bias_stored, 16 * (NBIAS + 1))
                if p % GW == 1:
                    cols = slice(p // GW * CH, (p // GW + 1) * CH)
                    act.dma_start(X[:, :, cols], rows(x_in)[:, :, cols]).then_inc(x_loaded, 16)
                transposed("merged1", HT, merged_tiles(p), None)
                if p == 3:
                    act.wait_ge(mem_loaded, 16)
                    for t in range(T):
                        ins = act.activation(JUNK[:, t, :], MEMR[:, t, :], ACT.Square, scale=D ** -0.5, accum_out=MS[:, t:t + 1])
                    ins.then_inc(norm_ms, 1)

            def chunk_squares(c):
                act.wait_ge(prod_free, 2 + PROD0["out1"] + c + 1)
                if c == 0:
                    act.wait_ge(norm_ms, 2)
                for t in range(T):
                    ins = act.activation(JUNK[:, t, c * CH:(c + 1) * CH], X[:, t, c * CH:(c + 1) * CH], ACT.Square,
                                         scale=D ** -0.5, accum_out=MSC[:, t, c:c + 1])
                return ins
            for p in range(NCH * GD):
                split(At(GROUP0["out1"]), p + RING)
                if p in (1, 2):
                    transposed("merged1", HT, merged_tiles(NCH * GW + p), None)
                if p == 3:
                    act.dma_start(FINALW[:], final_w.partition_broadcast(P)).then_inc(fw_loaded, 16)
                if 4 <= p < 4 + KT:
                    transposed("mem", MEMT, [p - 4], "mem")
                if p % GD == 1 and p > GD:
                    chunk_squares(p // GD - 1)
            for p in range(GD):
                g = At(GROUP0["mem0"])
                evacuations("mem0", g, 0, p, 1, lambda c: CKV[:, :, c:c + CH])
                split(g, p + RING)
                if p == 0:
                    chunk_squares(NCH - 1).then_inc(x_sq, 1)
                if p >= 4:
                    transposed("h2", HT, [2 * p - 8, 2 * p - 7], "ffn")

            def up_copy(u, end, f, tile):
                act.wait_ge(group_used, end)
                if tile.per or tile.base >= FT:
                    act.wait_ge(ffn_sum, tile.count(1 - FT))
                act.activation(FC[:, f, :], PS[:, 4 * (u.base % 2) + f, 0:S], ACT.Copy).then_inc(ffn_copied, 1)

            def silu(tile, f, blk):
                act.wait_ge(ffn_conv, tile.count(1))
                act.activation(FA[:, f, :], FY[:, f % 2, :], ACT.Silu).then_inc(ffn_silu, 1)

            def block_hi(blk, end):
                act.wait_ge(ffn_prod, blk.count(1))
                if end is not None:
                    act.wait_ge(group_used, end)
                act.activation(ACTT[:, :, 0, :], FP[:], ACT.Copy).then_inc(ffn_hi, 1)

            g0 = GROUP0["ffn"]
            for p in range(2 * GD):
                if p < 4:
                    transposed("h2", HT, [8 + 2 * p, 9 + 2 * p], "ffn")
                split(At(g0), p + RING)
                if p == 7:
                    for f in range(FT):
                        up_copy(At(0), g0 + GD, f, At(f))
                if 9 <= p <= 12:
                    silu(At(p - 9), p - 9, None)
            for f in range(FT):
                up_copy(At(1), g0 + 2 * GD, f, At(FT + f))
            with act.Fori(0, FB - 1) as b:
                g = At(g0 + 2 * GD, b, 3 * GD)
                for p in range(3 * GD):
                    split(g, p + RING)
                    if p == 4:
                        block_hi(At(0, b, 1), g.count())
                    if p in (7, 15):
                        for f in range(FT):
                            up_copy(At(2 + p // 8, b, 4), g.count(p + 1), f, At(8 + p // 8 * FT + f, b, 8))
                    if 9 <= p <= 12:
                        silu(At(8 + p - 9, b, 8), p - 9, None)
            for p in range(GD):
                g = At(GROUP0["mem1"])
                split(g, p + RING)
                if p == FT:
                    block_hi(At(FB - 1), g.count())
                evacuations("mem1", g, 0, p, 1, lambda c: CKV[:, :, CH + c:CH + c + CH])
            for p in range(GD):
                split(At(GROUP0["ffn_down"]), p + RING)

            for p in range(2 * GD):
                g = At(GROUP0["mem2"])
                split(g, p + RING)
                if p == 0:
                    act.wait_ge(x_done, 1)
                    mean_squares([(X[:, t, :], MS[:, t:t + 1]) for t in range(T)], D ** -0.5, norm_ms)
                if p in (4, 5):
                    act.wait_ge(x_done, p - 2)
                    ins = act.activation(PS[:, 4:8, :].rearrange("p b n -> p (b n)"), X[:, p - 4, :], ACT.Square,
                                         scale=D ** -0.5, accum_out=MST[:, 0, 0, p - 4:p - 3])
                    if p == 4:
                        link(ins)
                    else:
                        ins.then_inc(norm_ms, 1)
                if p >= 8 and p % 2 == 0:
                    cols = slice((p // 2 - 4) * CH, (p // 2 - 3) * CH)
                    act.dma_start(rows(x_scratch)[:, :, cols], X[:, :, cols]).then_inc(x_stored, 16)
                transposed("h3", HT, h3_tiles(p), "norm2")
                evacuations("mem2", g, 0, p, 2, lambda c: CKV[:, :, 2 * CH + c:3 * CH + c])
            act.wait_ge(x_stored, 16 * NCH)
            project("c_proj", 2, lambda c: PB[:, :, ds(c, CH)])
            act.wait_ge(prod_free, 2 + PROD0["a_proj"])
            act.activation(PB[:, :, W:2 * W], PB[:, :, W:2 * W], ACT.Silu).then_inc(gate_ready, 1)

            def c_step(i, p):
                if p == 0:
                    head_squares(CMEM, At(0, i, 1))
                st = head_steps(CMEM, At(C0, i, 1), At(8, i, 1), i, ("cq", "ck"), (4, 6, 9, 14))
                if p in st:
                    st[p]()
            with act.Fori(0, 4) as i:
                ch.enter(i, 3)
                g = At(GROUP0["a_proj"], i, 2 * GD)
                for p in range(2 * GD):
                    split(g, p + RING)
                    if p % GD == GD - 1:
                        c = p // GD
                        dst = PAC[:, ds(i * 2 + c, 1)].rearrange("p a t n -> p (a t) n")
                        evacuate(At(PROD0["a_proj"] + c, i, 2), g.count(p + 1), dst)
                    c_step(i, p)
            ch.leave(4)

            act.wait_ge(head_out, C0 + 4 + 1)
            act.wait_ge(bias_stored, 16 * (NBIAS + 1))
            for g in range(4):
                act.dma_start(BIAS[32 * g:32 * g + 32, :, :].rearrange("p h (s k) -> p h s k", s=3),
                              bias_scratch[8 * g:8 * g + 8].rearrange("h s p k -> p h s k")).then_inc(bias_loaded, 16)

            squares = [(PAC[:, h // 4, t, h % 4 * P:(h % 4 + 1) * P], MST[:, 0, t, h:h + 1]) for h in range(8) for t in range(T)]
            squares += [(PAC[:, 2, t, h * P:(h + 1) * P], MST[:, 1, t, h:h + 1]) for h in range(2) for t in range(T)]

            def index_step(p):
                if p == 0:
                    act.wait_ge(idx_tr, 2)
                    act.activation(QKT[:, 1, 0, :], PS[:, 5, 0:S], ACT.Copy).then_inc(idx_ready, 1)
                elif p % 2 and p // 2 < PAIRS:
                    act.wait_ge(idx_tr, p // 2 + 3)
                    act.activation(QKT[:, 0, 0, :], PS[:, 4, 0:S], ACT.Copy).then_inc(idx_ready, 1)
                elif p % 2 == 0 and p // 2 <= PAIRS:
                    k = p // 2 - 1
                    act.wait_ge(idx_dots, k + 1)
                    act.wait_ge(idx_sum, k + 1)
                    act.activation(SC[:, 0:CAUS], PS[:, 6, 0:CAUS], ACT.Relu)
                    act.activation(PR[:, 0:CAUS], PS[:, 7, 0:CAUS], ACT.Relu).then_inc(idx_relu, 1)
                elif p == TOPK_AT:
                    act.activation(PAC[:, 3:5], PAC[:, 3:5], ACT.Silu).then_inc(gate_ready, 1)
                elif p > TOPK_AT:
                    for src, acc in squares[4 * (p - TOPK_AT - 1):4 * (p - TOPK_AT)]:
                        link(act.activation(JK[:, 0:P], src, ACT.Square, scale=P ** -0.5, accum_out=acc))
            act.wait_ge(prod_free, 2 + PROD0["b_proj"])
            for p in range(3 * GD):
                g = At(GROUP0["b_proj"])
                split(g, p + RING)
                evacuations("b_proj", g, 0, p, 3, lambda c: PB[:, :, c + (PB_Z - CH if c else 0):c + (PB_Z if c else CH)])
                index_step(p)
            act.sem_inc(a_ms, 1)
            def gates_b(name, chunk, count, steps=None):
                for p in range(count * GD):
                    split(At(GROUP0[name]), p + RING)
                    evacuations(name, At(GROUP0[name]), 0, p, count, lambda c: gate_chunk(chunk * CH + c), ACT.Sigmoid)
                    if steps:
                        steps(p)

            def latent_squares(p):
                if p == 0:
                    act.wait_ge(prod_free, 2 + PROD0["gates_b0"])
                    for t in range(T):
                        act.activation(PS[:, 4 + 2 * t, :], PB[:, t, 0:512], ACT.Square, scale=512 ** -0.5, accum_out=MS[:, t:t + 1])
                        act.activation(PS[:, 5 + 2 * t, 0:256], PAC[:, 7, t, KV_LAT], ACT.Square, scale=1 / 16.0,
                                       accum_out=MS[:, 2 + t:3 + t])
                        ins = act.activation(PS[:, 5 + 2 * t, 256:320], PAC[:, 7, t, KPE], ACT.Square, scale=192 ** -0.5,
                                             accum_out=MS[:, 4 + t:5 + t])
                    ins.then_inc(lat_ms, 1)
                elif p == 2:
                    act.activation(PB[:, :, PB_Z:PB_Z + W], PB[:, :, PB_Z:PB_Z + W], ACT.Silu).then_inc(gate_ready, 1)
                elif 4 <= p < 7:
                    transposed("lat", LATT, [2 * p - 8, 2 * p - 7], "lat")
            gates_b("gates_b0", 0, 1, latent_squares)

            def a_step(i, p):
                r = p // 6
                st = head_steps(ASP, At(A0 + r, i, 4), At(12 + r, i, 4), i * 4 + r, ("aq", "ak"), (0, 1, 3, 5), 1 if r else 2)
                if p - 6 * r in st:
                    st[p - 6 * r]()
            merge("merge_c", 2, 2, 0, a_step)

            g0, n0 = GROUP0["b_up"], PROD0["b_up"]
            scale = 192 ** -0.5

            def square_q(c):
                act.wait_ge(prod_free, 2 + n0 + c + 1)
                cols = slice(c * CH, (c + 1) * CH)
                return act.activation(SQQ[:, :, cols], QB[:, :, cols], ACT.Square, scale=scale)

            def square_k(c):
                act.wait_ge(prod_free, 2 + n0 + 3 + c + 1)
                src = KVB[:, :, c * CH:(c + 1) * CH].rearrange("p t (h d) -> p t h d", h=2)[:, :, :, 0:P]
                return act.activation(SQK[:, :, 2 * c:2 * c + 2, :], src, ACT.Square, scale=scale)
            for p in range(10):
                split(At(g0), p + RING)
                if p == 0:
                    act.wait_ge(head_out, A0 + 8 + 1)
                    act.wait_ge(prod_free, 2 + n0)
                if p < 6 and p % 2:
                    evacuate(At(n0 + p // 2), g0 + p + 1, QB[:, :, p // 2 * CH:(p // 2 + 1) * CH])
                if p in (2, 4):
                    square_q(p // 2 - 1)
                if p >= 6:
                    evacuate(At(n0 + 3 + p - 6), g0 + p + 1, KVB[:, :, (p - 6) * CH:(p - 5) * CH])
                if p == 6:
                    square_q(2).then_inc(bq_sq, 1)
                if p > 6:
                    square_k(p - 7)
            square_k(3).then_inc(bk_sq, 1)
            gates_b("gates_b1", 1, 1)

            def b_step(i, p):
                r = p // 6
                st = head_steps(BLA, At(B0 + r, i, 2), At(20 + r, i, 2), i * 2 + r, ("bqn", "bkn"), (0, 1, 3, 5))
                if p - 6 * r in st:
                    st[p - 6 * r]()
            merge("merge_a", NCH, 1, 0, b_step)
            act.wait_ge(head_out, HEADS + 1)
            act.dma_start(X[:], rows(x_scratch)).then_inc(x_back, 16)
            gates_b("gates_b", 2, 2)
            for p in range(NCH * GW):
                split(At(GROUP0["up_b"]), p + RING)
                transposed("merged2", HT, merged_tiles(p), None)
            for p in range(NCH * GD):
                if p + RING < NCH * GD:
                    split(At(GROUP0["out2"]), p + RING)
                if p in (1, 2):
                    transposed("merged2", HT, merged_tiles(NCH * GW + p), None)
                if p % GD == GD - 1:
                    c = p // GD
                    act.wait_ge(out_ready, c + 1)
                    act.dma_start(rows(out)[:, :, c * CH:(c + 1) * CH], X[:, :, c * CH:(c + 1) * CH]).then_inc(out_stored, 16)
            act.wait_ge(out_stored, 16 * NCH)
            act.wait_ge(bias_stored, 16 * (NBIAS + 1))

        @block.vector
        def _(dve):
            ch = Chain(dve.wait_ge, dve_chain)
            link = ch.link

            def split(g, j):
                dve.wait_ge(hi_split, g.count(j + 1))
                s = g.slot(j)
                dve.tensor_tensor(WL[:, s], RAW[:, s], WH[:, s].bitcast(F32), ALU.subtract).then_inc(lo_split, 1)

            def stream(name, iters, per, steps=None, first=0):
                with dve.Fori(first, iters) as i:
                    for p in range(per):
                        split(At(GROUP0[name], i, per), p + RING)
                        if steps:
                            steps(i, p)

            def scaled_rows(dst, src, t, gain=None, cols=slice(0, D), inv=MS):
                if gain is None:
                    return dve.tensor_scalar(dst[:, t, cols], src[:, t, cols], inv[:, t:t + 1], None, ALU.mult)
                return dve.scalar_tensor_tensor(out=dst[:, t, cols], in0=src[:, t, cols], scalar=MS[:, t:t + 1],
                                                in1=gain, op0=ALU.mult, op1=ALU.mult)

            def rows_by_halves(n):
                dve.wait_ge(norm_rstd, n)
                for cols in (slice(0, D // 2), slice(D // 2, D)):
                    for t in range(T):
                        ins = scaled_rows(ROWS, X, t, cols=cols)
                    ins.then_inc(norm_rows, 1)

            def transposed(name, dst, ks, gain):
                for k in ks:
                    at = TR[name] + k
                    dve.wait_ge(tr_hi, at + 1)
                    hi, ps = dst[:, k, 0, :].bitcast(F32), PS[:, 4 + at % 4, 0:S]
                    if gain:
                        ins = dve.scalar_tensor_tensor(out=dst[:, k, 1, :], in0=ps, scalar=par(gain, k), in1=hi,
                                                       op0=ALU.mult, op1=ALU.subtract)
                    else:
                        ins = dve.tensor_tensor(dst[:, k, 1, :], ps, hi, ALU.subtract)
                    ins.then_inc(tr_lo, 1)

            def head_scores(br, H, M, h):
                dve.wait_ge(scores, H.count(1))
                if br is RET:
                    dve.tensor_tensor(PT[:, 0:CAUS], PS[:, 6, 0:CAUS], DECAY[:, ds(h, 1), :].rearrange("p a n -> p (a n)"),
                                      ALU.mult).then_inc(pt_ready, 1)
                    dve.sem_inc(probs, 1)
                    return
                if br["causal"]:
                    mask = BIAS[:, ds(h, 1), :].rearrange("p a n -> p (a n)") if br is ASP else con("mask")
                    link(dve.scalar_tensor_tensor(out=SC[:, 0:CAUS], in0=PS[:, 6, 0:CAUS], scalar=br["scale"], in1=mask,
                                                  op0=ALU.mult, op1=ALU.add))
                    cut, end = P, CAUS
                else:
                    link(dve.tensor_scalar(SC[:], PS[:, 6, :], br["scale"], None, ALU.mult))
                    cut, end = S, 2 * S
                dve.tensor_reduce(NM[:, 0:1], SC[:, 0:cut], AX_X, ALU.max, negate=True)
                dve.tensor_reduce(NM[:, 1:2], SC[:, cut:end], AX_X, ALU.max, negate=True).then_inc(maxima, 1)

            def head_values(br, H, gate):
                dv = br["dv"]
                if br is RET:
                    dve.wait_ge(o_rstd, At(H.base - RET0, H.i, H.per).count(1))
                    inv = MS
                else:
                    dve.wait_ge(probs, H.count(1))
                    link(dve.reciprocal(RI[:], RS[:]))
                    inv = RI
                dve.wait_ge(pv_done, H.count(1))
                for t in range(T):
                    o, ps = OF[:, t, 0:dv], PS[:, 4, t * dv:(t + 1) * dv]
                    if gate is None:
                        ins = dve.tensor_scalar(o, ps, inv[:, t:t + 1], None, ALU.mult)
                    else:
                        ins = dve.scalar_tensor_tensor(out=o, in0=ps, scalar=inv[:, t:t + 1], in1=gate(t),
                                                       op0=ALU.mult, op1=ALU.mult)
                ins.then_inc(o_rows, 1)

            def head_output(br, H, h):
                dve.wait_ge(ot_hi, H.count(1))
                nd = br["dv"] // P
                for c in range(nd):
                    u = U[br["u"]]
                    hi, lo = u[:, ds(h * nd + c, 1), 0, :].bitcast(F32), u[:, ds(h * nd + c, 1), 1, :]
                    ps = PS[:, 5:6, c * S:(c + 1) * S]
                    if br is RET:
                        ins = dve.scalar_tensor_tensor(out=lo, in0=ps, scalar=par("ret", h * nd + c), in1=hi,
                                                       op0=ALU.mult, op1=ALU.subtract)
                    else:
                        ins = dve.tensor_tensor(lo, ps, hi, ALU.subtract)
                ins.then_inc(head_out, 1)

            def head_steps(br, H, M, h, gate=None, at=(1, 4, 6)):
                return dict(zip(at, (lambda: head_scores(br, H, M, h), lambda: head_values(br, H, gate),
                                     lambda: head_output(br, H, h))))

            for s, n in ((head_out, 1), (dist_used, 1), (idx_sum, 1), (ffn_free, 2)):
                dve.sem_inc(s, n)

            rows_by_halves(1)
            dve.wait_ge(par_loaded, 16)
            split(At(0), 0)
            transposed("h1", HT, pairs_ahead(0), "attn")
            for j in range(1, RING):
                split(At(0), j)
            for p in range(2 * GD):
                if 0 < p < GD:
                    transposed("h1", HT, pairs_ahead(p), "attn")
                split(At(GROUP0["moba_proj"]), p + RING)
            dve.wait_ge(rel_hi, 1)
            dve.tensor_tensor(REL[:, 1, :], par("rel", 0, 32), REL[:, 0, :].bitcast(F32), ALU.subtract).then_inc(rel_lo, 1)

            dve.wait_ge(tables_loaded, 16)
            dve.wait_ge(pos_loaded, 16)
            posf = RI
            link(dve.tensor_copy(posf[:], POSI[:]))
            for t in range(T):
                link(dve.tensor_scalar(ANG[:, 0, t], con("freq"), posf[:, t:t + 1], None, ALU.mult))
            ang = ANG[:, 0].rearrange("p t d -> p (t d)")
            mag = ANG[:, 1].rearrange("p t d -> p (t d)")
            turns_i = ANGI[:]
            turns = JK[:, 0:T * 32]
            link(dve.tensor_scalar(turns_i, ang, float(1 / (2 * np.pi)), None, ALU.mult))
            link(dve.tensor_copy(turns, turns_i))
            for part in (6.28125, 0.0019340515136718750, 1.2556659146770e-06):
                link(dve.scalar_tensor_tensor(out=ang, in0=turns, scalar=-part, in1=ang, op0=ALU.mult, op1=ALU.add))
            link(dve.tensor_scalar(ang, ang, 3.1415925, -3.1415925, ALU.min, ALU.max))
            dve.scalar_tensor_tensor(out=mag, in0=ang, scalar=-1.0, in1=ang, op0=ALU.mult, op1=ALU.max).then_inc(ang_ready, 1)
            stream("moba_proj", 3, 2 * GD, first=1)

            with dve.Fori(0, 4) as i:
                ch.enter(i, 4)
                for p in range(2 * GD):
                    split(At(GROUP0["ret_proj"], i, 2 * GD), p + RING)
                    for r in range(2):
                        st = head_steps(MOBA, At(MOBA0 + r, i, 2), At(r, i, 2), i * 2 + r, None, (3, 6, 7))
                        if p - 8 * r in st:
                            st[p - 8 * r]()
            ch.leave(4)
            dve.wait_ge(gate_ready, 1)
            dve.wait_ge(decay_loaded, 16)

            def merge(name, iters, chunks, merged, links=0, steps=None):
                add = name == "merge_a"
                per = chunks * (GD + GW)
                with dve.Fori(0, iters) as i:
                    ch.enter(i, links)
                    g = At(GROUP0[name], i, per)
                    for p in range(per):
                        split(g, p + RING)
                        if steps:
                            steps(i, p)
                        b, r = p // (GD + GW), p % (GD + GW)
                        if r == GD + GW - 1:
                            n = At(PROD0[name] + 2 * b + 1, i, 2 * chunks)
                            dve.wait_ge(prod_free, n.count(2))
                            dve.wait_ge(group_used, g.count(p + 1))
                            ps = PS[:, 2 * (n.base % 2):2 * (n.base % 2) + 2, :]
                            m = merged[:, :, ds(i * (chunks * CH) + b * CH, CH)]
                            dve.tensor_tensor(TMP[:] if add else m, ps, SG[name][:], ALU.mult).then_inc(prod_free, 1)
                            if add:
                                dve.wait_ge(prod_free, n.count(3))
                                dve.tensor_tensor(m, m, TMP[:], ALU.add)
                ch.leave(iters)

            def ret_step(i, p):
                st = head_steps(RET, At(RET0, i, 1), None, i, lambda t: PA[:, t, ds(i * 256 + 3 * W, 256)], (5, 8, 10))
                if p in st:
                    st[p]()
            merge("merge_moba", NCH, 1, MERGED["merged1"], 0, ret_step)

            def bias_step(i, p):
                if p + 2 not in BIAS_AT:
                    return
                k = At(BIAS_AT.index(p + 2), i, len(BIAS_AT))
                dve.wait_ge(dist_ready, k.count(1))
                dve.wait_ge(bias_done, k.count(1))
                hot = OH[:, k.base % 2]
                link(dve.tensor_scalar(hot, DI[:], con("lo"), None, ALU.is_ge))
                dve.scalar_tensor_tensor(out=hot, in0=DI[:], scalar=con("hi"), in1=hot.bitcast(F32), op0=ALU.is_lt,
                                         op1=ALU.mult).then_inc(onehot, 1)
                dve.wait_ge(onehot, k.count(1))
                dve.sem_inc(dist_used, 1)
            with dve.Fori(0, 2) as i:
                ch.enter(i, len(BIAS_AT))
                for p in range(2 * GD):
                    split(At(GROUP0["gates_ret"], i, 2 * GD), p + RING)
                    bias_step(i, p)
            ch.leave(2)

            def up_chunk(name, merged, c):
                n, end = PROD0[name] + c, GROUP0[name] + (c + 1) * GW
                cols = slice(c * CH, (c + 1) * CH)
                dve.wait_ge(group_used, end)
                ps = PS[:, 2 * (n % 2):2 * (n % 2) + 2, :]
                gated = gate_chunk(c * CH)
                dve.tensor_tensor(gated, ps, gated, ALU.mult).then_inc(prod_free, 1)
                dve.wait_ge(prod_free, 2 + n + 1)
                dve.tensor_tensor(merged[:, :, cols], merged[:, :, cols], gated, ALU.add).then_inc(merged_ready, 1)

            dve.wait_ge(prod_free, 2 + PROD0["up_ret"])
            for p in range(NCH * GW):
                split(At(GROUP0["up_ret"]), p + RING)
                transposed("merged1", HT, merged_tiles(p), None)
                if p % GW == GW - 1:
                    up_chunk("up_ret", MERGED["merged1"], p // GW)
                if p in (8, 12):
                    dve.wait_ge(norm_rstd, 2)
                    ins = scaled_rows(MEMR, MEMR, p // 4 - 2)
                    if p == 12:
                        ins.then_inc(norm_rows, 1)

            def residual(name, p):
                c = p // GD
                n = PROD0[name] + c
                dve.wait_ge(group_used, GROUP0[name] + p + 1)
                o = X[:, :, c * CH:(c + 1) * CH]
                return dve.tensor_tensor(o, PS[:, 2 * (n % 2):2 * (n % 2) + 2, :], o, ALU.add)
            dve.wait_ge(x_loaded, 16 * NCH)
            for p in range(NCH * GD):
                split(At(GROUP0["out1"]), p + RING)
                if p in (1, 2):
                    transposed("merged1", HT, merged_tiles(NCH * GW + p), None)
                if 4 <= p < 4 + KT:
                    transposed("mem", MEMT, [p - 4], "mem")
                if p % GD == GD - 1:
                    residual("out1", p).then_inc(prod_free, 1)
            for p in range(GD):
                split(At(GROUP0["mem0"]), p + RING)
                if p == 1:
                    dve.wait_ge(x_sq, 1)
                    dve.tensor_reduce(MS[:, 0:T], MSC[:], AX_X, ALU.add).then_inc(norm_ms, 1)
                    link(dve.memset(FU[:, :, 0:2], 0.0))
                if p == 2:
                    rows_by_halves(3)
                if p >= 4:
                    transposed("h2", HT, [2 * p - 8, 2 * p - 7], "ffn")

            def up_sums(u, tile):
                for f in range(FT):
                    dve.wait_ge(ffn_copied, tile.count(f + 1))
                    dve.tensor_tensor(FU[:, f, 2:S + 2], PS[:, 4 * (u.base % 2) + f, S:2 * S], FC[:, f, :], ALU.add).then_inc(ffn_sum, 1)
                dve.wait_ge(ffn_sum, tile.count(FT))
                dve.sem_inc(ffn_free, 1)

            def conv(f, tile, feature, silu_done):
                z, y = FU[:, f, :], FY[:, f % 2, :]
                if silu_done is not None:
                    dve.wait_ge(ffn_silu, silu_done)
                link(dve.tensor_scalar(y, z[:, 2:S + 2], par("conv", feature * 4 + 2), par("conv", feature * 4 + 3),
                                       ALU.mult, ALU.add))
                link(dve.scalar_tensor_tensor(out=y, in0=z[:, 1:S + 1], scalar=par("conv", feature * 4 + 1), in1=y,
                                              op0=ALU.mult, op1=ALU.add))
                dve.scalar_tensor_tensor(out=y, in0=z[:, 0:S], scalar=par("conv", feature * 4), in1=y,
                                         op0=ALU.mult, op1=ALU.add).then_inc(ffn_conv, 1)

            def b_tile(f, tile, feature, silu_done):
                conv(f, tile, feature, silu_done)
                dve.wait_ge(ffn_conv, tile.count(1))
                ins = dve.tensor_tensor(FP[:, f, :], FA[:, f, :], FY[:, f % 2, :], ALU.mult)
                if f == FT - 1:
                    ins.then_inc(ffn_prod, 1)

            def block_lo(blk):
                dve.wait_ge(ffn_hi, blk.count(1))
                dve.tensor_tensor(ACTT[:, :, 1, :], FP[:], ACTT[:, :, 0, :].bitcast(F32), ALU.subtract).then_inc(ffn_lo, 1)

            def down_add(u, end):
                dve.wait_ge(group_used, end)
                half, c0 = 4 * (u.base % 2), 2 * (u.base % 2)
                for c in range(2):
                    o = X[:, :, (c0 + c) * CH:(c0 + c + 1) * CH]
                    ins = dve.tensor_tensor(o, PS[:, half + 2 * c:half + 2 * c + 2, :], o, ALU.add)
                ins.then_inc(ffn_free, 1)

            g0 = GROUP0["ffn"]
            for p in range(2 * GD):
                if p < 4:
                    transposed("h2", HT, [8 + 2 * p, 9 + 2 * p], "ffn")
                split(At(g0), p + RING)
                if p == 7:
                    up_sums(At(0), At(0))
                if 8 <= p <= 11:
                    f = p - 8
                    conv(f, At(f), f, f - 1 if f >= 2 else None)
            up_sums(At(1), At(FT))
            with dve.Fori(0, FB - 1) as b:
                ch.enter(b, 2 * 2 * FT)
                g = At(g0 + 2 * GD, b, 3 * GD)
                for p in range(3 * GD):
                    split(g, p + RING)
                    if p < FT:
                        b_tile(p, At(FT + p, b, 8), b * FT + (NFT // 2 + p), At(FT, b, FT).count())
                    if p == FT:
                        block_lo(At(0, b, 1))
                    if p in (7, 15):
                        up_sums(At(2 + p // 8, b, 4), At(8 + p // 8 * FT, b, 8))
                    if 8 <= p <= 11:
                        f = p - 8
                        conv(f, At(8 + f, b, 8), b * FT + (FT + f), At(FT + f - 1, b, FT).count() if f >= 2 else None)
                    if p == 20:
                        down_add(At(4, b, 4), g.count(2 * GD + 4))
                    if p == 23:
                        down_add(At(5, b, 4), g.count(3 * GD))
            ch.leave(FB - 1)
            for p in range(GD):
                split(At(GROUP0["mem1"]), p + RING)
                if p < FT:
                    b_tile(p, At(8 * (FB - 1) + FT + p), (FB - 1) * FT + NFT // 2 + p, FB * FT)
                if p == FT:
                    block_lo(At(FB - 1))
            for p in range(GD):
                split(At(GROUP0["ffn_down"]), p + RING)
                if p == 3:
                    down_add(At(4 * FB - 2), GROUP0["ffn_down"] + 4)
                if p == 7:
                    down_add(At(4 * FB - 1), GROUP0["ffn_down"] + 8)
            dve.wait_ge(ffn_free, 2 + 4 * FB)
            dve.sem_inc(x_done, 1)

            dve.wait_ge(fw_loaded, 16)
            for p in range(2 * GD):
                split(At(GROUP0["mem2"]), p + RING)
                if p in (1, 2):
                    dve.wait_ge(norm_rstd, 4)
                    scaled_rows(X, X, p - 1, FINALW[:]).then_inc(x_done, 1)
                if p in (7, 8):
                    dve.wait_ge(norm_rstd, 5)
                    scaled_rows(ROWS, X, p - 7, inv=MST[:, 0, 0]).then_inc(norm_rows, 1)
                transposed("h3", HT, h3_tiles(p), "norm2")
            stream("c_proj", 2, 2 * GD)

            dve.wait_ge(gate_ready, 2)
            with dve.Fori(0, 4) as i:
                ch.enter(i, 2)
                st = head_steps(CMEM, At(C0, i, 1), At(8, i, 1), i, lambda t: PB[:, t, ds(i * 256 + W, 256)], (6, 11, 14))
                for p in range(2 * GD):
                    split(At(GROUP0["a_proj"], i, 2 * GD), p + RING)
                    if p in st:
                        st[p]()
            ch.leave(4)

            assert TOPK_AT + 8 - 3 * GD == 2
            masked, left = SC, OF[:].rearrange("p t d -> p (t d)")
            halves = [(0, slice(0, P)), (1, slice(P, CAUS))]

            def topk_round(r):
                src = left
                if r == 0:
                    src = masked
                    link(dve.tensor_tensor(masked[:, 0:CAUS], PT[:, 0:CAUS], con("mask"), ALU.add))
                for t, cols in halves:
                    ins = dve.max(M8[:, t, :], src[:, cols])
                link(ins)
                for t, cols in halves:
                    ins = dve.match_replace(left[:, cols], M8[:, t, :], src[:, cols], TAKEN)
                link(ins)

            link(dve.memset(PT[:, 0:CAUS], 0.0))
            dve.wait_ge(prod_free, 2 + PROD0["b_proj"])
            for p in range(3 * GD):
                split(At(GROUP0["b_proj"]), p + RING)
                if p % 2 and 3 <= p < TOPK_AT:
                    k = (p - 3) // 2
                    dve.wait_ge(idx_relu, k + 2)
                    for j, src in enumerate((SC, PR)):
                        for t, cols in halves:
                            w = PAC[:, 7, t, IW + 2 * k + j:IW + 2 * k + j + 1]
                            ins = dve.scalar_tensor_tensor(out=PT[:, cols], in0=src[:, cols], scalar=w, in1=PT[:, cols],
                                                           op0=ALU.mult, op1=ALU.add)
                        link(ins)
                    dve.sem_inc(idx_sum, 1)
                if p >= TOPK_AT:
                    topk_round(p - TOPK_AT)
            for p in range(GD):
                split(At(GROUP0["gates_b0"]), p + RING)
                if p < 2:
                    topk_round(3 * GD - TOPK_AT + p)
                if p == 2:
                    link(dve.tensor_scalar(left[:, 0:CAUS], left[:, 0:CAUS], TAKEN, -1.0, ALU.is_equal, ALU.add))
                    link(dve.scalar_tensor_tensor(out=SC[:, 0:CAUS], in0=left[:, 0:CAUS], scalar=-NEG, in1=con("mask"),
                                                  op0=ALU.mult, op1=ALU.add))
                    dve.wait_ge(lat_rstd, 1)
                    for t in range(T):
                        dve.tensor_scalar(PB[:, t, 0:512], PB[:, t, 0:512], MS[:, t:t + 1], None, ALU.mult)
                        dve.tensor_scalar(PB[:, t, PB_KV], PAC[:, 7, t, KV_LAT], MS[:, 2 + t:3 + t], None, ALU.mult)
                    dve.tensor_copy(PB[:, :, PB_KPE], PAC[:, 7, :, KPE]).then_inc(lat_rows, 1)
                if 4 <= p < 7:
                    transposed("lat", LATT, [2 * p - 8, 2 * p - 7], "lat")
                if p in (3, 4):
                    dve.wait_ge(bias_loaded, 64)
                    half = BIAS[:, (p - 3) * 4:(p - 2) * 4]
                    dve.tensor_tensor(half, half, SC[:, 0:CAUS].unsqueeze(1).broadcast_to([P, REL_HEADS // 2, CAUS]),
                                      ALU.add).then_inc(sel_ready, 1)
            dve.wait_ge(sel_ready, 2)
            dve.wait_ge(gate_ready, 3)

            def a_step(i, p):
                r = p // 6

                def gate(t):
                    return PAC[:, ds(i + 3, 1), t, r * P:(r + 1) * P].rearrange("p a d -> p (a d)")
                st = head_steps(ASP, At(A0 + r, i, 4), At(12 + r, i, 4), i * 4 + r, gate, (1, 4, 5))
                if p - 6 * r in st:
                    st[p - 6 * r]()
            merge("merge_c", 2, 2, MERGED["merged2"], 4 * 2, a_step)
            for p in range(10):
                split(At(GROUP0["b_up"]), p + RING)
                if p == 8:
                    dve.wait_ge(bq_sq, 1)
                    dve.tensor_reduce(MST[:, 0].rearrange("p t h -> p (t h)"), SQQ[:].rearrange("p t (h d) -> p (t h) d", d=192),
                                      AX_X, ALU.add)
            dve.wait_ge(bk_sq, 1)
            dve.tensor_reduce(MST[:, 1].rearrange("p t h -> p (t h)"), SQK[:].rearrange("p t h d -> p (t h) d"),
                              AX_X, ALU.add).then_inc(b_ms, 1)
            for p in range(GD):
                split(At(GROUP0["gates_b1"]), p + RING)
            dve.wait_ge(gate_ready, 4)

            def b_step(i, p):
                r = p // 6
                h = i * 2 + r
                st = head_steps(BLA, At(B0 + r, i, 2), At(20 + r, i, 2), h, lambda t: PB[:, t, ds(h * P + PB_Z, P)], (1, 4, 5))
                if p - 6 * r in st:
                    st[p - 6 * r]()
            merge("merge_a", NCH, 1, MERGED["merged2"], 2 * 2, b_step)
            for p in range(2 * GD):
                split(At(GROUP0["gates_b"]), p + RING)
            dve.wait_ge(prod_free, 2 + PROD0["up_b"])
            for p in range(NCH * GW):
                split(At(GROUP0["up_b"]), p + RING)
                transposed("merged2", HT, merged_tiles(p), None)
                if p % GW == GW - 1:
                    up_chunk("up_b", MERGED["merged2"], p // GW)
            dve.wait_ge(x_back, 16)
            for p in range(NCH * GD):
                if p + RING < NCH * GD:
                    split(At(GROUP0["out2"]), p + RING)
                if p in (1, 2):
                    transposed("merged2", HT, merged_tiles(NCH * GW + p), None)
                if p % GD == GD - 1:
                    link(residual("out2", p))
                    dve.sem_inc(prod_free, 1)
                    dve.sem_inc(out_ready, 1)


def groups_of(w):
    k, n = w.shape
    return w.reshape(k // (GK * P), GK, P, n // CH, CH).transpose(3, 0, 2, 1, 4).reshape(n // CH, -1, P, GK * CH)


def lay_out(x):
    w_in, w_in2 = x["w_in"][0], x["w_in_2"][0]
    stream = np.empty((GROUPS, P, GK * CH), np.float32)
    at = [0]

    def put(*parts):
        for c in range(len(parts[0])):
            for part in parts:
                stream[at[0]:at[0] + part.shape[1]] = part[c]
                at[0] += part.shape[1]

    def padded(w, n):
        return np.concatenate([w, np.zeros((w.shape[0], n - w.shape[1]), w.dtype)], 1)

    put(groups_of(w_in[:, 4 * W:7 * W]))
    put(groups_of(w_in[:, 0:4 * W]))
    gates = 7 * W
    put(groups_of(w_in[:, gates + D:gates + 2 * D]), groups_of(x["w_moba_up"][0]))
    put(groups_of(w_in[:, gates:gates + D]))
    put(groups_of(x["w_ret_up"][0]))
    put(groups_of(x["w_out"][0]))
    up, down = groups_of(x["w_ffn_up"][0]), x["w_ffn_down"][0]
    mem = groups_of(x["w_mem_kv_2"][0])
    put(mem[0:1])
    for b in range(FB + 1):
        if b < FB:
            put(up[b:b + 1])
            put(up[FB + b:FB + b + 1])
        else:
            put(mem[1:2])
        if b:
            put(groups_of(down[(b - 1) * CH:b * CH]))
    put(mem[2:4])
    put(groups_of(w_in2[:, 5520:7568]))
    put(groups_of(padded(np.concatenate([w_in2[:, 0:3664], w_in2[:, 4176:4496]], 1), 4096)))
    put(groups_of(np.concatenate([w_in2[:, 3664:4176], w_in2[:, 4496:5520]], 1)))
    branch = x["w_branch_2"][0]
    a_gate, b_gate, c_gate = [groups_of(w_in2[:, 7568 + b * D:7568 + (b + 1) * D]) for b in range(3)]
    put(b_gate[0:1])
    put(c_gate, groups_of(branch[2]))
    put(groups_of(x["w_b_uq_2"][0]))
    put(groups_of(x["w_b_ukv_2"][0]))
    put(b_gate[1:2])
    put(a_gate, groups_of(branch[0]))
    put(b_gate[2:4])
    put(groups_of(branch[1]))
    put(groups_of(x["w_out_2"][0]))
    assert at[0] == GROUPS

    pack = np.zeros((P, NPAR), np.float32)

    def par(name, value):
        o, n = PAR[name]
        pack[:, o:o + n] = value

    def columns(v):
        return v.reshape(-1, P).T

    par("attn", columns(x["attn_norm_w"]))
    par("ffn", columns(x["ffn_norm_w"]))
    par("norm2", columns(x["norm_g_2"]))
    par("mem", columns(x["mem_norm_g_2"]))
    par("ret", columns(x["ret_norm_w"]))
    par("aq", columns(x["a_q_norm_g_2"]))
    par("ak", columns(x["a_k_norm_g_2"]))
    par("lat", np.concatenate([columns(x["b_q_lat_norm_g_2"]), columns(x["b_kv_lat_norm_g_2"])], 1))
    par("cq", columns(x["c_q_norm_g_2"]))
    par("ck", columns(x["c_k_norm_g_2"]))
    par("bqn", x["b_q_norm_g_2"][:, 0:P].T)
    par("bkn", x["b_k_norm_g_2"][:, 0:P].T)
    par("brope", np.concatenate([x["b_q_norm_g_2"][:, P:], x["b_k_norm_g_2"][:, P:]], 1))
    taps = np.concatenate([x["conv_w"][0], x["conv_b"]], 0)
    par("conv", taps.reshape(4, NFT, P).transpose(2, 1, 0).reshape(P, -1))
    table = np.zeros((P, 32), np.float32)
    for g in range(4):
        table[32 * g:32 * g + 32, 8 * g:8 * g + 8] = x["rel_bias_2"]
    par("rel", table)

    pos = x["positions_2"].reshape(S)
    ints = np.zeros((P, POSN + 2), np.int32)
    for g in range(4):
        rows = slice(32 * g, 32 * g + 32)
        ints[rows, 0:32] = pos[32 * g:32 * g + 32]
        ints[rows, 32:64] = pos[P + 32 * g:P + 32 * g + 32]
    ints[:, 64:POSN] = pos
    ints[:, POSN:] = pos.reshape(T, P).T
    return stream, pack, ints


def kernel(**inputs):
    import concourse.bacc as bacc
    from concourse.bass_utils import run_bass_kernel_spmd

    x = {name: np.asarray(a) for name, a in inputs.items()}
    stream, pack, ints = lay_out(x)
    arrays = {"x_in": x["x"].reshape(S, D), "mem_in": x["mem_2"].reshape(S, D), "w_stream": stream, "params": pack,
              "final_w": x["final_norm_w"], "pos_pack": ints, "constants": make_constants()}
    arrays = {name: np.ascontiguousarray(a) for name, a in arrays.items()}
    nc = bacc.Bacc("TRN2", target_bir_lowering=False, num_devices=1, dynamic_dma_scratch_size=DMA_SCRATCH)
    args = [nc.dram_tensor(name, a.shape, mybir.dt.from_np(a.dtype), kind="ExternalInput").ap() for name, a in arrays.items()]
    out = nc.dram_tensor("out", (S, D), F32, kind="ExternalOutput").ap()
    build(nc, *args, out)
    r = run_bass_kernel_spmd(nc, [arrays], core_ids=[0])
    return r.results[0]["out"].reshape(1, S, D)
```
